# Optimizing a Trainium2 kernel written in Bass

```python
import math
import jax
import jax.numpy as jnp
from jax import lax
import numpy as np
import jax, jax.numpy as jnp

D_MODEL = 1024
BATCH = 1
SEQ = 256
DEPTH = 2

GRID_W = 64
CTX_LEN = 256
NORM_EPS = 1e-6

RW_HEAD_DIM = 64
RW_DIM = D_MODEL // 2
RW_HEADS = RW_DIM // RW_HEAD_DIM
RW_LORA_W = 32
RW_LORA_A = 32
RW_LORA_G = 96
RW_GN_EPS = 64e-5
RW_COLS = 3 * RW_DIM + 2 * RW_LORA_W + 2 * RW_LORA_A + RW_LORA_G
RW_SPLITS = (RW_DIM, 2 * RW_DIM, 3 * RW_DIM, 3 * RW_DIM + 2 * RW_LORA_W, 3 * RW_DIM + 2 * RW_LORA_W + 2 * RW_LORA_A)

MB_HEAD_DIM = 64
MB_DIM = D_MODEL // 2
MB_HEADS = MB_DIM // MB_HEAD_DIM
MB_GROUPS = 2
MB_STATE = 128
MB_CONV = 5
MB_CHUNK = 128
MB_XBC = MB_DIM + 2 * MB_GROUPS * MB_STATE
MB_COLS = MB_DIM + MB_XBC + 2 * MB_HEADS
MB_SPLITS = (MB_DIM, MB_DIM + MB_XBC)

MIX_IN = RW_COLS + MB_COLS
MIX_OUT = RW_DIM + MB_DIM

NA_HEAD_DIM = 64
NA_HEADS = D_MODEL // NA_HEAD_DIM
NA_KH = 8
NA_KW = 16
NA_QB = 16
NA_KB = 32

D_FF = 2816
N_EXPERTS = 8
TOP_K = 2


def _rms_norm(h, g):
    hf = h.astype(jnp.float32)
    hf = hf * lax.rsqrt(jnp.mean(hf * hf, axis=-1, keepdims=True) + NORM_EPS)
    return (hf * g.astype(jnp.float32)).astype(h.dtype)

def _modulate(h, shift, scale):
    return h * (1 + scale) + shift

def _heads(t, n_heads):
    return t.reshape(t.shape[:-1] + (n_heads, t.shape[-1] // n_heads))

def _swiglu(h, w1, w3, w2):
    return (jax.nn.silu(h @ w1) * (h @ w3)) @ w2

def _centred_shift(z, mu_prev, mu_next):
    z_prev = jnp.pad(z, ((0, 0), (1, 0), (0, 0)))[:, :-1]
    z_next = jnp.pad(z, ((0, 0), (0, 1), (0, 0)))[:, 1:]
    return z + mu_prev * (z_prev - z) + mu_next * (z_next - z)

def _centred_dwconv(x, w, b):
    k_w, ch = w.shape
    y = lax.conv_general_dilated(x, w[:, None, :].astype(x.dtype), window_strides=(1,),
                                 padding=[(k_w // 2, k_w // 2)],
                                 dimension_numbers=('NWC', 'WIO', 'NWC'), feature_group_count=ch)
    return y + b

def _rwkv7_scan(s0, r, w, k, v, a, b):
    def step(S, inp):
        r_t, w_t, k_t, v_t, a_t, b_t = inp
        sa = jnp.einsum('bhvk,bhk->bhv', S, a_t)
        S = S * w_t[:, :, None, :] + sa[..., None] * b_t[:, :, None, :] + v_t[..., None] * k_t[:, :, None, :]
        return S, jnp.einsum('bhvk,bhk->bhv', S, r_t)
    xs = tuple(jnp.moveaxis(t, 1, 0) for t in (r, w, k, v, a, b))
    s_fin, ys = lax.scan(step, s0, xs)
    return s_fin, jnp.moveaxis(ys, 0, 1)

def _segsum(x):
    n = x.shape[-1]
    cs = jnp.cumsum(x, axis=-1)
    return jnp.where(np.tril(np.ones((n, n), dtype=bool)), cs[..., :, None] - cs[..., None, :], -jnp.inf)

def _ssd_chunked(s0, X, A, Bm, Cm):
    b, t, nh, p = X.shape
    n = Bm.shape[-1]
    nc, cl = t // MB_CHUNK, MB_CHUNK
    X = X.reshape(b, nc, cl, nh, p)
    Bm = Bm.reshape(b, nc, cl, nh, n)
    Cm = Cm.reshape(b, nc, cl, nh, n)
    A = A.reshape(b, nc, cl, nh).transpose(0, 3, 1, 2)
    A_cs = jnp.cumsum(A, axis=-1)
    L = jnp.exp(_segsum(A))
    y_diag = jnp.einsum('bclhn,bcshn,bhcls,bcshp->bclhp', Cm, Bm, L, X)
    decay_states = jnp.exp(A_cs[..., -1:] - A_cs)
    states = jnp.einsum('bclhn,bhcl,bclhp->bchpn', Bm, decay_states, X)
    states = jnp.concatenate([s0[:, None], states], axis=1)
    chunk_decay = jnp.exp(_segsum(jnp.pad(A_cs[..., -1], ((0, 0), (0, 0), (1, 0)))))
    states = jnp.einsum('bhzc,bchpn->bzhpn', chunk_decay, states)
    y_off = jnp.einsum('bclhn,bchpn,bhcl->bclhp', Cm, states[:, :-1], jnp.exp(A_cs))
    return states[:, -1], (y_diag + y_off).reshape(b, t, nh, p)

def _prefix_scan(scan_fn, ctx_args, lat_args, s0, reverse):
    if reverse:
        ctx_args = tuple(jnp.flip(t, axis=1) for t in ctx_args)
        lat_args = tuple(jnp.flip(t, axis=1) for t in lat_args)
    s_ctx, y_ctx = scan_fn(s0, *ctx_args)
    _, y_lat = scan_fn(s_ctx, *lat_args)
    if reverse:
        y_ctx, y_lat = jnp.flip(y_ctx, axis=1), jnp.flip(y_lat, axis=1)
    return y_ctx, y_lat

def _rwkv_mamba_mixer(a_ctx, a_lat, w_in, w_out, rw_mu, rw_w0, rw_w_up, rw_a0, rw_a_up, rw_g_up,
                      rw_k_k, rw_k_a, rw_r_k, rw_gn_w, rw_gn_b, mb_conv_w, mb_conv_b,
                      mb_dt_bias, mb_a_log, mb_d, mb_norm_w):
    f32 = jnp.float32

    def prepare(h):
        b, t, _ = h.shape
        z = h @ w_in
        z_rw = _centred_shift(z[..., :RW_COLS], rw_mu[0], rw_mu[1])
        r, k, v, lw, la, lg = jnp.split(z_rw, RW_SPLITS, axis=-1)
        lw = lw.reshape(b, t, 2, RW_LORA_W)
        la = la.reshape(b, t, 2, RW_LORA_A)
        logw = (rw_w0 + jnp.einsum('btdl,dlc->btdc', jnp.tanh(lw), rw_w_up)).astype(f32)
        decay = jnp.exp(-jnp.exp(-jax.nn.softplus(-logw) - 0.5))
        iclr = jax.nn.sigmoid((rw_a0 + jnp.einsum('btdl,dlc->btdc', la, rw_a_up)).astype(f32))
        gate = jax.nn.sigmoid(lg) @ rw_g_up
        kk = _heads(k * rw_k_k, RW_HEADS).astype(f32)
        kk = kk / jnp.maximum(jnp.sqrt(jnp.sum(kk * kk, axis=-1, keepdims=True)), 1e-12)
        k_dir = _heads((k[:, :, None, :] * (1 + (iclr - 1) * rw_k_a)).astype(f32), RW_HEADS)
        rh = _heads(r.astype(f32), RW_HEADS)
        vh = _heads(v.astype(f32), RW_HEADS)
        dh = _heads(decay, RW_HEADS)
        ih = _heads(iclr, RW_HEADS)
        rw_args = [(rh, dh[:, :, d], k_dir[:, :, d], vh, -kk, kk * ih[:, :, d]) for d in range(2)]
        bonus_f = jnp.sum(rh * k_dir[:, :, 0] * rw_r_k[0].astype(f32), axis=-1, keepdims=True)
        bonus_b = jnp.sum(rh * k_dir[:, :, 1] * rw_r_k[1].astype(f32), axis=-1, keepdims=True)
        bonus = (bonus_f + bonus_b) * vh
        zg, xbc, dt_raw = jnp.split(z[..., RW_COLS:], MB_SPLITS, axis=-1)
        xbc = jax.nn.silu(_centred_dwconv(xbc, mb_conv_w, mb_conv_b))
        xm, bm, cm = jnp.split(xbc, (MB_DIM, MB_DIM + MB_GROUPS * MB_STATE), axis=-1)
        xm = _heads(xm.astype(f32), MB_HEADS)
        rep = MB_HEADS // MB_GROUPS
        bm = jnp.repeat(_heads(bm.astype(f32), MB_GROUPS), rep, axis=2)
        cm = jnp.repeat(_heads(cm.astype(f32), MB_GROUPS), rep, axis=2)
        dt = jax.nn.softplus(dt_raw.reshape(b, t, 2, MB_HEADS).astype(f32) + mb_dt_bias.astype(f32))
        a_neg = -jnp.exp(mb_a_log.astype(f32))
        mb_args = [(xm * dt[:, :, d, :, None], dt[:, :, d] * a_neg[d], bm, cm) for d in range(2)]
        return rw_args, mb_args, bonus, gate, xm, zg

    pc, pl = prepare(a_ctx), prepare(a_lat)
    bsz = a_lat.shape[0]
    s0_rw = jnp.zeros((bsz, RW_HEADS, RW_HEAD_DIM, RW_HEAD_DIM), f32)
    s0_mb = jnp.zeros((bsz, MB_HEADS, MB_HEAD_DIM, MB_STATE), f32)
    yrf_c, yrf_l = _prefix_scan(_rwkv7_scan, pc[0][0], pl[0][0], s0_rw, False)
    yrb_c, yrb_l = _prefix_scan(_rwkv7_scan, pc[0][1], pl[0][1], s0_rw, True)
    ymf_c, ymf_l = _prefix_scan(_ssd_chunked, pc[1][0], pl[1][0], s0_mb, False)
    ymb_c, ymb_l = _prefix_scan(_ssd_chunked, pc[1][1], pl[1][1], s0_mb, True)

    def finish(h, p, y_rw, y_mb):
        b, t, _ = h.shape
        _, _, bonus, gate, xm, zg = p
        mu = jnp.mean(y_rw, axis=-1, keepdims=True)
        var = jnp.mean(jnp.square(y_rw - mu), axis=-1, keepdims=True)
        y_rw = ((y_rw - mu) * lax.rsqrt(var + RW_GN_EPS)).reshape(b, t, RW_DIM) * rw_gn_w + rw_gn_b
        o_rw = (y_rw + bonus.reshape(b, t, RW_DIM)) * gate
        y_mb = (y_mb + mb_d.astype(f32)[:, None] * xm).reshape(b, t, MB_DIM) * jax.nn.silu(zg.astype(f32))
        y_mb = y_mb.reshape(b, t, MB_GROUPS, MB_DIM // MB_GROUPS)
        y_mb = (y_mb * lax.rsqrt(jnp.mean(y_mb * y_mb, axis=-1, keepdims=True) + NORM_EPS)).reshape(b, t, MB_DIM) * mb_norm_w
        return jnp.concatenate([o_rw, y_mb], axis=-1).astype(h.dtype) @ w_out

    return (finish(a_ctx, pc, yrf_c + yrb_c, ymf_c + ymb_c),
            finish(a_lat, pl, yrf_l + yrb_l, ymf_l + ymb_l))

def _neighbourhood_attention(a_ctx, a_lat, w_qkv, w_out, rpb, with_ctx_queries):
    b, t, d_model = a_lat.shape
    rows = t // GRID_W
    kh = min(NA_KH, rows)
    scale = NA_HEAD_DIM ** -0.5
    q, k, v = jnp.split(a_lat @ w_qkv, 3, axis=-1)
    qc, kc, vc = jnp.split(a_ctx @ w_qkv, 3, axis=-1)
    q_grid = (_heads(q, NA_HEADS) * scale).reshape(b, rows, GRID_W, NA_HEADS, NA_HEAD_DIM)
    k_grid = _heads(k, NA_HEADS).reshape(b, rows, GRID_W, NA_HEADS, NA_HEAD_DIM)
    v_grid = _heads(v, NA_HEADS).reshape(b, rows, GRID_W, NA_HEADS, NA_HEAD_DIM)
    qc, kc, vc = _heads(qc, NA_HEADS) * scale, _heads(kc, NA_HEADS), _heads(vc, NA_HEADS)

    n_cb = GRID_W // NA_QB
    q_cols = np.arange(GRID_W).reshape(n_cb, NA_QB)
    kb_start = np.clip(np.arange(n_cb) * NA_QB - NA_KW // 2, 0, GRID_W - NA_KB)
    key_cols = kb_start[:, None] + np.arange(NA_KB)
    win_start = np.clip(q_cols - NA_KW // 2, 0, GRID_W - NA_KW)
    kcol = key_cols[:, None, :]
    col_in = (kcol >= win_start[..., None]) & (kcol < win_start[..., None] + NA_KW)
    col_bias_idx = np.clip(kcol - q_cols[:, :, None] + NA_KW - 1, 0, 2 * NA_KW - 2)
    mask = np.broadcast_to(col_in[:, :, None, :], (n_cb, NA_QB, kh, NA_KB)).reshape(n_cb, NA_QB, kh * NA_KB)
    n_lat = kh * NA_KB

    def row_block(r):
        rs = jnp.clip(r - kh // 2, 0, rows - kh)
        k_rows = lax.dynamic_slice_in_dim(k_grid, rs, kh, axis=1)
        v_rows = lax.dynamic_slice_in_dim(v_grid, rs, kh, axis=1)
        k_blk = k_rows[:, :, key_cols].transpose(0, 2, 1, 3, 4, 5).reshape(b, n_cb, n_lat, NA_HEADS, NA_HEAD_DIM)
        v_blk = v_rows[:, :, key_cols].transpose(0, 2, 1, 3, 4, 5).reshape(b, n_cb, n_lat, NA_HEADS, NA_HEAD_DIM)
        q_blk = lax.dynamic_index_in_dim(q_grid, r, axis=1, keepdims=False).reshape(b, n_cb, NA_QB, NA_HEADS, NA_HEAD_DIM)
        row_idx = rs + jnp.arange(kh) - r + (NA_KH - 1)
        bias = rpb[:, row_idx][:, :, col_bias_idx]
        bias = bias.transpose(0, 2, 3, 1, 4).reshape(NA_HEADS, n_cb, NA_QB, n_lat).astype(jnp.float32)
        s_lat = jnp.einsum('bjqhd,bjkhd->bhjqk', q_blk, k_blk).astype(jnp.float32) + bias
        s_lat = jnp.where(mask, s_lat, -jnp.inf)
        s_ctx = jnp.einsum('bjqhd,bkhd->bhjqk', q_blk, kc).astype(jnp.float32)
        p = jax.nn.softmax(jnp.concatenate([s_lat, s_ctx], axis=-1), axis=-1).astype(v.dtype)
        o = (jnp.einsum('bhjqk,bjkhd->bjqhd', p[..., :n_lat], v_blk)
             + jnp.einsum('bhjqk,bkhd->bjqhd', p[..., n_lat:], vc))
        return o.reshape(b, GRID_W, d_model)

    o_rows = lax.map(row_block, jnp.arange(rows))
    o_lat = o_rows.transpose(1, 0, 2, 3).reshape(b, t, d_model) @ w_out
    o_ctx = None
    if with_ctx_queries:
        s = jnp.einsum('bqhd,bkhd->bhqk', qc, kc).astype(jnp.float32)
        p = jax.nn.softmax(s, axis=-1).astype(vc.dtype)
        o_ctx = jnp.einsum('bhqk,bkhd->bqhd', p, vc).reshape(a_ctx.shape) @ w_out
    return o_ctx, o_lat

def _moe_swiglu(h, router_w, router_b, w1, w3, w2):
    logits = (h @ router_w).astype(jnp.float32) + router_b.astype(jnp.float32)
    top_vals, top_idx = lax.top_k(logits, TOP_K)
    top_w = jax.nn.softmax(top_vals, axis=-1)
    gates = jnp.sum(jax.nn.one_hot(top_idx, N_EXPERTS, dtype=jnp.float32) * top_w[..., None], axis=-2).astype(h.dtype)
    out = jnp.zeros_like(h)
    for e in range(N_EXPERTS):
        out = out + gates[..., e:e + 1] * _swiglu(h, w1[e], w3[e], w2[e])
    return out

def first_inputs(seed: int = 0) -> dict:
    key = jax.random.key(seed)
    keys = iter(jax.random.split(key, 64))
    d = D_MODEL
    ne, no = (DEPTH + 1) // 2, DEPTH // 2

    def nrm(shape, scale):
        return scale * jax.random.normal(next(keys), shape, jnp.float32)

    def uni(shape, lo, hi):
        return jax.random.uniform(next(keys), shape, jnp.float32, lo, hi)

    dt0 = jnp.exp(uni((ne, 2, MB_HEADS), math.log(1e-3), math.log(1e-1)))
    return {
        'x': nrm((BATCH, SEQ, d), 1.0),
        'c': nrm((BATCH, d), 1.0),
        'ctx': nrm((BATCH, CTX_LEN, d), 1.0),
        'c_ctx': nrm((d,), 1.0),
        'w_ada': nrm((DEPTH, d, 6 * d), 0.5 * d ** -0.5),
        'b_ada': nrm((DEPTH, 6 * d), 0.02),
        'norm_mix': 1.0 + nrm((DEPTH, d), 0.05),
        'norm_ffn': 1.0 + nrm((DEPTH, d), 0.05),
        'norm_final': 1.0 + nrm((d,), 0.05),
        'mix_w_in': nrm((ne, d, MIX_IN), d ** -0.5),
        'mix_w_out': nrm((ne, MIX_OUT, d), MIX_OUT ** -0.5),
        'rw_mu': uni((ne, 2, RW_COLS), 0.0, 0.5),
        'rw_w0': uni((ne, 2, RW_DIM), -6.0, 1.0),
        'rw_w_up': nrm((ne, 2, RW_LORA_W, RW_DIM), 0.5 * RW_LORA_W ** -0.5),
        'rw_a0': nrm((ne, 2, RW_DIM), 0.5),
        'rw_a_up': nrm((ne, 2, RW_LORA_A, RW_DIM), 0.5 * RW_LORA_A ** -0.5),
        'rw_g_up': nrm((ne, RW_LORA_G, RW_DIM), RW_LORA_G ** -0.5),
        'rw_k_k': 0.85 + nrm((ne, RW_DIM), 0.05),
        'rw_k_a': 1.0 + nrm((ne, RW_DIM), 0.05),
        'rw_r_k': nrm((ne, 2, RW_HEADS, RW_HEAD_DIM), 0.1),
        'rw_gn_w': 1.0 + nrm((ne, RW_DIM), 0.05),
        'rw_gn_b': nrm((ne, RW_DIM), 0.02),
        'mb_conv_w': nrm((ne, MB_CONV, MB_XBC), MB_CONV ** -0.5),
        'mb_conv_b': nrm((ne, MB_XBC), 0.02),
        'mb_dt_bias': dt0 + jnp.log(-jnp.expm1(-dt0)),
        'mb_a_log': jnp.log(uni((ne, 2, MB_HEADS), 1.0, 16.0)),
        'mb_d': 1.0 + nrm((ne, MB_HEADS), 0.1),
        'mb_norm_w': 1.0 + nrm((ne, MB_DIM), 0.05),
        'ffn_w1': nrm((ne, d, D_FF), d ** -0.5),
        'ffn_w3': nrm((ne, d, D_FF), d ** -0.5),
        'ffn_w2': nrm((ne, D_FF, d), D_FF ** -0.5),
        'na_w_qkv': nrm((no, d, 3 * d), d ** -0.5),
        'na_w_out': nrm((no, d, d), d ** -0.5),
        'na_rpb': nrm((no, NA_HEADS, 2 * NA_KH - 1, 2 * NA_KW - 1), 0.1),
        'moe_router_w': nrm((no, d, N_EXPERTS), d ** -0.5),
        'moe_router_b': nrm((no, N_EXPERTS), 0.01),
        'moe_w1': nrm((no, N_EXPERTS, d, D_FF), d ** -0.5),
        'moe_w3': nrm((no, N_EXPERTS, d, D_FF), d ** -0.5),
        'moe_w2': nrm((no, N_EXPERTS, D_FF, d), D_FF ** -0.5),
    }

def first_block(x, c, ctx, c_ctx, w_ada, b_ada, norm_mix, norm_ffn, norm_final, mix_w_in, mix_w_out,
              rw_mu, rw_w0, rw_w_up, rw_a0, rw_a_up, rw_g_up, rw_k_k, rw_k_a, rw_r_k, rw_gn_w, rw_gn_b,
              mb_conv_w, mb_conv_b, mb_dt_bias, mb_a_log, mb_d, mb_norm_w, ffn_w1, ffn_w3, ffn_w2,
              na_w_qkv, na_w_out, na_rpb, moe_router_w, moe_router_b, moe_w1, moe_w3, moe_w2):
    h_ctx, h_lat = ctx, x
    c_lat_act, c_ctx_act = jax.nn.silu(c), jax.nn.silu(c_ctx)
    for i in range(DEPTH):
        j = i // 2
        update_ctx = i < DEPTH - 1
        m_lat = jnp.split((c_lat_act @ w_ada[i] + b_ada[i])[:, None, :], 6, axis=-1)
        m_ctx = jnp.split(c_ctx_act @ w_ada[i] + b_ada[i], 6, axis=-1)
        a_lat = _modulate(_rms_norm(h_lat, norm_mix[i]), m_lat[0], m_lat[1])
        a_ctx = _modulate(_rms_norm(h_ctx, norm_mix[i]), m_ctx[0], m_ctx[1])
        if i % 2 == 0:
            o_ctx, o_lat = _rwkv_mamba_mixer(a_ctx, a_lat, mix_w_in[j], mix_w_out[j], rw_mu[j], rw_w0[j],
                                             rw_w_up[j], rw_a0[j], rw_a_up[j], rw_g_up[j], rw_k_k[j],
                                             rw_k_a[j], rw_r_k[j], rw_gn_w[j], rw_gn_b[j], mb_conv_w[j],
                                             mb_conv_b[j], mb_dt_bias[j], mb_a_log[j], mb_d[j], mb_norm_w[j])
        else:
            o_ctx, o_lat = _neighbourhood_attention(a_ctx, a_lat, na_w_qkv[j], na_w_out[j], na_rpb[j], update_ctx)

        def channel_mixer(t):
            if i % 2 == 0:
                return _swiglu(t, ffn_w1[j], ffn_w3[j], ffn_w2[j])
            return _moe_swiglu(t, moe_router_w[j], moe_router_b[j], moe_w1[j], moe_w3[j], moe_w2[j])

        h_lat = h_lat + m_lat[2] * o_lat
        h_lat = h_lat + m_lat[5] * channel_mixer(_modulate(_rms_norm(h_lat, norm_ffn[i]), m_lat[3], m_lat[4]))
        if update_ctx:
            h_ctx = h_ctx + m_ctx[2] * o_ctx
            h_ctx = h_ctx + m_ctx[5] * channel_mixer(_modulate(_rms_norm(h_ctx, norm_ffn[i]), m_ctx[3], m_ctx[4]))
    return _rms_norm(h_lat, norm_final)


CONV_WIDTH = 3
D_CONV = 512
N_DIFF_HEADS = 4
DIFF_QK_DIM = 64
DIFF_V_DIM = 128
D_ATTN = N_DIFF_HEADS * DIFF_V_DIM
N_FOURIER_GROUPS = 8
FOURIER_GROUP = D_MODEL // N_FOURIER_GROUPS
D_FF_2 = 4 * D_MODEL
Q_BLOCK = 128
ROPE_BASE = 10000.0
LN_EPS = 1e-6
SUBLN_EPS = 1e-5
DEEPNORM_ALPHA = (2.0 * DEPTH) ** 0.25
DEEPNORM_BETA = (8.0 * DEPTH) ** -0.25
N_EVEN = (DEPTH + 1) // 2
N_ODD = DEPTH // 2
COL_CONV = 3 * D_CONV
COL_Q = N_DIFF_HEADS * 2 * DIFF_QK_DIM
COL_K = N_DIFF_HEADS * 2 * DIFF_QK_DIM
COL_V = D_ATTN
Q0 = COL_CONV
K0 = Q0 + COL_Q
V0 = K0 + COL_K
D_IN = V0 + COL_V


def layer_norm(x):
    xf = x.astype(jnp.float32)
    mu = jnp.mean(xf, axis=-1, keepdims=True)
    var = jnp.mean(jnp.square(xf - mu), axis=-1, keepdims=True)
    return ((xf - mu) * lax.rsqrt(var + LN_EPS)).astype(x.dtype)

def layer_norm_affine(x, g, b):
    xf = x.astype(jnp.float32)
    mu = jnp.mean(xf, axis=-1, keepdims=True)
    var = jnp.mean(jnp.square(xf - mu), axis=-1, keepdims=True)
    y = (xf - mu) * lax.rsqrt(var + LN_EPS) * g.astype(jnp.float32) + b.astype(jnp.float32)
    return y.astype(x.dtype)

def modulation(cond, w, b):
    return jnp.split(jax.nn.silu(cond) @ w + b, 6, axis=-1)

def modulate(h, shift, scale):
    return layer_norm(h) * (1.0 + scale) + shift

def post_norm_residual(h, y, gate, g, b):
    return layer_norm_affine(DEEPNORM_ALPHA * h + gate * y, g, b)

def rope_1d(x, pos):
    half = x.shape[-1] // 2
    inv = ROPE_BASE ** (-jnp.arange(half, dtype=jnp.float32) / half)
    ang = pos.astype(jnp.float32)[:, None] * inv[None, :]
    cos = jnp.cos(ang)[:, None, None, :].astype(x.dtype)
    sin = jnp.sin(ang)[:, None, None, :].astype(x.dtype)
    x1, x2 = x[..., :half], x[..., half:]
    return jnp.concatenate([x1 * cos - x2 * sin, x1 * sin + x2 * cos], axis=-1)

def rope_2d(x, row, col):
    d = x.shape[-1] // 2
    return jnp.concatenate([rope_1d(x[..., :d], row), rope_1d(x[..., d:], col)], axis=-1)

def short_conv(u, w):
    n = u.shape[1]
    pad = CONV_WIDTH // 2
    up = jnp.pad(u, ((0, 0), (pad, pad), (0, 0)))
    return sum(up[:, t:t + n] * w[t] for t in range(CONV_WIDTH))

def conv_mixer(p, w):
    gb, gc, v = jnp.split(p, 3, axis=-1)
    return gb * short_conv(gc * v, w)

def heads_qk(p):
    return p.reshape(p.shape[0], p.shape[1], N_DIFF_HEADS, 2, DIFF_QK_DIM)

def heads_v(p):
    return p.reshape(p.shape[0], p.shape[1], N_DIFF_HEADS, DIFF_V_DIM)

def diff_attend(q, k, v, lam):
    s = jnp.einsum('bqhcd,bkhcd->bhcqk', q, k).astype(jnp.float32) * (DIFF_QK_DIM ** -0.5)
    p = jax.nn.softmax(s, axis=-1)
    pd = (p[:, :, 0] - lam * p[:, :, 1]).astype(v.dtype)
    return jnp.einsum('bhqk,bkhd->bqhd', pd, v)

def diff_attention_blocks(q, k, v, lam):
    b, n = q.shape[0], q.shape[1]
    nb = n // Q_BLOCK
    qb = q.reshape(b, nb, Q_BLOCK, N_DIFF_HEADS, 2, DIFF_QK_DIM).transpose(1, 0, 2, 3, 4, 5)
    out = lax.map(lambda blk: diff_attend(blk, k, v, lam), qb)
    return out.transpose(1, 0, 2, 3, 4).reshape(b, n, N_DIFF_HEADS, DIFF_V_DIM)

def sub_ln(o, g, lam_init):
    of = o.astype(jnp.float32)
    y = of * lax.rsqrt(jnp.mean(of * of, axis=-1, keepdims=True) + SUBLN_EPS)
    y = y * g.astype(jnp.float32) * (1.0 - lam_init)
    return y.reshape(o.shape[0], o.shape[1], D_ATTN).astype(o.dtype)

def fourier_mix(u):
    b, n, _ = u.shape
    ug = u.astype(jnp.float32).reshape(b, n, N_FOURIER_GROUPS, FOURIER_GROUP)
    f = jnp.fft.fft2(ug, axes=(1, 3), norm='ortho').real
    return f.reshape(b, n, D_MODEL).astype(u.dtype)

def sq_relu_mlp(u, w1, w2):
    return jnp.square(jax.nn.relu(u @ w1)) @ w2

def second_inputs(seed: int = 0) -> dict:
    key = jax.random.key(seed)
    ks = jax.random.split(key, 16)
    f32 = jnp.float32

    def nrm(k, shape, s):
        return s * jax.random.normal(k, shape, f32)

    return {
        'x': nrm(ks[0], (BATCH, SEQ, D_MODEL), 1.0),
        'c': nrm(ks[1], (BATCH, D_MODEL), 1.0),
        'ctx': nrm(ks[2], (BATCH, CTX_LEN, D_MODEL), 1.0),
        'c_ctx': nrm(ks[3], (D_MODEL,), 1.0),
        'ada_w': nrm(ks[4], (DEPTH, D_MODEL, 6 * D_MODEL), 0.5 * D_MODEL ** -0.5),
        'ada_b': nrm(ks[5], (DEPTH, 6 * D_MODEL), 0.01),
        'ln_g': 1.0 + nrm(ks[6], (DEPTH, 2, D_MODEL), 0.05),
        'ln_b': nrm(ks[7], (DEPTH, 2, D_MODEL), 0.02),
        'mlp_w1': nrm(ks[8], (DEPTH, D_MODEL, D_FF_2), D_MODEL ** -0.5),
        'mlp_w2': nrm(ks[9], (DEPTH, D_FF_2, D_MODEL), DEEPNORM_BETA * D_FF_2 ** -0.5),
        'w_in': nrm(ks[10], (N_EVEN, D_MODEL, D_IN), D_MODEL ** -0.5),
        'conv_w': nrm(ks[11], (N_EVEN, CONV_WIDTH, D_CONV), CONV_WIDTH ** -0.5),
        'lambda_qk': nrm(ks[12], (N_EVEN, 4, DIFF_QK_DIM), 0.1),
        'subln_g': 1.0 + nrm(ks[13], (N_EVEN, DIFF_V_DIM), 0.05),
        'w_out_mix': nrm(ks[14], (N_EVEN, D_CONV + D_ATTN, D_MODEL), DEEPNORM_BETA * (D_CONV + D_ATTN) ** -0.5),
        'w_out_fourier': nrm(ks[15], (N_ODD, D_MODEL, D_MODEL), DEEPNORM_BETA * D_MODEL ** -0.5),
    }

def second_block(x, c, ctx, c_ctx, ada_w, ada_b, ln_g, ln_b, mlp_w1, mlp_w2, w_in, conv_w, lambda_qk, subln_g, w_out_mix, w_out_fourier):
    n = x.shape[1]
    rows = n // GRID_W
    row = jnp.repeat(jnp.arange(rows, dtype=jnp.int32), GRID_W)
    col = jnp.tile(jnp.arange(GRID_W, dtype=jnp.int32), rows)
    last_attn = 2 * ((DEPTH - 1) // 2)
    cond_lat = c[:, None, :]
    cond_ctx = c_ctx[None, None, :]
    h, hc = x, ctx
    for i in range(DEPTH):
        j = i // 2
        update_ctx = i < last_attn
        sh1, sc1, g1, sh2, sc2, g2 = modulation(cond_lat, ada_w[i], ada_b[i])
        u = modulate(h, sh1, sc1)
        if update_ctx or i == last_attn:
            mc = modulation(cond_ctx, ada_w[i], ada_b[i])
            uc = modulate(hc, mc[0], mc[1])
        if i % 2 == 0:
            lam_init = 0.8 - 0.6 * math.exp(-0.3 * i)
            lq = lambda_qk[j].astype(jnp.float32)
            lam = jnp.exp(jnp.sum(lq[0] * lq[1])) - jnp.exp(jnp.sum(lq[2] * lq[3])) + lam_init
            p = u @ w_in[j]
            q = rope_2d(heads_qk(p[..., Q0:K0]), row, col)
            k = rope_2d(heads_qk(p[..., K0:V0]), row, col)
            v = heads_v(p[..., V0:])
            if update_ctx:
                pc = uc @ w_in[j]
                kvc = pc[..., K0:]
            else:
                kvc = uc @ w_in[j][:, K0:]
            kc = heads_qk(kvc[..., :COL_K])
            vc = heads_v(kvc[..., COL_K:])
            k_all = jnp.concatenate([k, kc], axis=1)
            v_all = jnp.concatenate([v, vc], axis=1)
            o = diff_attention_blocks(q, k_all, v_all, lam)
            y = jnp.concatenate([conv_mixer(p[..., :COL_CONV], conv_w[j]), sub_ln(o, subln_g[j], lam_init)], axis=-1) @ w_out_mix[j]
            if update_ctx:
                oc = diff_attend(heads_qk(pc[..., Q0:K0]), kc, vc, lam)
                yc = jnp.concatenate([conv_mixer(pc[..., :COL_CONV], conv_w[j]), sub_ln(oc, subln_g[j], lam_init)], axis=-1) @ w_out_mix[j]
        else:
            y = fourier_mix(u) @ w_out_fourier[j]
            if update_ctx:
                yc = fourier_mix(uc) @ w_out_fourier[j]
        h = post_norm_residual(h, y, g1, ln_g[i, 0], ln_b[i, 0])
        h = post_norm_residual(h, sq_relu_mlp(modulate(h, sh2, sc2), mlp_w1[i], mlp_w2[i]), g2, ln_g[i, 1], ln_b[i, 1])
        if update_ctx:
            hc = post_norm_residual(hc, yc, mc[2], ln_g[i, 0], ln_b[i, 0])
            hc = post_norm_residual(hc, sq_relu_mlp(modulate(hc, mc[3], mc[4]), mlp_w1[i], mlp_w2[i]), mc[5], ln_g[i, 1], ln_b[i, 1])
    return h


def setup_inputs(seed=0):
    out = dict(first_inputs(seed))
    for name, value in second_inputs(seed + 1).items():
        if name != "x":
            out[name + "_2"] = value
    return out


def reference(
    x, c, ctx, c_ctx, w_ada, b_ada, norm_mix, norm_ffn, norm_final, mix_w_in, mix_w_out, rw_mu,
    rw_w0, rw_w_up, rw_a0, rw_a_up, rw_g_up, rw_k_k, rw_k_a, rw_r_k, rw_gn_w, rw_gn_b,
    mb_conv_w, mb_conv_b, mb_dt_bias, mb_a_log, mb_d, mb_norm_w, ffn_w1, ffn_w3, ffn_w2,
    na_w_qkv, na_w_out, na_rpb, moe_router_w, moe_router_b, moe_w1, moe_w3, moe_w2, c_2, ctx_2,
    c_ctx_2, ada_w_2, ada_b_2, ln_g_2, ln_b_2, mlp_w1_2, mlp_w2_2, w_in_2, conv_w_2,
    lambda_qk_2, subln_g_2, w_out_mix_2, w_out_fourier_2,
):
    x = first_block(
        x, c, ctx, c_ctx, w_ada, b_ada, norm_mix, norm_ffn, norm_final, mix_w_in, mix_w_out,
        rw_mu, rw_w0, rw_w_up, rw_a0, rw_a_up, rw_g_up, rw_k_k, rw_k_a, rw_r_k, rw_gn_w,
        rw_gn_b, mb_conv_w, mb_conv_b, mb_dt_bias, mb_a_log, mb_d, mb_norm_w, ffn_w1, ffn_w3,
        ffn_w2, na_w_qkv, na_w_out, na_rpb, moe_router_w, moe_router_b, moe_w1, moe_w3, moe_w2,
    )
    return second_block(
        x, c_2, ctx_2, c_ctx_2, ada_w_2, ada_b_2, ln_g_2, ln_b_2, mlp_w1_2, mlp_w2_2, w_in_2,
        conv_w_2, lambda_qk_2, subln_g_2, w_out_mix_2, w_out_fourier_2,
    )


_drawn_inputs = setup_inputs


def setup_inputs(seed=0):
    import zlib

    import numpy as np

    out = dict(_drawn_inputs(seed))
    spreads = {}
    factors = {'rw_w_up': 5.039,
     'rw_k_k': 2.896,
     'rw_k_a': 2.956,
     'rw_gn_w': 5.097,
     'rw_gn_b': 19.76,
     'mb_conv_b': 4.258,
     'mb_d': 4.603,
     'mb_norm_w': 2.811,
     'na_rpb': 27.257,
     'moe_router_b': 17.977,
     'ctx_2': 3.707,
     'ada_b_2': 5.807,
     'lambda_qk_2': 8.0,
     'subln_g_2': 8.0}
    for name, (base, spread) in spreads.items():
        noise = np.random.default_rng([zlib.crc32(name.encode()), seed]).standard_normal(out[name].shape)
        drawn = base * np.exp(spread * noise) if base else spread * noise
        out[name] = jnp.asarray(drawn.astype(out[name].dtype))
    for name, factor in factors.items():
        out[name] = (out[name] * factor).astype(out[name].dtype)
    return out
```

```python
import math
from contextlib import ExitStack

import numpy as np

import concourse.bass as bass
from concourse import mybir

F32 = mybir.dt.float32
ALU = mybir.AluOpType
ACT = mybir.ActivationFunctionType
AX = mybir.AxisListType

P = 128
D = 1024
KT = D // P
TC = 256
TL = 256
T = TC + TL
NCH = T // P
CTX, LAT = slice(0, TC), slice(TC, T)
SEQS = (CTX, LAT)
RMS_EPS, LN_EPS, GN_EPS, SUBLN_EPS = 1e-6, 1e-6, 64e-5, 1e-5
RW = 512
HD = 64
RW_COLS = 3 * RW + 64 + 64 + 96
ZG0 = RW_COLS
XBC0 = ZG0 + RW
DT0 = XBC0 + 1024
FF = 2816
FT = FF // P
FF2 = 4096
F2T = FF2 // P
NE = 8
GRID_W, NA_KW = 64, 16
ALPHA = 4.0 ** 0.25
LAM_INIT = 0.8 - 0.6 * math.exp(0.0)
DECAY = math.exp(-0.5)

RING = 6
SLOT = FT * P

COLUMNS = [("b_ada", 96), ("ada_b_2", 96), ("norm_mix", 16), ("norm_ffn", 16), ("norm_final", 8),
           ("c", 8), ("c_ctx", 8), ("c_2", 8), ("c_ctx_2", 8), ("rw_a0", 8), ("rw_k_k", 4),
           ("rw_k_a", 4), ("rw_r_k", 8), ("rw_gn_w", 4), ("rw_gn_b", 4), ("mb_conv_w", 40),
           ("mb_conv_b", 8), ("mb_norm_w", 4), ("mu_prev", 13), ("mu_next", 13), ("ln_g_2", 32),
           ("ln_b_2", 32), ("conv_w_2", 12), ("subln_g_2", 1)]
ROWS = [("mb_dt_bias", 16), ("mb_a_log", 16), ("mb_d", 8), ("moe_router_b", 8), ("lambda_qk_2", 256)]


def offsets(parts):
    out, n = {}, 0
    for name, width in parts:
        out[name] = n
        n += width
    return out, n


COL, NCOL = offsets(COLUMNS)
ROW, NROW = offsets(ROWS)

CONSTS = [("ident", 128), ("mean", 128), ("head", 128), ("upper", 128), ("upper_in", 128),
          ("lower", 128), ("lower_in", 128), ("diag16", 128), ("off32", 128), ("off64", 128),
          ("off128", 128), ("decay_f", 258), ("decay_b", 258), ("cs128", 256), ("dft_c", 512),
          ("dft_s", 512), ("cos", 256), ("sin", 256), ("turn", 128), ("win", 64), ("out_win", 64),
          ("first", 64), ("ones", 128)]
CO, NCONST = offsets(CONSTS)
BIG = -1e30


def constants():
    i = np.arange(P)[:, None]
    t = np.arange(P)[None, :]
    c = {}
    c["ident"] = i == t
    c["mean"] = np.full((P, P), 1.0 / D)
    c["ones"] = np.ones((P, P))
    c["head"] = i // HD == t // HD
    c["upper"], c["upper_in"], c["lower"], c["lower_in"] = i < t, i <= t, i > t, i >= t
    c["diag16"] = i // 16 == t // 16
    for size in (32, 64, 128):
        c[f"off{size}"] = (i // size == t // size) & (i // (size // 2) != t // (size // 2))
    mid = P // 2
    c["decay_f"] = -DECAY * np.concatenate(
        [(i <= t) * 1.0 - (i < mid), (i < t) * 1.0 - (i < mid), i < mid, i >= mid], 1)
    c["decay_b"] = -DECAY * np.concatenate(
        [(i >= t) * 1.0 - (i >= mid), (i > t) * 1.0 - (i >= mid), i >= mid, i < mid], 1)
    ang = 2 * np.pi * ((i * t) % P) / P
    c["cs128"] = np.concatenate([np.cos(ang), np.sin(ang)], 1)
    n = np.arange(TL)
    ang = 2 * np.pi * ((n[:, None] * n[None, :]) % TL) / TL
    norm = 1 / math.sqrt(TL * P)
    c["dft_c"] = (norm * np.cos(ang)).reshape(2, P, TL).transpose(1, 0, 2).reshape(P, 512)
    c["dft_s"] = (-norm * np.sin(ang)).reshape(2, P, TL).transpose(1, 0, 2).reshape(P, 512)
    half = 16
    inv = np.float32(10000.0) ** (-np.arange(half, dtype=np.float32) / np.float32(half))
    ch = np.arange(P)
    pos = np.where((ch % 64 < 32)[:, None], (n // GRID_W)[None, :], (n % GRID_W)[None, :])
    ang = pos.astype(np.float32) * inv[ch % half][:, None].astype(np.float32)
    c["cos"], c["sin"] = np.cos(ang), np.sin(ang)
    turn = np.zeros((P, P))
    for m in range(P):
        if m % 32 < half:
            turn[m + half, m] = -1.0
        else:
            turn[m - half, m] = 1.0
    c["turn"] = turn
    q, k = np.arange(P)[:, None] % GRID_W, np.arange(GRID_W)[None, :]
    start = np.clip(q - NA_KW // 2, 0, GRID_W - NA_KW)
    win = (k >= start) & (k < start + NA_KW)
    c["win"], c["out_win"] = win, np.where(win, 0.0, BIG)
    a, b = np.arange(NE)[:, None], np.arange(NE)[None, :]
    c["first"] = np.broadcast_to((b < a).reshape(1, 64), (P, 64))
    return np.ascontiguousarray(
        np.concatenate([np.asarray(c[n], np.float32) for n, _ in CONSTS], 1))


def plan_slots(w):
    slots, first = [], {}

    def add(name, source, k0, kt, cols):
        first[name] = len(slots)
        for n0, width in cols:
            src = source[k0:k0 + kt * P, n0:n0 + width].rearrange("(k p) n -> p k n", p=P)
            slots.append((kt, width, src))

    def by(start, n, width=256):
        return [(start + n0, min(width, n - n0)) for n0 in range(0, n, width)]

    def align():
        while len(slots) % RING:
            slots.append(None)

    first["ada"] = 0
    slots += ["ada"] * 96
    win = w["mix_w_in"][0]
    add("zg", win, 0, KT, by(ZG0, RW))
    add("dt", win, 0, KT, [(DT0, 16)])
    add("xbc", win, 0, KT, by(XBC0, 1024))
    add("rkv", win, 0, KT, by(0, 3 * RW))
    add("lora", win, 0, KT, [(3 * RW, 224)])
    first["rwkv_end"] = len(slots)
    add("mix_out", w["mix_w_out"][0], 0, KT, by(0, D))
    first["ffn"] = len(slots)
    for b in range(FT // 2):
        add(("ffn1", b), w["ffn_w1"][0], 0, KT, [(256 * b, 256)])
        add(("ffn3", b), w["ffn_w3"][0], 0, KT, [(256 * b, 256)])
    add("ffn2", w["ffn_w2"][0], 0, FT, by(0, D, P))
    add("qkv", w["na_w_qkv"][0], 0, KT, by(0, 3 * D))
    add("na_out", w["na_w_out"][0], 0, KT, by(0, D))
    add("router", w["moe_router_w"][0], 0, KT, [(0, NE)])
    align()
    first["moe"] = len(slots)
    slots += ["moe"] * (NE * 30)
    add("in2", w["w_in_2"][0], 0, KT, by(0, 3072))
    add("out2", w["w_out_mix_2"][0], 0, KT, by(0, D))

    def mlp(i):
        add(("mlp1", i), w["mlp_w1_2"][i], 0, KT, by(0, FF2))
        first["mlp2", i] = len(slots)
        for n in range(KT):
            for half in range(2):
                add(("mlp2", i, n, half), w["mlp_w2_2"][i], half * 16 * P, 16, [(n * P, P)])

    mlp(0)
    add("fourier", w["w_out_fourier_2"][0], 0, KT, by(0, D))
    mlp(1)
    return slots, first


class Counts:

    def __init__(self, known=None):
        self.known = known
        self.count = {}
        self.values = {}

    def did(self, engine, *names):
        self.count[engine] = self.count.get(engine, 0) + 1
        for name in names:
            assert (engine, name) not in self.values, (engine, name)
            self.values[engine, name] = self.count[engine]
        return 1

    def at(self, engine, name):
        return 1 if self.known is None else self.known[engine, name]

    def now(self, engine):
        return self.count[engine]

    def loop(self, engine, name, before, turns):
        per = self.count.get(engine, 0) - before
        self.values[engine, ("per", name)] = per
        self.count[engine] = before + per * turns
        self.values[engine, ("end", name)] = self.count[engine]


def build(nc, w, out, counts, stop="end"):
    did, at, now = counts.did, counts.at, counts.now
    SY, PE, AC, VE = "sync", "tensor", "scalar", "vector"
    slots, first = plan_slots(w)
    with ExitStack() as ctx:
        def sb(name, cols, *shape):
            t = ctx.enter_context(nc.sbuf_tensor(name, [P, cols], F32))
            return t[:, :]

        def sem(name):
            return ctx.enter_context(nc.semaphore(name))

        def cut(t, start, *dims):
            n = int(np.prod(dims))
            ap = t[:, start:start + n]
            if len(dims) == 2:
                ap = ap.rearrange("p (a b) -> p a b", a=dims[0])
            if len(dims) == 3:
                ap = ap.rearrange("p (a b c) -> p a b c", a=dims[0], b=dims[1])
            if len(dims) == 4:
                ap = ap.rearrange("p (a b c d) -> p a b c d", a=dims[0], b=dims[1], c=dims[2])
            return ap

        consts, cols, rows = sb("consts", NCONST), sb("cols", NCOL), sb("rows", NROW)
        h_t, a_t, mix_t = sb("h", KT * T), sb("a", KT * T), sb("mix", KT * T)
        hT, aT, mix = (cut(t, 0, KT, T) for t in (h_t, a_t, mix_t))
        ring_t = sb("ring", RING * SLOT)
        csil = cut(sb("csil", 32), 0, 2, KT, 2)
        mods = cut(sb("mods", 384), 0, 192, 2)
        gs = cut(sb("gs", 128), 0, 8, KT, 2)
        tmpA, tmpB = sb("tmpA", T), sb("tmpB", T)
        small = sb("small", 800)
        arena = sb("arena", 15872)
        bank = [ctx.enter_context(nc.psum_tensor(f"bank{b}", [P, 512], F32))[:, :] for b in range(8)]

        def const(name, width=128):
            return consts[:, CO[name]:CO[name] + width]

        def col(name, k, n=1):
            return cols[:, COL[name] + k:COL[name] + k + n]

        def row(name, n):
            return rows[:, ROW[name]:ROW[name] + n]

        def mod(block, layer, piece, k, s):
            return mods[:, 96 * block + 48 * layer + 8 * piece + k, s:s + 1]

        ident = const("ident")
        loaded = sem("loaded")
        w_full = [sem(f"w_full{i}") for i in range(RING)]
        pe_done, act_done, vec_done = sem("pe_done"), sem("act_done"), sem("vec_done")
        ctx2_in, bias_in, up_in, stored = sem("ctx2_in"), sem("bias_in"), sem("up_in"), sem("stored")

        def slot(s):
            kt, width, _ = slots[s]
            return cut(ring_t, (s % RING) * SLOT, kt, width)

        def filled(s):
            return 16 * sum(slots[i] is not None for i in range(s % RING, s + 1, RING))

        xpad = cut(arena, 0, 8, 2, TC + 4)
        xb = cut(arena, 4160, 8, T)
        xt = cut(arena, 8256, NCH, RW)
        bt = cut(arena, 10304, NCH, 256)
        zg = cut(arena, 11328, NCH, RW)
        ym = cut(arena, 13376, NCH, RW)
        gram = cut(arena, 0, 2, 2, NCH, P)
        xdt = cut(arena, 2048, NCH, RW)
        dec_t, mt_t = mix_t[:, 0:1024], mix_t[:, 1024:2048]
        dec, mt = cut(mix_t, 0, 8, P), cut(mix_t, 1024, 8, P)
        xd2, st_m = tmpA, tmpB
        dt_raw, dtv, a_tok, cs, ecs, sp1 = (cut(small, 64 * i, NCH, 2, 8) for i in range(6))
        a_neg, etot, dcs = small[:, 384:400], small[:, 400:408], small[:, 408:416]
        ss_m, rs_m = cut(small, 416, NCH, 2), cut(small, 424, NCH, 2)

        r_, k_, v_ = (cut(arena, 2048 * i, 4, T) for i in range(3))
        kk = cut(arena, 6144, 4, T)
        vt = cut(arena, 8192, NCH, RW)
        llw, llg = arena[:, 10240:10752], arena[:, 10752:11264]
        upw, gup = arena[:, 11264:11776], arena[:, 11776:12288]
        w0row = arena[:, 12288:13312]
        zpad = [cut(arena, 13312 + 516 * i, 2, TC + 2) for i in range(4)]
        mu0 = small[:, 0:13]
        mu0g, mug = small[:, 13:14], small[:, 14:16]
        sig = [cut(ring_t, 2048 * d, NCH, RW) for d in range(2)]
        ic = [cut(ring_t, 4096 + 2048 * d, 4, T) for d in range(2)]
        kd = [cut(ring_t, 8192 + 2048 * d, 4, T) for d in range(2)]
        yt = cut(ring_t, 12288, NCH, RW)
        gate, bonus = cut(a_t, 0, 4, T), cut(a_t, 2048, 4, T)
        kdka = cut(mix_t, 0, 4, T)

        free = {"arena": [10240, 15872], "k": [2048, 4096], "v": [4096, 6144], "mix": [0, 2048],
                "ring": [14336, 16896]}
        of = {"arena": arena, "k": arena, "v": arena, "mix": mix_t, "ring": ring_t}

        def take(where, *dims):
            start = free[where][0]
            free[where][0] += int(np.prod(dims))
            assert free[where][0] <= free[where][1], where
            return cut(of[where], start, *dims)

        ex, ei = take("arena", 2, 258), take("arena", 2, P)
        ar = take("arena", 2, 256)
        bh, kh = take("arena", 2, P), take("arena", 2, P)
        sin_ = take("arena", 2, P)
        bkt = take("arena", 4, P)
        bb = take("k", 4, 256)
        kb = take("k", 4, 256)
        dm = take("arena", 4, P)
        D_, E_ = [take("arena", 4, P) for _ in range(2)], [take("v", 4, P) for _ in range(2)]
        T_, TT_ = [take("ring", 4, P) for _ in range(2)], [take("ring", 4, P) for _ in range(2)]
        bm, zt = take("v", 4, P), take("v", 4, P)
        xs, us = take("mix", 2, P), take("mix", 2, P)
        stt_ = take("mix", 2, P)
        state = take("mix", 8, P)

        G = cut(arena, 0, FT, T)
        sg = [tmpA, tmpB]

        q1 = cut(arena, 0, KT, TL)
        k1 = cut(mix_t, 0, KT, T)
        v1 = cut(arena, 2048, NCH, D)
        rb = cut(arena, 6144, 16, 6 * GRID_W)
        pr = cut(arena, 12288, 2, T)
        pt = cut(arena, 13312, NCH, TL)
        stat = small[:, 0:16]
        o1 = cut(a_t, 0, KT, TL)

        Gm = cut(arena, 0, FT, TL)
        gbc = cut(arena, 5632, NE, TL)
        sgm = [cut(arena, 7680 + 256 * i, TL) for i in range(2)]
        um = [cut(arena, 8192 + 256 * i, TL) for i in range(2)]
        lg, gates, ge, rank = (cut(small, 16 * i, 2, NE) for i in range(4))
        cmp_, cm2 = cut(small, 64, 2, NE, NE), cut(small, 192, 2, NE, NE)
        mx, sm = small[:, 320:322], small[:, 322:324]

        gb = cut(arena, 0, 4, TL)
        gc = cut(arena, 1024, 4, TL)
        vp = cut(arena, 2048, 4, TL + 2)
        q2, k2 = cut(arena, 3080, 4, TL), cut(arena, 4104, 4, T)
        v2 = cut(arena, 6152, NCH, 512)
        p2 = cut(arena, 8200, 4, T)
        pt2 = cut(arena, 10248, NCH, TL)
        o2 = cut(arena, 11272, 4, TL)
        rt = cut(arena, 12296, 2, TL)
        pd = cut(arena, 12808, 2, T)
        lamv = small[:, 0:8]
        lprod = cut(small, 16, 4, 64)
        G2 = cut(arena, 0, F2T, TL)
        fab = cut(arena, 0, 2, KT, 256)

        block = ctx.enter_context(nc.Block())

        @block.sync
        def _(sy):
            for dst, src in ((consts, w["consts"]), (cols, w["cols"]), (rows, w["rows"]),
                             (hT[:, :, CTX], w["ctxT"].rearrange("(k p) n -> p k n", p=P)),
                             (hT[:, :, LAT], w["xT"].rearrange("(k p) n -> p k n", p=P))):
                sy.dma_start(dst, src).then_inc(loaded, 16)

            def load(s):
                if slots[s] is None:
                    return
                old = s - RING
                while slots[old] is None:
                    old -= RING
                if isinstance(slots[old], str):
                    sy.wait_ge(pe_done, at(PE, ("end", slots[old])))
                else:
                    sy.wait_ge(pe_done, at(PE, ("slot", old)))
                sy.dma_start(slot(s), slots[s][2]).then_inc(w_full[s % RING], 16)

            n = 0
            for b, name in enumerate(("w_ada", "ada_w_2")):
                for layer in range(2):
                    src = w[name][layer].rearrange("(k p) n -> p k n", p=P)
                    if not n:
                        for s in range(RING):
                            sy.dma_start(cut(ring_t, s * SLOT, KT, 256),
                                         src[:, :, s * 256:s * 256 + 256]).then_inc(w_full[s], 16)
                    with sy.Fori(0 if n else 1, 4) as turn:
                        for s in range(RING):
                            sy.wait_ge(pe_done, turn * RING + ((n - 1) * RING + s + 1))
                            sy.dma_start(cut(ring_t, s * SLOT, KT, 256),
                                         src[:, :, bass.ds(turn * 1536 + s * 256, 256)]
                                         ).then_inc(w_full[s], 16)
                    n += 4
            s = 96
            while s < len(slots):
                if s == first["mix_out"]:
                    sy.wait_ge(vec_done, at(VE, "ym end"))
                    sy.wait_ge(pe_done, at(PE, ("ym turned", 3)))
                    up = w["rw_w_up"][0].rearrange("d l c -> (d l) c")
                    sy.dma_start(upw[0:64, :], up).then_inc(up_in, 16)
                    up = w["rw_a_up"][0].rearrange("d l c -> (d l) c")
                    sy.dma_start(upw[64:128, :], up).then_inc(up_in, 16)
                    sy.dma_start(gup[0:96, :], w["rw_g_up"][0]).then_inc(up_in, 16)
                    sy.dma_start(w0row, w["w0row"]).then_inc(up_in, 16)
                    sy.dma_start(mug[0:96, :], w["mu_g"]).then_inc(up_in, 16)
                    sy.wait_ge(vec_done, at(VE, "o_rw"))
                    sy.wait_ge(pe_done, at(PE, ("yr turned", 3)))
                if s == first["qkv"]:
                    sy.wait_ge(pe_done, at(PE, ("ffn out", KT - 1)))
                    sy.dma_start(rb.rearrange("p h n -> p (h n)"), w["bias"]).then_inc(bias_in, 16)
                if slots[s] == "moe":
                    for b in range(s - RING, s):
                        if slots[b] is not None:
                            sy.wait_ge(pe_done, at(PE, ("slot", b)))
                    per = at(PE, ("per", "moe"))
                    with sy.Fori(0, NE) as e:
                        for i in range(30):
                            prev = (i - RING) % 30
                            if i < RING:
                                sy.wait_ge(pe_done, e * per + (at(PE, ("moe slot", prev)) - per))
                            else:
                                sy.wait_ge(pe_done, e * per + at(PE, ("moe slot", prev)))
                            if i < 22:
                                src = w["moe_w1" if i % 2 == 0 else "moe_w3"][0]
                                src = src.rearrange("e (k p) n -> e p k n", p=P)
                                src = src[bass.ds(e, 1), :, :, (i // 2) * 256:(i // 2 + 1) * 256]
                                dst = cut(ring_t, (i % RING) * SLOT, KT, 256)
                            else:
                                src = w["moe_w2"][0].rearrange("e (k p) n -> e p k n", p=P)
                                src = src[bass.ds(e, 1), :, :, (i - 22) * P:(i - 21) * P]
                                dst = cut(ring_t, (i % RING) * SLOT, FT, P)
                            src = src.rearrange("e p k n -> p (e k) n")
                            sy.dma_start(dst, src).then_inc(w_full[i % RING], 16)
                    s += NE * 30
                    continue
                load(s)
                if s == first["qkv"] + 11:
                    sy.wait_ge(vec_done, at(VE, ("norm", 2, KT - 1)))
                    sy.dma_start(hT[:, :, CTX], w["ctx2T"].rearrange("(k p) n -> p k n", p=P)
                                 ).then_inc(ctx2_in, 16)
                s += 1
            sy.wait_ge(act_done, at(AC, ("norm", 12, KT - 1, 1)))
            sy.dma_start(out.rearrange("(k p) n -> p k n", p=P), hT[:, :, LAT]).then_inc(stored, 16)
            sy.wait_ge(stored, 16)

        @block.tensor
        def _(pe):
            mm = nc.tensor.matmul

            def full(s):
                pe.wait_ge(w_full[s % RING], filled(s))
                return slot(s)

            def across(st, sl, src, b, name):
                n = sl.stop - sl.start
                for k in range(KT):
                    i = mm(bank[b][:, 0:n], const("mean"), src[:, k, sl], start=(k == 0),
                           stop=(k == KT - 1))
                i.then_inc(pe_done, did(PE, (name, st)))

            def rms(st, sl):
                pe.wait_ge(act_done, at(AC, ("square", st)))
                across(st, sl, mix, 0, "norm sum")

            def ln(st, sl):
                across(st, sl, hT, 1, "norm mean")
                rms(st, sl)

            def product(name, s0, n_slots, rhs, sl, banks, before):
                n = sl.stop - sl.start
                j = 0
                for s in range(s0, s0 + n_slots):
                    ws = full(s)
                    for t in range(2):
                        b = banks[j % len(banks)]
                        if j >= len(banks):
                            before(j - len(banks))
                        for k in range(KT):
                            i = mm(bank[b][:, 0:n], ws[:, k, t * P:t * P + P], rhs[:, k, sl],
                                   start=(k == 0), stop=(k == KT - 1))
                        marks = [(name, j)] + ([("slot", s)] if t else [])
                        i.then_inc(pe_done, did(PE, *marks))
                        j += 1

            pe.wait_ge(loaded, 5 * 16)
            pe.wait_ge(act_done, at(AC, ("cond", 3)))
            n = 0
            for b in range(2):
                for layer in range(2):
                    before = counts.count.get(PE, 0)
                    with pe.Fori(0, 4) as turn:
                        for s in range(RING):
                            pe.wait_ge(w_full[s], turn * 16 + 16 * (n + 1))
                            ws = cut(ring_t, s * SLOT, KT, 256)
                            for t in range(2):
                                for k in range(KT):
                                    i = mm(bank[7][:, bass.ds(turn * 24 + n * 24 + 4 * s + 2 * t, 2)],
                                           ws[:, k, t * P:t * P + P], csil[:, b, k, :],
                                           start=(k == 0), stop=(k == KT - 1))
                            i.then_inc(pe_done, did(PE, ("ada", b, layer, s)))
                    n += 4
                    counts.loop(PE, "ada" if n == 16 else ("ada", b, layer), before, 4)

            rms(0, slice(0, T))
            pe.wait_ge(act_done, at(AC, ("norm", 0, KT - 1, 1)))
            for half in range(2):
                s = first["zg"] + half
                ws = full(s)
                for c in range(NCH):
                    for k in range(KT):
                        i = mm(bank[2 + c][:, half * 256:half * 256 + 256], aT[:, k, c * P:c * P + P],
                               ws[:, k, :], start=(k == 0), stop=(k == KT - 1),
                               skip_group_check=True)
                i.then_inc(pe_done, did(PE, ("zg", half), ("slot", s)))
            s = first["dt"]
            ws = full(s)
            for c in range(NCH):
                for k in range(KT):
                    i = mm(bank[6][:, 16 * c:16 * c + 16], aT[:, k, c * P:c * P + P], ws[:, k, :],
                           start=(k == 0), stop=(k == KT - 1), skip_group_check=True)
            i.then_inc(pe_done, did(PE, "dt", ("slot", s)))
            product("xbc", first["xbc"], 4, aT, slice(0, T), [0, 1],
                    lambda j: pe.wait_ge(act_done, at(AC, ("xbc", j))))

            def turned(name, src, b, sources=4):
                for m in range(sources):
                    i = nc.tensor.transpose(bank[b][:, m * P:m * P + P], src(m), ident)
                i.then_inc(pe_done, did(PE, name))

            pe.wait_ge(act_done, at(AC, ("xb", 7)))
            pe.wait_ge(act_done, at(AC, ("zg", 3)))
            for c in range(NCH):
                cs_ = slice(c * P, c * P + P)
                if c >= 2:
                    pe.wait_ge(vec_done, at(VE, ("bt", c - 2)))
                turned(("xt", c), lambda m: xb[:, m, cs_], 2 + c % 2)
                turned(("bt", c), lambda m: xb[:, 4 + m, cs_], 4 + c % 2, 2)
            for g in range(2):
                for c in range(NCH):
                    cs_ = slice(c * P, c * P + P)
                    i = mm(bank[g][:, c * P:c * P + P], xb[:, 4 + g, cs_], xb[:, 6 + g, cs_],
                           start=True, stop=True, skip_group_check=True)
            i.then_inc(pe_done, did(PE, "gram"))
            pe.wait_ge(vec_done, at(VE, "a_tok"))
            for c in range(NCH):
                for d in range(2):
                    i = mm(bank[6][:, 16 * c + 8 * d:16 * c + 8 * d + 8],
                           const("upper_in" if d == 0 else "lower_in"), a_tok[:, c, d, :],
                           start=True, stop=True, skip_group_check=True)
            i.then_inc(pe_done, did(PE, "cs"))
            u = 0
            for d in range(2):
                for step in range(NCH):
                    c = step if d == 0 else step ^ 1
                    cs_ = slice(c * P, c * P + P)
                    if u:
                        pe.wait_ge(vec_done, at(VE, ("dcs", u - 1)))
                    else:
                        pe.wait_ge(vec_done, at(VE, ("gram", 1)))
                        pe.wait_ge(vec_done, at(VE, ("bt", 3)))
                    for h in range(8):
                        i = mm(bank[h // 4][:, (h % 4) * P:(h % 4) * P + P],
                               a_tok[:, c, d, h:h + 1].broadcast_to([P, P]),
                               const("upper_in" if d == 0 else "lower_in"),
                               start=True, stop=True, skip_group_check=True)
                    i.then_inc(pe_done, did(PE, ("decay", u)))
                    if step:
                        for g in range(2):
                            i = mm(bank[3][:, 256 * g:256 * g + 256], xb[:, 6 + g, cs_],
                                   st_m[:, 256 * g:256 * g + 256], start=True, stop=True,
                                   skip_group_check=True)
                        i.then_inc(pe_done, did(PE, ("y off", u)))
                    pe.wait_ge(vec_done, at(VE, ("mt", u)))
                    for h in range(8):
                        i = mm(bank[2][:, h * HD:h * HD + HD], mt[:, h, :],
                               xdt[:, c, h * HD:h * HD + HD], start=True, stop=True,
                               skip_group_check=True)
                    i.then_inc(pe_done, did(PE, ("y diag", u)))
                    pe.wait_ge(vec_done, at(VE, ("xd2", u)))
                    for g in range(2):
                        i = mm(bank[4][:, 256 * g:256 * g + 256], bt[:, c, g * P:g * P + P],
                               xd2[:, 256 * g:256 * g + 256], start=True, stop=True,
                               skip_group_check=True)
                    i.then_inc(pe_done, did(PE, ("states", u)))
                    pe.wait_ge(vec_done, at(VE, ("unit", u)))
                    u += 1
            pe.wait_ge(vec_done, at(VE, "ym end"))
            for j in range(4):
                turned(("ym turned", j), lambda m: ym[:, m, j * P:j * P + P], 2 + j)

            product("rkv", first["rkv"], 6, aT, slice(0, T), [0, 1],
                    lambda j: pe.wait_ge(act_done, at(AC, ("rkv", j))))
            s = first["lora"]
            ws = full(s)
            for t, m in ((0, 128), (1, 96)):
                pe.wait_ge(act_done, at(AC, ("rkv", 10 + t)))
                for k in range(KT):
                    i = mm(bank[t][0:m, :], ws[:, k, t * P:t * P + m], aT[:, k, :],
                           start=(k == 0), stop=(k == KT - 1))
                i.then_inc(pe_done, did(PE, ("rkv", 12 + t), *([("slot", s)] if t else [])))
            pe.wait_ge(act_done, at(AC, ("norm ym", 3)))
            pe.wait_ge(vec_done, at(VE, ("shift", 11)))
            for c in range(NCH):
                turned(("vt", c), lambda m: v_[:, m, c * P:c * P + P], 4 + c)
            pe.wait_ge(act_done, at(AC, "lg"))
            pe.wait_ge(up_in, 5 * 16)
            for d in range(2):
                for c in range(NCH):
                    b = c % 2
                    if c >= 2 or d:
                        pe.wait_ge(vec_done, at(VE, ("w0", d if c >= 2 else 0, (c - 2) % 4)))
                    else:
                        pe.wait_ge(act_done, at(AC, ("rkv", 12 + c)))
                    mm(bank[b], llw[32 * d:32 * d + 32, c * P:c * P + P],
                       upw[32 * d:32 * d + 32, :], start=True, stop=True
                       ).then_inc(pe_done, did(PE, ("w", d, c)))
            n = 0
            for d in range(2):
                for j in range(4):
                    b = 2 + n % 2
                    if n >= 2:
                        pe.wait_ge(act_done, at(AC, ("ic", (n - 2) // 4, (n - 2) % 4)))
                    else:
                        pe.wait_ge(vec_done, at(VE, ("w0", 0, 1)))
                    mm(bank[b], upw[64 + 32 * d:96 + 32 * d, j * P:j * P + P],
                       llw[64 + 32 * d:96 + 32 * d, :], start=True, stop=True
                       ).then_inc(pe_done, did(PE, ("ic", d, j)))
                    n += 1
            for j in range(4):
                if j >= 2:
                    pe.wait_ge(act_done, at(AC, ("gate", j - 2)))
                else:
                    pe.wait_ge(vec_done, at(VE, ("w0", 1, 2 + j)))
                mm(bank[j % 2], gup[0:96, j * P:j * P + P], llg[0:96, :], start=True, stop=True
                   ).then_inc(pe_done, did(PE, ("gate", j)))
            for j in range(4):
                pe.wait_ge(vec_done, at(VE, ("kk sq", j)))
                if j == 0:
                    pe.wait_ge(act_done, at(AC, ("vt", 3)))
                mm(bank[4 + j], const("head"), kdka[:, j, :], start=True, stop=True
                   ).then_inc(pe_done, did(PE, ("kk", j)))
            for j in range(4):
                pe.wait_ge(vec_done, at(VE, ("rk", j)))
                if j == 0:
                    pe.wait_ge(vec_done, at(VE, ("kk", 3)))
                mm(bank[4 + j], const("head"), kdka[:, j, :], start=True, stop=True
                   ).then_inc(pe_done, did(PE, ("rk", j)))

            u = 0
            for d in range(2):
                for step in range(NCH):
                    c = step if d == 0 else step ^ 1
                    cs_ = slice(c * P, c * P + P)
                    for pg in range(2):
                        if u:
                            pe.wait_ge(vec_done, at(VE, ("state", u - 1)))
                        else:
                            pe.wait_ge(vec_done, at(VE, "bonus"))
                            pe.wait_ge(act_done, at(AC, ("gate", 3)))
                            pe.wait_ge(act_done, at(AC, ("sig", 1, 3)))
                        for jj in range(2):
                            j = 2 * pg + jj
                            mm(bank[jj][:, 0:258], sig[d][:, c, j * P:j * P + P],
                               const("decay_f" if d == 0 else "decay_b", 258), start=True, stop=True
                               ).then_inc(pe_done, did(PE, ("decays", u, jj)))
                        pe.wait_ge(vec_done, at(VE, ("kh", u)))
                        for m in range(4):
                            i = nc.tensor.transpose(bank[2][:, m * P:m * P + P],
                                                    (bh if m < 2 else kh)[:, m % 2, :], ident)
                        i.then_inc(pe_done, did(PE, ("bkt", u)))
                        for q in range(2):
                            hp = slice(64 * q, 64 * q + 64)
                            for jj in range(2):
                                mm(bank[3 + q][:, 256 * jj:256 * jj + 256], bh[hp, jj, :],
                                   ar[hp, jj, :], start=True, stop=True, skip_group_check=True)
                                i = mm(bank[5 + q][:, 256 * jj:256 * jj + 256], kh[hp, jj, :],
                                       ar[hp, jj, :], start=True, stop=True, skip_group_check=True)
                            i.then_inc(pe_done, did(PE, ("grams", u, q)))
                        for q in range(2):
                            hp = slice(64 * q, 64 * q + 64)
                            for jj in range(2):
                                i = mm(bank[q][:, P * jj:P * jj + P], ar[hp, jj, 0:P], bh[hp, jj, :],
                                       start=True, stop=True, skip_group_check=True)
                            i.then_inc(pe_done, did(PE, ("A", u, q)))

                        def four(name, b, lhs, rhs):
                            for m in range(4):
                                i = mm(bank[b][:, m * P:m * P + P], lhs[:, m, :], rhs[:, m, :],
                                       start=True, stop=True, skip_group_check=True)
                            i.then_inc(pe_done, did(PE, (name, u)))

                        pe.wait_ge(vec_done, at(VE, ("D0", u)))
                        four("E2", 7, D_[0], E_[0])
                        pe.wait_ge(act_done, at(AC, ("bkt", u)))
                        four("D2", 2, E_[0], D_[0])
                        pe.wait_ge(act_done, at(AC, ("E2", u)))
                        pe.wait_ge(vec_done, at(VE, ("T1", u)))
                        four("T2", 3, E_[1], T_[0])
                        four("TT2", 4, T_[0], E_[1])
                        pe.wait_ge(act_done, at(AC, ("D2", u)))
                        four("E4", 7, D_[1], E_[1])
                        four("D4", 2, E_[1], D_[1])
                        pe.wait_ge(act_done, at(AC, ("E4", u)))
                        pe.wait_ge(vec_done, at(VE, ("TT2", u)))
                        four("T4", 3, E_[0], T_[1])
                        four("TT4", 4, T_[1], E_[0])
                        pe.wait_ge(act_done, at(AC, ("D4", u)))
                        four("E8", 7, D_[0], E_[0])
                        pe.wait_ge(act_done, at(AC, ("E8", u)))
                        pe.wait_ge(vec_done, at(VE, ("TT4", u)))
                        four("T8", 3, E_[1], T_[0])
                        four("TT8", 4, T_[0], E_[1])
                        cur = 1
                        for lv in range(3):
                            pe.wait_ge(vec_done, at(VE, ("bm", u, lv)))
                            pe.wait_ge(vec_done, at(VE, ("TT8", u) if lv == 0 else ("TTm", u, lv - 1)))
                            four(("Z", lv), 7, bm, TT_[cur])
                            pe.wait_ge(act_done, at(AC, ("Z", u, lv)))
                            if lv < 2:
                                four(("Tm", lv), 3, zt, T_[cur])
                            four(("TTm", lv), 4, T_[cur], zt)
                            cur = 1 - cur
                        pe.wait_ge(vec_done, at(VE, ("sin", u)))
                        for jj in range(2):
                            mm(bank[0][:, P * jj:P * jj + P], ar[:, jj, 0:P], sin_[:, jj, :],
                               start=True, stop=False, skip_group_check=True)
                            for q in range(2):
                                h = 4 * pg + 2 * jj + q
                                i = mm(bank[0][:, P * jj + HD * q:P * jj + HD * q + HD],
                                       kb[:, 2 * q + jj, 0:P], vt[:, c, h * HD:h * HD + HD],
                                       start=False, stop=True, skip_group_check=True)
                        i.then_inc(pe_done, did(PE, ("x", u)))
                        pe.wait_ge(act_done, at(AC, ("xs", u)))
                        pe.wait_ge(vec_done, at(VE, ("TTm", u, 2)))
                        for jj in range(2):
                            for q in range(2):
                                i = mm(bank[1][:, P * jj + HD * q:P * jj + HD * q + HD],
                                       TT_[cur][:, 2 * q + jj, :], xs[:, jj, HD * q:HD * q + HD],
                                       start=True, stop=True, skip_group_check=True)
                        i.then_inc(pe_done, did(PE, ("u", u)))
                        pe.wait_ge(act_done, at(AC, ("us", u)))
                        for jj in range(2):
                            mm(bank[5][:, P * jj:P * jj + P], ar[:, jj, P:2 * P], sin_[:, jj, :],
                               start=True, stop=False, skip_group_check=True)
                            for q in range(2):
                                h = 4 * pg + 2 * jj + q
                                o = bank[5][:, P * jj + HD * q:P * jj + HD * q + HD]
                                mm(o, bb[:, 2 * q + jj, P:2 * P], us[:, jj, HD * q:HD * q + HD],
                                   start=False, stop=False, skip_group_check=True)
                                i = mm(o, kb[:, 2 * q + jj, P:2 * P], vt[:, c, h * HD:h * HD + HD],
                                       start=False, stop=True, skip_group_check=True)
                        i.then_inc(pe_done, did(PE, ("y", u)))
                        for jj in range(2):
                            j = 2 * pg + jj
                            mm(bank[6][:, P * jj:P * jj + P], bkt[:, jj, :], us[:, jj, :],
                               start=True, stop=False, skip_group_check=True)
                            i = mm(bank[6][:, P * jj:P * jj + P], bkt[:, 2 + jj, :],
                                   vt[:, c, j * P:j * P + P], start=False, stop=True,
                                   skip_group_check=True)
                        i.then_inc(pe_done, did(PE, ("s", u)))
                        u += 1
            pe.wait_ge(vec_done, at(VE, "yr norm"))
            for j in range(4):
                turned(("yr turned", j), lambda m: yt[:, m, j * P:j * P + P], 1 + j)
            pe.wait_ge(vec_done, at(VE, "o_rw"))
            product("mix out", first["mix_out"], 4, mix, slice(0, T), [6, 7],
                    lambda j: pe.wait_ge(vec_done, at(VE, ("mix res", j))))

            rms(1, slice(0, T))
            pe.wait_ge(act_done, at(AC, ("norm", 1, KT - 1, 1)))
            for j in range(FT):
                for i_, kind in enumerate(("ffn1", "ffn3")):
                    s = first[kind, j // 2]
                    ws = full(s)
                    if j >= 2 and i_ == 0:
                        pe.wait_ge(vec_done, at(VE, ("gu", j - 2)))
                    t = j % 2
                    for k in range(KT):
                        i = mm(bank[2 * t + i_], ws[:, k, t * P:t * P + P], aT[:, k, :],
                               start=(k == 0), stop=(k == KT - 1))
                    i.then_inc(pe_done, did(PE, (kind, "tile", j), *([("slot", s)] if t else [])))
            pe.wait_ge(vec_done, at(VE, ("gu", FT - 1)))
            for n in range(KT):
                s = first["ffn2"] + n
                ws = full(s)
                if n >= 4:
                    pe.wait_ge(vec_done, at(VE, ("ffn res", n - 4)))
                for k in range(FT):
                    i = mm(bank[4 + n % 4], ws[:, k, :], G[:, k, :], start=(k == 0), stop=(k == FT - 1))
                i.then_inc(pe_done, did(PE, ("ffn out", n), ("slot", s)))

            rms(2, slice(0, T))
            pe.wait_ge(act_done, at(AC, ("norm", 2, KT - 1, 1)))
            product("q1", first["qkv"], 4, aT, LAT, [1, 2],
                    lambda j: pe.wait_ge(act_done, at(AC, ("q1", j))))
            pe.wait_ge(act_done, at(AC, ("q1", 7)))
            product("k1", first["qkv"] + 4, 4, aT, slice(0, T), [1, 2],
                    lambda j: pe.wait_ge(act_done, at(AC, ("k1", j))))
            n = 0
            for half in range(4):
                s = first["qkv"] + 8 + half
                ws = full(s)
                for c in range(NCH):
                    if n >= 2:
                        pe.wait_ge(act_done, at(AC, ("v1", n - 2)))
                    for k in range(KT):
                        i = mm(bank[3 + n % 2][:, 0:256], aT[:, k, c * P:c * P + P], ws[:, k, :],
                               start=(k == 0), stop=(k == KT - 1))
                    i.then_inc(pe_done, did(PE, ("v1", n), *([("slot", s)] if c == 3 else [])))
                    n += 1
            pe.wait_ge(act_done, at(AC, ("v1", 15)))
            pe.wait_ge(act_done, at(AC, ("k1", 7)))
            for hd in range(16):
                hp, j = slice(64 * (hd % 2), 64 * (hd % 2) + 64), hd // 2
                for qt in range(2):
                    if hd:
                        pe.wait_ge(act_done, at(AC, ("exp1", hd - 1, qt)))
                    mm(bank[qt], q1[hp, j, qt * P:qt * P + P], k1[hp, j, :], start=True, stop=True
                       ).then_inc(pe_done, did(PE, ("s1", hd, qt)))
                for qt in range(2):
                    pe.wait_ge(vec_done, at(VE, ("p1", hd, qt)))
                    if hd:
                        pe.wait_ge(act_done, at(AC, ("pt1", hd - 1, qt)))
                    turned(("pt1", hd, qt), lambda m: pr[:, qt, m * P:m * P + P], 2 + qt)
                pe.wait_ge(act_done, at(AC, ("pt1", hd, 1)))
                if hd >= 2:
                    pe.wait_ge(vec_done, at(VE, ("o1", hd - 2)))
                for m in range(NCH):
                    i = mm(bank[4 + hd % 2][hp, 0:TL], v1[:, m, hd * HD:hd * HD + HD], pt[:, m, :],
                           start=(m == 0), stop=(m == NCH - 1))
                i.then_inc(pe_done, did(PE, ("o1", hd)))
            pe.wait_ge(vec_done, at(VE, ("o1", 15)))
            product("na out", first["na_out"], 4, o1, slice(0, TL), [6, 7],
                    lambda j: pe.wait_ge(vec_done, at(VE, ("na res", j))))

            rms(3, LAT)
            pe.wait_ge(act_done, at(AC, ("norm", 3, KT - 1, 1)))
            s = first["router"]
            ws = full(s)
            for c in range(2):
                for k in range(KT):
                    i = mm(bank[1][:, 8 * c:8 * c + 8], aT[:, k, TC + c * P:TC + c * P + P],
                           ws[:, k, :], start=(k == 0), stop=(k == KT - 1), skip_group_check=True)
            i.then_inc(pe_done, did(PE, "router", ("slot", s)))
            pe.wait_ge(vec_done, at(VE, "gates"))
            for e in range(NE):
                for c in range(2):
                    i = mm(bank[e // 2][:, 256 * (e % 2) + c * P:256 * (e % 2) + c * P + P],
                           gates[:, c, e:e + 1].broadcast_to([P, P]), ident, start=True, stop=True,
                           skip_group_check=True)
                i.then_inc(pe_done, did(PE, ("gate row", e)))
            pe.wait_ge(vec_done, at(VE, "zero"))
            for n in range(4):
                mm(bank[4 + n], um[0][:, 0:P], tmpA, start=True, stop=False, skip_group_check=True)
            pe.wait_ge(act_done, at(AC, ("gate row", NE - 1)))
            before = now(PE)
            vper, aper = at(VE, ("per", "moe")), at(AC, ("per", "moe"))
            with pe.Fori(0, NE) as e:
                for j in range(FT):
                    t = j % 2
                    for i_ in range(2):
                        i0 = 2 * (j // 2) + i_
                        pe.wait_ge(w_full[i0 % RING], e * 80 + filled(first["moe"] + i0))
                        ws = cut(ring_t, (i0 % RING) * SLOT, KT, 256)
                        if i_ == 0:
                            if j >= 2:
                                pe.wait_ge(vec_done, e * vper + at(VE, ("gu m", j - 2)))
                            else:
                                pe.wait_ge(vec_done, e * vper + (at(VE, ("gu m", FT - 2 + j)) - vper))
                        for k in range(KT):
                            i = mm(bank[2 * t + i_][:, 0:TL], ws[:, k, t * P:t * P + P],
                                   aT[:, k, LAT], start=(k == 0), stop=(k == KT - 1))
                        i.then_inc(pe_done, did(PE, ("moe tile", i_, j),
                                                *([("moe slot", i0)] if t else [])))
                pe.wait_ge(vec_done, e * vper + at(VE, ("gu m", FT - 1)))
                for n in range(KT):
                    i0 = 22 + n
                    pe.wait_ge(w_full[i0 % RING], e * 80 + filled(first["moe"] + i0))
                    ws = cut(ring_t, (i0 % RING) * SLOT, FT, P)
                    for k in range(FT):
                        i = mm(bank[4 + n // 2][:, 256 * (n % 2):256 * (n % 2) + 256], ws[:, k, :],
                               Gm[:, k, :], start=False, stop=(k == FT - 1), skip_group_check=True)
                    i.then_inc(pe_done, did(PE, ("moe slot", i0)))
            counts.loop(PE, "moe", before, NE)

            pe.wait_ge(vec_done, at(VE, "moe res"))
            rms(4, LAT)

            pe.wait_ge(ctx2_in, 16)
            pe.wait_ge(act_done, at(AC, ("norm", 4, KT - 1, 1)))
            ln(5, slice(0, T))
            pe.wait_ge(act_done, at(AC, ("norm", 5, KT - 1, 1)))
            product("in2", first["in2"], 8, aT, LAT, [2, 3],
                    lambda j: pe.wait_ge(act_done, at(AC, ("in2", j))))
            pe.wait_ge(act_done, at(AC, ("in2", 15)))
            product("k2", first["in2"] + 8, 2, aT, slice(0, T), [2, 3],
                    lambda j: pe.wait_ge(act_done, at(AC, ("k2", j))))
            n = 0
            for half in range(2):
                s = first["in2"] + 10 + half
                ws = full(s)
                for c in range(NCH):
                    if n >= 2:
                        pe.wait_ge(act_done, at(AC, ("v2", n - 2)))
                    for k in range(KT):
                        i = mm(bank[4 + n % 2][:, 0:256], aT[:, k, c * P:c * P + P], ws[:, k, :],
                               start=(k == 0), stop=(k == KT - 1))
                    i.then_inc(pe_done, did(PE, ("v2", n), *([("slot", s)] if c == 3 else [])))
                    n += 1
            pe.wait_ge(act_done, at(AC, ("k2", 3)))
            for n in range(8):
                src = q2[:, n, :] if n < 4 else k2[:, n - 4, LAT]
                if n >= 2:
                    pe.wait_ge(vec_done, at(VE, ("rope", n - 2)))
                mm(bank[6 + n % 2][:, 0:TL], const("turn"), src, start=True, stop=True
                   ).then_inc(pe_done, did(PE, ("turn", n)))
            pe.wait_ge(vec_done, at(VE, ("rope", 7)))
            pe.wait_ge(act_done, at(AC, ("v2", 7)))
            for hd in range(4):
                for qt in range(2):
                    for cp in range(2):
                        hp = slice(64 * cp, 64 * cp + 64)
                        if hd or qt:
                            pe.wait_ge(act_done, at(AC, ("exp2", *((hd, 0) if qt else (hd - 1, 1)), cp)))
                        mm(bank[cp], q2[hp, hd, qt * P:qt * P + P], k2[hp, hd, :], start=True, stop=True
                           ).then_inc(pe_done, did(PE, ("s2", hd, qt, cp)))
                    pe.wait_ge(vec_done, at(VE, ("p2", hd, qt)))
                    if hd:
                        pe.wait_ge(act_done, at(AC, ("pt2", hd - 1, qt)))
                    turned(("pt2", hd, qt), lambda m: pd[:, qt, m * P:m * P + P], 2 + qt)
                pe.wait_ge(act_done, at(AC, ("pt2", hd, 1)))
                if hd >= 2:
                    pe.wait_ge(act_done, at(AC, ("o2", hd - 2)))
                for m in range(NCH):
                    i = mm(bank[4 + hd % 2][:, 0:TL], v2[:, m, hd * P:hd * P + P], pt2[:, m, :],
                           start=(m == 0), stop=(m == NCH - 1))
                i.then_inc(pe_done, did(PE, ("o2", hd)))
            for hd in range(4):
                pe.wait_ge(act_done, at(AC, ("o2 sq", hd)))
                i = mm(bank[6 + hd // 2][:, 256 * (hd % 2):256 * (hd % 2) + 256], const("ones"),
                       mix[:, 4 + hd, CTX], start=True, stop=True, skip_group_check=True)
            i.then_inc(pe_done, did(PE, "subln"))
            pe.wait_ge(vec_done, at(VE, "o_attn"))
            pe.wait_ge(vec_done, at(VE, "o_conv"))

            def outwards(name, s0, st, rhs):
                product(name, s0, 4, rhs, LAT, [2, 3],
                        lambda j: pe.wait_ge(vec_done, at(VE, (name, j))))
                pe.wait_ge(vec_done, at(VE, (name, KT - 1)))
                ln(st, LAT)
                pe.wait_ge(act_done, at(AC, ("norm", st, KT - 1, 1)))

            def mlp(i, st):
                ln(st, LAT)
                pe.wait_ge(act_done, at(AC, ("norm", st, KT - 1, 1)))
                product(("mlp1", i), first["mlp1", i], 16, aT, LAT, [2, 3],
                        lambda j: pe.wait_ge(vec_done, at(VE, ("relu2", i, j))))
                pe.wait_ge(vec_done, at(VE, ("relu2", i, F2T - 1)))
                for n in range(KT):
                    if n >= 2:
                        pe.wait_ge(vec_done, at(VE, (("mlp", i), n - 2)))
                    for half in range(2):
                        s = first["mlp2", i, n, half]
                        ws = full(s)
                        for k in range(16):
                            j = mm(bank[4 + n % 2][:, 0:TL], ws[:, k, :], G2[:, 16 * half + k, :],
                                   start=(half + k == 0), stop=(half * k == 15))
                        j.then_inc(pe_done, did(PE, ("slot", s), *([(("mlp", i), n)] if half else [])))
                pe.wait_ge(vec_done, at(VE, (("mlp", i), KT - 1)))
                ln(st + 1, LAT)
                pe.wait_ge(act_done, at(AC, ("norm", st + 1, KT - 1, 1)))

            outwards("out2", first["out2"], 6, mix)
            mlp(0, 7)

            ln(9, LAT)
            pe.wait_ge(act_done, at(AC, ("norm", 9, KT - 1, 1)))
            n = 0
            for c in range(2):
                for g in range(0, KT, 2):
                    if n >= 2:
                        pe.wait_ge(act_done, at(AC, ("fab", n - 2)))
                    for m in range(2):
                        i = mm(bank[2 + n % 2][:, 256 * m:256 * m + 256],
                               aT[:, g + m, TC + c * P:TC + c * P + P], const("cs128", 256),
                               start=True, stop=True, skip_group_check=True)
                    i.then_inc(pe_done, did(PE, ("fab", n)))
                    n += 1
            pe.wait_ge(act_done, at(AC, ("fab", 7)))
            dft = (cut(const("dft_c", 512), 0, 2, TL), cut(const("dft_s", 512), 0, 2, TL))
            for g in range(KT):
                if g >= 2:
                    pe.wait_ge(act_done, at(AC, ("fm", g - 2)))
                for c in range(2):
                    for part in range(2):
                        i = mm(bank[4 + g % 2][:, 0:TL], fab[:, c, g, part * P:part * P + P],
                               dft[part][:, c, :], start=(c + part == 0), stop=(c + part == 2))
                i.then_inc(pe_done, did(PE, ("fm", g)))
            pe.wait_ge(act_done, at(AC, ("fm", KT - 1)))
            outwards("fourier", first["fourier"], 10, mix)
            mlp(1, 11)

        MODULATED = {0: (0, 0, 0), 1: (0, 0, 3), 2: (0, 1, 0), 3: (0, 1, 3),
                     5: (1, 0, 0), 7: (1, 0, 3), 9: (1, 1, 0), 11: (1, 1, 3)}
        GS = {st: i for i, st in enumerate(MODULATED)}
        AFFINE = {6: 0, 8: 8, 10: 16, 12: 24}

        @block.scalar
        def _(ac):
            act = nc.scalar.activation

            def norm(st, sl, centred):
                n = sl.stop - sl.start
                if centred:
                    ac.wait_ge(vec_done, at(VE, ("centre", st)))
                src = aT if centred else hT
                act(mix[:, :, sl], src[:, :, sl], ACT.Square).then_inc(act_done, did(AC, ("square", st)))
                ac.wait_ge(vec_done, at(VE, ("var", st)))
                act(tmpB[:, 0:n], tmpA[:, 0:n], ACT.Sqrt).then_inc(act_done, did(AC, ("sqrt", st)))
                for k in range(KT):
                    ac.wait_ge(vec_done, at(VE, ("norm", st, k)))
                    for s in range(2):
                        if s == 0 and sl == LAT:
                            continue
                        dst, bias = aT, 0.0
                        if st in MODULATED:
                            scale, bias = gs[:, GS[st], k, s:s + 1], mod(*MODULATED[st], k, s)
                        elif st in AFFINE:
                            dst = hT
                            scale = col("ln_g_2", AFFINE[st] + k)
                            bias = col("ln_b_2", AFFINE[st] + k)
                        else:
                            dst, scale = hT, col("norm_final", k)
                        act(dst[:, k, SEQS[s]], aT[:, k, SEQS[s]], ACT.Identity, bias=bias,
                            scale=scale).then_inc(act_done, did(AC, ("norm", st, k, s)))

            def copy(name, dst, src, scale=1.0):
                act(dst, src, ACT.Copy, scale=scale).then_inc(act_done, did(AC, name))

            ac.wait_ge(loaded, 5 * 16)
            for i, name in enumerate(("c_ctx", "c", "c_ctx_2", "c_2")):
                act(csil[:, i // 2, :, i % 2], col(name, 0, 8), ACT.Silu
                    ).then_inc(act_done, did(AC, ("cond", i)))

            norm(0, slice(0, T), False)
            ac.wait_ge(pe_done, at(PE, ("zg", 1)))
            for c in range(NCH):
                act(zg[:, c, :], bank[2 + c], ACT.Silu).then_inc(act_done, did(AC, ("zg", c)))
            ac.wait_ge(vec_done, at(VE, "xpad edges"))
            for j in range(8):
                ac.wait_ge(pe_done, at(PE, ("xbc", j)))
                copy(("xbc", j), xpad[:, j, :, 2:TC + 2],
                     bank[j % 2].rearrange("p (s t) -> p s t", s=2))
            for j in range(8):
                ac.wait_ge(vec_done, at(VE, ("conv", j)))
                act(xb[:, j, :], xb[:, j, :], ACT.Silu).then_inc(act_done, did(AC, ("xb", j)))
            ac.wait_ge(vec_done, at(VE, "dt_raw"))
            flat = small[:, 320:384]
            act(flat, small[:, 0:64], ACT.Abs).then_inc(act_done, did(AC, "abs"))
            ac.wait_ge(act_done, now(AC))
            act(flat, flat, ACT.Exp, scale=-1.0).then_inc(act_done, did(AC, "exp abs"))
            ac.wait_ge(act_done, now(AC))
            act(flat, flat, ACT.Ln, bias=1.0).then_inc(act_done, did(AC, "ln"))
            act(a_neg, row("mb_a_log", 16), ACT.Exp).then_inc(act_done, did(AC, "a_neg"))
            ac.wait_ge(vec_done, at(VE, "cs"))
            act(small[:, 256:320], small[:, 192:256], ACT.Exp).then_inc(act_done, did(AC, "ecs"))
            for u in range(8):
                ac.wait_ge(vec_done, at(VE, ("dec", u)))
                act(mt_t, dec_t, ACT.Exp).then_inc(act_done, did(AC, ("exp dec", u)))
                ac.wait_ge(vec_done, at(VE, ("dcs", u)))
                act(small[:, 400:416], small[:, 400:416], ACT.Exp
                    ).then_inc(act_done, did(AC, ("exp tot", u)))
            ac.wait_ge(vec_done, at(VE, "ss_m"))
            act(small[:, 424:432], small[:, 416:424], ACT.Sqrt).then_inc(act_done, did(AC, "rs_m"))
            for j in range(4):
                ac.wait_ge(pe_done, at(PE, ("ym turned", j)))
                act(mix[:, 4 + j, :], bank[2 + j], ACT.Copy, scale=col("mb_norm_w", j)
                    ).then_inc(act_done, did(AC, ("norm ym", j)))

            ac.wait_ge(vec_done, at(VE, "zpad edges"))
            for j in range(14):
                ac.wait_ge(pe_done, at(PE, ("rkv", j)))
                if j >= 4:
                    ac.wait_ge(vec_done, at(VE, ("shift", j - 4)))
                m = 96 if j == 13 else P
                copy(("rkv", j), zpad[j % 4][0:m, :, 1:TC + 1],
                     bank[j % 2][0:m, :].rearrange("p (s t) -> p s t", s=2))
            for c in range(NCH):
                ac.wait_ge(pe_done, at(PE, ("vt", c)))
                copy(("vt", c), vt[:, c, :], bank[4 + c])
            ac.wait_ge(vec_done, at(VE, ("shift", 12)))
            act(llw[0:64, :], llw[0:64, :], ACT.Tanh).then_inc(act_done, did(AC, "tanh"))
            ac.wait_ge(vec_done, at(VE, ("shift", 13)))
            act(llg[0:96, :], llg[0:96, :], ACT.Sigmoid).then_inc(act_done, did(AC, "lg"))
            for d in range(2):
                for c in range(NCH):
                    ac.wait_ge(vec_done, at(VE, ("w0", d, c)))
                    act(sig[d][:, c, :], sig[d][:, c, :], ACT.Sigmoid
                        ).then_inc(act_done, did(AC, ("sig", d, c)))
            for d in range(2):
                for j in range(4):
                    ac.wait_ge(pe_done, at(PE, ("ic", d, j)))
                    act(ic[d][:, j, :], bank[2 + j % 2], ACT.Sigmoid, bias=col("rw_a0", 4 * d + j)
                        ).then_inc(act_done, did(AC, ("ic", d, j)))
            for j in range(4):
                ac.wait_ge(pe_done, at(PE, ("gate", j)))
                copy(("gate", j), gate[:, j, :], bank[j % 2])
            for j in range(4):
                ac.wait_ge(vec_done, at(VE, ("kk var", j)))
                act(tmpB, tmpA, ACT.Sqrt).then_inc(act_done, did(AC, ("kk root", j)))
            u = 0
            for d in range(2):
                for step in range(NCH):
                    for pg in range(2):
                        for jj in range(2):
                            ac.wait_ge(pe_done, at(PE, ("decays", u, jj)))
                            act(ex[:, jj, :], bank[jj][:, 0:258], ACT.Exp
                                ).then_inc(act_done, did(AC, ("ex", u, jj)))
                            act(ei[:, jj, :], bank[jj][:, 0:P], ACT.Exp, scale=-1.0
                                ).then_inc(act_done, did(AC, ("ei", u, jj)))
                        for name, b, dst in (("bkt", 2, bkt), ("E2", 7, E_[1]), ("D2", 2, D_[1]),
                                             ("E4", 7, E_[0]), ("D4", 2, D_[0]), ("E8", 7, E_[1])):
                            ac.wait_ge(pe_done, at(PE, (name, u)))
                            copy((name, u), dst, bank[b].rearrange("p (a b) -> p a b", a=4))
                        for lv in range(3):
                            ac.wait_ge(pe_done, at(PE, (("Z", lv), u)))
                            copy(("Z", u, lv), zt, bank[7].rearrange("p (a b) -> p a b", a=4))
                        ac.wait_ge(pe_done, at(PE, ("x", u)))
                        copy(("xs", u), xs, bank[0][:, 0:256].rearrange("p (a b) -> p a b", a=2))
                        ac.wait_ge(pe_done, at(PE, ("u", u)))
                        copy(("us", u), us, bank[1][:, 0:256].rearrange("p (a b) -> p a b", a=2))
                        u += 1
            ac.wait_ge(vec_done, at(VE, "yr var"))
            act(small[:, 96:128], small[:, 64:96], ACT.Sqrt).then_inc(act_done, did(AC, "yr root"))
            for j in range(4):
                ac.wait_ge(pe_done, at(PE, ("yr turned", j)))
                act(mix[:, j, :], bank[1 + j], ACT.Identity, scale=col("rw_gn_w", j),
                    bias=col("rw_gn_b", j)).then_inc(act_done, did(AC, ("gn", j)))

            ac.wait_ge(vec_done, at(VE, ("mix res", KT - 1)))
            norm(1, slice(0, T), False)
            for j in range(FT):
                ac.wait_ge(pe_done, at(PE, ("ffn1", "tile", j)))
                if j >= 2:
                    ac.wait_ge(vec_done, at(VE, ("gu", j - 2)))
                act(sg[j % 2], bank[2 * (j % 2)], ACT.Silu).then_inc(act_done, did(AC, ("sg", j)))

            ac.wait_ge(vec_done, at(VE, ("ffn res", KT - 1)))
            norm(2, slice(0, T), False)
            for j in range(KT):
                ac.wait_ge(pe_done, at(PE, ("q1", j)))
                copy(("q1", j), q1[:, j, :], bank[1 + j % 2][:, 0:TL], HD ** -0.5)
            for j in range(KT):
                ac.wait_ge(pe_done, at(PE, ("k1", j)))
                copy(("k1", j), k1[:, j, :], bank[1 + j % 2])
            for n in range(16):
                ac.wait_ge(pe_done, at(PE, ("v1", n)))
                copy(("v1", n), v1[:, n % 4, 256 * (n // 4):256 * (n // 4) + 256],
                     bank[3 + n % 2][:, 0:256])
            for hd in range(16):
                for qt in range(2):
                    ac.wait_ge(vec_done, at(VE, ("m1", hd, qt)))
                    act(pr[:, qt, :], pr[:, qt, :], ACT.Exp, bias=stat[:, qt:qt + 1],
                        accum_out=stat[:, 2 + qt:3 + qt]).then_inc(act_done, did(AC, ("exp1", hd, qt)))
                for qt in range(2):
                    ac.wait_ge(pe_done, at(PE, ("pt1", hd, qt)))
                    if hd:
                        ac.wait_ge(pe_done, at(PE, ("o1", hd - 1)))
                    copy(("pt1", hd, qt), pt[:, :, qt * P:qt * P + P],
                         bank[2 + qt].rearrange("p (a b) -> p a b", a=4))

            ac.wait_ge(vec_done, at(VE, ("na res", KT - 1)))
            norm(3, LAT, False)
            ac.wait_ge(vec_done, at(VE, "lg max"))
            act(small[:, 32:48], small[:, 32:48], ACT.Exp).then_inc(act_done, did(AC, "ge"))
            for e in range(NE):
                ac.wait_ge(pe_done, at(PE, ("gate row", e | 1)))
                copy(("gate row", e), gbc[:, e, :], bank[e // 2][:, 256 * (e % 2):256 * (e % 2) + 256])
            before = now(AC)
            pper, vper = at(PE, ("per", "moe")), at(VE, ("per", "moe"))
            with ac.Fori(0, NE) as e:
                for j in range(FT):
                    ac.wait_ge(pe_done, e * pper + at(PE, ("moe tile", 0, j)))
                    if j >= 2:
                        ac.wait_ge(vec_done, e * vper + at(VE, ("gu m", j - 2)))
                    else:
                        ac.wait_ge(vec_done, e * vper + (at(VE, ("gu m", FT - 2 + j)) - vper))
                    act(sgm[j % 2], bank[2 * (j % 2)][:, 0:TL], ACT.Silu
                        ).then_inc(act_done, did(AC, ("sg m", j)))
            counts.loop(AC, "moe", before, NE)
            ac.wait_ge(vec_done, at(VE, "moe res"))
            norm(4, LAT, False)

            norm(5, slice(0, T), True)
            for j in range(16):
                ac.wait_ge(pe_done, at(PE, ("in2", j)))
                src = bank[2 + j % 2][:, 0:TL]
                if j < 8:
                    copy(("in2", j), (gb if j < 4 else gc)[:, j % 4, :], src)
                elif j < 12:
                    copy(("in2", j), vp[:, j - 8, 1:TL + 1], src)
                else:
                    copy(("in2", j), q2[:, j - 12, :], src, HD ** -0.5)
            for j in range(4):
                ac.wait_ge(pe_done, at(PE, ("k2", j)))
                copy(("k2", j), k2[:, j, :], bank[2 + j % 2])
            for n in range(8):
                ac.wait_ge(pe_done, at(PE, ("v2", n)))
                copy(("v2", n), v2[:, n % 4, 256 * (n // 4):256 * (n // 4) + 256],
                     bank[4 + n % 2][:, 0:256])
            ac.wait_ge(vec_done, at(VE, "lam sums"))
            act(lamv[:, 2:4], lamv[:, 0:2], ACT.Exp).then_inc(act_done, did(AC, "lam"))
            for hd in range(4):
                for qt in range(2):
                    for cp in range(2):
                        ac.wait_ge(vec_done, at(VE, ("m2", hd, qt, cp)))
                        act(p2[:, cp, :], bank[cp], ACT.Exp, bias=small[:, 150 + cp:151 + cp],
                            accum_out=small[:, 152 + cp:153 + cp]
                            ).then_inc(act_done, did(AC, ("exp2", hd, qt, cp)))
                for qt in range(2):
                    ac.wait_ge(pe_done, at(PE, ("pt2", hd, qt)))
                    if hd:
                        ac.wait_ge(pe_done, at(PE, ("o2", hd - 1)))
                    copy(("pt2", hd, qt), pt2[:, :, qt * P:qt * P + P],
                         bank[2 + qt].rearrange("p (a b) -> p a b", a=4))
                ac.wait_ge(pe_done, at(PE, ("o2", hd)))
                copy(("o2", hd), o2[:, hd, :], bank[4 + hd % 2][:, 0:TL])
                act(mix[:, 4 + hd, CTX], bank[4 + hd % 2][:, 0:TL], ACT.Square
                    ).then_inc(act_done, did(AC, ("o2 sq", hd)))
            for i, t in enumerate((tmpA, tmpB)):
                ac.wait_ge(vec_done, at(VE, ("subln", i)))
                act(t, t, ACT.Sqrt).then_inc(act_done, did(AC, ("subln", i)))

            norm(6, LAT, True)
            norm(7, LAT, True)
            norm(8, LAT, True)
            norm(9, LAT, True)
            for n in range(8):
                ac.wait_ge(pe_done, at(PE, ("fab", n)))
                copy(("fab", n), fab[:, n // 4, 2 * (n % 4):2 * (n % 4) + 2, :],
                     bank[2 + n % 2].rearrange("p (a b) -> p a b", a=2))
            for g in range(KT):
                ac.wait_ge(pe_done, at(PE, ("fm", g)))
                copy(("fm", g), mix[:, g, LAT], bank[4 + g % 2][:, 0:TL])
            norm(10, LAT, True)
            norm(11, LAT, True)
            norm(12, LAT, True)

        @block.vector
        def _(ve):
            V = nc.vector

            def wide(ap, *shape):
                return ap.broadcast_to([P, *shape])

            def norm(st, sl, centred):
                n = sl.stop - sl.start
                eps = LN_EPS if centred else RMS_EPS
                if centred:
                    ve.wait_ge(pe_done, at(PE, ("norm mean", st)))
                    V.tensor_tensor(aT[:, :, sl], hT[:, :, sl], wide(bank[1][:, None, 0:n], KT, n),
                                    ALU.subtract).then_inc(vec_done, did(VE, ("centre", st)))
                ve.wait_ge(pe_done, at(PE, ("norm sum", st)))
                V.tensor_scalar(tmpA[:, 0:n], bank[0][:, 0:n], eps, None, ALU.add
                                ).then_inc(vec_done, did(VE, ("var", st)))
                ve.wait_ge(act_done, at(AC, ("sqrt", st)))
                V.reciprocal(tmpA[:, 0:n], tmpB[:, 0:n]).then_inc(vec_done, did(VE, ("rstd", st)))
                ve.wait_ge(vec_done, now(VE))
                src = aT if centred else hT
                for k in range(KT):
                    V.tensor_tensor(aT[:, k, sl], src[:, k, sl], tmpA[:, 0:n], ALU.mult
                                    ).then_inc(vec_done, did(VE, ("norm", st, k)))

            def op(name, ins):
                ins.then_inc(vec_done, did(VE, name))
                ve.wait_ge(vec_done, now(VE))

            def residual(name, j, src, gate, seqs):
                for s in seqs:
                    part = src[:, SEQS[s]] if len(seqs) == 2 else src
                    V.scalar_tensor_tensor(hT[:, j, SEQS[s]], part, mod(*gate, j, s), hT[:, j, SEQS[s]],
                                           ALU.mult, ALU.add
                                           ).then_inc(vec_done, did(VE, (name, j) if s else (name, j, "ctx")))

            V.memset(xpad, 0.0).then_inc(vec_done, did(VE, "xpad edges"))
            ve.wait_ge(loaded, 5 * 16)
            for b, name in enumerate(("b_ada", "ada_b_2")):
                ve.wait_ge(pe_done, at(PE, ("end", "ada")))
                V.tensor_tensor(mods[:, 96 * b:96 * b + 96, :],
                                cut(bank[7], 192 * b, 96, 2),
                                wide(col(name, 0, 96)[:, :, None], 96, 2), ALU.add
                                ).then_inc(vec_done, did(VE, ("mods", b)))
            ve.wait_ge(vec_done, now(VE))
            for st, (b, layer, piece) in MODULATED.items():
                at0 = 96 * b + 48 * layer + 8 * (piece + 1)
                g = GS[st]
                if b:
                    V.tensor_scalar(gs[:, g, :, :], mods[:, at0:at0 + 8, :], 1.0, None, ALU.add
                                    ).then_inc(vec_done, did(VE, ("gs", g)))
                else:
                    w_ = col("norm_ffn" if piece else "norm_mix", 8 * layer, 8)
                    V.scalar_tensor_tensor(gs[:, g, :, :], mods[:, at0:at0 + 8, :], 1.0,
                                           wide(w_[:, :, None], 8, 2), ALU.add, ALU.mult
                                           ).then_inc(vec_done, did(VE, ("gs", g)))

            norm(0, slice(0, T), False)
            ve.wait_ge(pe_done, at(PE, "dt"))
            V.tensor_tensor(dt_raw.rearrange("p c d h -> p c (d h)"), cut(bank[6], 0, NCH, 16),
                            wide(row("mb_dt_bias", 16)[:, None, :], NCH, 16), ALU.add
                            ).then_inc(vec_done, did(VE, "dt_raw"))
            for j in range(8):
                ve.wait_ge(act_done, at(AC, ("xbc", j)))
                dst = xb[:, j, :].rearrange("p (s t) -> p s t", s=2)
                op(("conv 0", j), V.tensor_scalar(dst, xpad[:, j, :, 0:TC], col("mb_conv_w", j),
                                                  col("mb_conv_b", j), ALU.mult, ALU.add))
                for tap in range(1, 5):
                    name = ("conv", j) if tap == 4 else ("conv part", j, tap)
                    op(name, V.scalar_tensor_tensor(dst, xpad[:, j, :, tap:tap + TC],
                                                    col("mb_conv_w", 8 * tap + j), dst,
                                                    ALU.mult, ALU.add))
            ve.wait_ge(act_done, at(AC, "a_neg"))
            op("dtv", V.scalar_tensor_tensor(small[:, 64:128], small[:, 0:64], 0.0, small[:, 320:384],
                                             ALU.max, ALU.add))
            op("a_tok", V.scalar_tensor_tensor(
                a_tok.rearrange("p c d h -> p c (d h)"), dtv.rearrange("p c d h -> p c (d h)"), -1.0,
                wide(a_neg[:, None, :], NCH, 16), ALU.mult, ALU.mult))
            for c in range(NCH):
                ve.wait_ge(pe_done, at(PE, ("xt", c)))
                V.tensor_copy(xt[:, c, :], bank[2 + c % 2]).then_inc(vec_done, did(VE, ("xt", c)))
                ve.wait_ge(pe_done, at(PE, ("bt", c)))
                V.tensor_copy(bt[:, c, :], bank[4 + c % 2][:, 0:256]).then_inc(vec_done, did(VE, ("bt", c)))
            ve.wait_ge(pe_done, at(PE, "cs"))
            V.tensor_copy(small[:, 192:256], bank[6][:, 0:64]).then_inc(vec_done, did(VE, "cs"))
            ve.wait_ge(pe_done, at(PE, "gram"))
            for d in range(2):
                for g in range(2):
                    mask = const("upper_in" if d == 0 else "lower_in")
                    V.tensor_tensor(gram[:, d, g, :, :], cut(bank[g], 0, NCH, P),
                                    wide(mask[:, None, :], NCH, P), ALU.mult
                                    ).then_inc(vec_done, did(VE, ("gram", d) if g else ("gram 0", d)))
            ve.wait_ge(vec_done, now(VE))
            u = 0
            for d in range(2):
                for c in range(NCH):
                    V.tensor_tensor(cut(xdt[:, c, :], 0, 8, HD), cut(xt[:, c, :], 0, 8, HD),
                                    wide(dtv[:, c, d, :][:, :, None], 8, HD), ALU.mult
                                    ).then_inc(vec_done, did(VE, ("xdt", d, c)))
                for step in range(NCH):
                    c = step if d == 0 else step ^ 1
                    last = P - 1 if d == 0 else 0
                    ve.wait_ge(pe_done, at(PE, ("decay", u)))
                    ve.wait_ge(vec_done, now(VE))
                    for h in range(8):
                        V.tensor_scalar(dec[:, h, :], bank[h // 4][:, (h % 4) * P:(h % 4) * P + P],
                                        cs[:, c, d, h:h + 1], 0.0, ALU.subtract, ALU.min
                                        ).then_inc(vec_done, did(VE, ("dec", u) if h == 7 else ("dec", u, h)))
                    for half in range(2):
                        tot = cut(bank[half], 0, 4, P)[:, :, last]
                        V.tensor_tensor(dcs[:, 4 * half:4 * half + 4], tot,
                                        cs[:, c, d, 4 * half:4 * half + 4], ALU.subtract
                                        ).then_inc(vec_done, did(VE, ("dcs part", u, half)))
                        V.tensor_copy(etot[:, 4 * half:4 * half + 4], tot
                                      ).then_inc(vec_done, did(VE, ("dcs", u) if half else ("etot", u)))
                    ve.wait_ge(act_done, at(AC, ("exp dec", u)))
                    for g in range(2):
                        V.tensor_tensor(mt[:, 4 * g:4 * g + 4, :], mt[:, 4 * g:4 * g + 4, :],
                                        wide(gram[:, d, g, c, :][:, None, :], 4, P), ALU.mult
                                        ).then_inc(vec_done, did(VE, ("mt", u) if g else ("mt 0", u)))
                    ve.wait_ge(act_done, at(AC, ("exp tot", u)))
                    V.tensor_tensor(cut(xd2, 0, 8, HD), cut(xdt[:, c, :], 0, 8, HD),
                                    wide(dcs[:, :, None], 8, HD), ALU.mult
                                    ).then_inc(vec_done, did(VE, ("xd2", u)))
                    ve.wait_ge(pe_done, at(PE, ("y diag", u)))
                    if d == 0:
                        op(("y", u), V.tensor_copy(ym[:, c, :], bank[2]))
                    else:
                        op(("y", u), V.tensor_tensor(ym[:, c, :], ym[:, c, :], bank[2], ALU.add))
                    if step:
                        if step == 1 and d == 0:
                            ve.wait_ge(act_done, at(AC, "ecs"))
                        op(("off", u), V.tensor_tensor(
                            cut(dec_t, 0, 8, HD), cut(bank[3], 0, 8, HD),
                            wide(ecs[:, c, d, :][:, :, None], 8, HD), ALU.mult))
                        op(("y2", u), V.tensor_tensor(ym[:, c, :], ym[:, c, :], dec_t[:, 0:512], ALU.add))
                        op(("st", u), V.tensor_tensor(cut(st_m, 0, 8, HD), cut(st_m, 0, 8, HD),
                                                      wide(etot[:, :, None], 8, HD), ALU.mult))
                        ve.wait_ge(pe_done, at(PE, ("states", u)))
                        op(("unit", u), V.tensor_tensor(st_m, st_m, bank[4], ALU.add))
                    else:
                        ve.wait_ge(pe_done, at(PE, ("states", u)))
                        op(("unit", u), V.tensor_copy(st_m, bank[4]))
                    u += 1
            tmp = cut(mix_t, 0, NCH, RW)
            for c in range(NCH):
                op(("dx", c), V.tensor_tensor(cut(tmp[:, c, :], 0, 8, HD), cut(xt[:, c, :], 0, 8, HD),
                                              wide(row("mb_d", 8)[:, :, None], 8, HD), ALU.mult))
            op("ym 1", V.tensor_tensor(ym, ym, tmp, ALU.add))
            op("ym 2", V.tensor_tensor(ym, ym, zg, ALU.mult))
            op("ym sq", V.tensor_tensor(tmp, ym, ym, ALU.mult))
            op("ym ss", V.tensor_reduce(small[:, 416:424], cut(mix_t, 0, 8, 256), AX.X, ALU.add))
            op("ss_m", V.tensor_scalar(small[:, 416:424], small[:, 416:424], 1.0 / 256, RMS_EPS,
                                       ALU.mult, ALU.add))
            ve.wait_ge(act_done, at(AC, "rs_m"))
            op("rs_m", V.reciprocal(small[:, 416:424], small[:, 424:432]))
            flat = ym.rearrange("p c (g n) -> p (c g) n", g=2)
            V.tensor_tensor(flat, flat, wide(small[:, 416:424][:, :, None], 8, 256), ALU.mult
                            ).then_inc(vec_done, did(VE, "ym end"))

            ve.wait_ge(pe_done, at(PE, ("ym turned", 3)))
            for i in range(4):
                V.memset(zpad[i], 0.0).then_inc(vec_done, did(VE, "zpad edges" if i == 3 else ("zpad", i)))
            op("mu sum", V.tensor_tensor(mu0, col("mu_prev", 0, 13), col("mu_next", 0, 13), ALU.add))
            op("mu0", V.tensor_scalar(mu0, mu0, -1.0, 1.0, ALU.mult, ALU.add))
            op("1 - k_a", V.tensor_scalar(small[:, 16:20], col("rw_k_a", 0, 4), -1.0, 1.0, ALU.mult, ALU.add))
            for j in range(14):
                m = 96 if j == 13 else P
                ve.wait_ge(act_done, at(AC, ("rkv", j)))
                if j == 13:
                    ve.wait_ge(up_in, 5 * 16)
                    op("mug sum", V.tensor_tensor(mu0g[0:96, :], mug[0:96, 0:1], mug[0:96, 1:2], ALU.add))
                    op("mu0g", V.tensor_scalar(mu0g[0:96, :], mu0g[0:96, :], -1.0, 1.0, ALU.mult, ALU.add))
                    dst, own, prev, next_ = llg[0:96, :], mu0g, mug[:, 0:1], mug[:, 1:2]
                else:
                    dst = llw if j == 12 else (r_, k_, v_)[j // 4][:, j % 4, :]
                    own, prev, next_ = mu0[:, j:j + 1], col("mu_prev", j), col("mu_next", j)
                dst = dst.rearrange("p (s t) -> p s t", s=2)
                z = zpad[j % 4][0:m, :, :]
                op(("shift 0", j), V.tensor_scalar(dst, z[:, :, 1:TC + 1], own[0:m, :], None, ALU.mult))
                op(("shift 1", j), V.scalar_tensor_tensor(dst, z[:, :, 0:TC], prev[0:m, :], dst,
                                                          ALU.mult, ALU.add))
                op(("shift", j), V.scalar_tensor_tensor(dst, z[:, :, 2:TC + 2], next_[0:m, :], dst,
                                                        ALU.mult, ALU.add))
            for d in range(2):
                for c in range(NCH):
                    ve.wait_ge(pe_done, at(PE, ("w", d, c)))
                    V.tensor_tensor(sig[d][:, c, :], bank[c % 2], w0row[:, RW * d:RW * d + RW], ALU.add
                                    ).then_inc(vec_done, did(VE, ("w0", d, c)))
            for j in range(4):
                op(("kk 0", j), V.tensor_scalar(kk[:, j, :], k_[:, j, :], col("rw_k_k", j), None, ALU.mult))
                op(("kk sq", j), V.tensor_tensor(kdka[:, j, :], kk[:, j, :], kk[:, j, :], ALU.mult))
            for j in range(4):
                ve.wait_ge(pe_done, at(PE, ("kk", j)))
                op(("kk var", j), V.tensor_scalar(tmpA, bank[4 + j], 1e-24, None, ALU.max))
                ve.wait_ge(act_done, at(AC, ("kk root", j)))
                op(("kk rstd", j), V.reciprocal(tmpA, tmpB))
                op(("kk", j), V.tensor_tensor(kk[:, j, :], kk[:, j, :], tmpA, ALU.mult))
            for d in range(2):
                for j in range(4):
                    ve.wait_ge(act_done, at(AC, ("ic", d, j)))
                    op(("kd 0", d, j), V.tensor_scalar(kd[d][:, j, :], ic[d][:, j, :], col("rw_k_a", j),
                                                       small[:, 16 + j:17 + j], ALU.mult, ALU.add))
                    op(("kd", d, j), V.tensor_tensor(kd[d][:, j, :], kd[d][:, j, :], k_[:, j, :], ALU.mult))
                    op(("b", d, j), V.tensor_tensor(ic[d][:, j, :], ic[d][:, j, :], kk[:, j, :], ALU.mult))
            for j in range(4):
                op(("rk 0", j), V.tensor_scalar(kdka[:, j, :], kd[0][:, j, :], col("rw_r_k", j), None, ALU.mult))
                op(("rk 1", j), V.scalar_tensor_tensor(kdka[:, j, :], kd[1][:, j, :], col("rw_r_k", 4 + j),
                                                       kdka[:, j, :], ALU.mult, ALU.add))
                op(("rk", j), V.tensor_tensor(kdka[:, j, :], kdka[:, j, :], r_[:, j, :], ALU.mult))
            for j in range(4):
                ve.wait_ge(pe_done, at(PE, ("rk", j)))
                V.tensor_tensor(bonus[:, j, :], bank[4 + j], v_[:, j, :], ALU.mult
                                ).then_inc(vec_done, did(VE, "bonus" if j == 3 else ("bonus", j)))
            op("state 0", V.memset(state, 0.0))
            u = 0
            for d in range(2):
                m_t = const("upper" if d == 0 else "lower", 256)
                m_a = const("lower" if d == 0 else "upper")
                for step in range(NCH):
                    c = step if d == 0 else step ^ 1
                    cs_ = slice(c * P, c * P + P)
                    for pg in range(2):
                        js = slice(2 * pg, 2 * pg + 2)
                        ve.wait_ge(act_done, at(AC, ("ei", u, 1)))
                        V.scalar_tensor_tensor(ar[:, :, 0:P], kk[:, js, cs_], -1.0, ex[:, :, P:2 * P],
                                               ALU.mult, ALU.mult).then_inc(vec_done, did(VE, ("ar a", u)))
                        V.tensor_tensor(ar[:, :, P:2 * P], r_[:, js, cs_], ex[:, :, 0:P], ALU.mult
                                        ).then_inc(vec_done, did(VE, ("ar r", u)))
                        V.tensor_tensor(bh, ic[d][:, js, cs_], ei, ALU.mult
                                        ).then_inc(vec_done, did(VE, ("bh", u)))
                        V.tensor_tensor(kh, kd[d][:, js, cs_], ei, ALU.mult
                                        ).then_inc(vec_done, did(VE, ("kh", u)))
                        for jj in range(2):
                            V.tensor_scalar(sin_[:, jj, :], state[:, 4 * d + 2 * pg + jj, :],
                                            ex[:, jj, 256:257], None, ALU.mult
                                            ).then_inc(vec_done, did(VE, ("sin", u) if jj else ("sin 0", u)))
                        for q in range(2):
                            ve.wait_ge(pe_done, at(PE, ("grams", u, q)))
                            for name, b, dst in (("bb", 3 + q, bb), ("kb", 5 + q, kb)):
                                V.tensor_tensor(dst[:, 2 * q:2 * q + 2, :], cut(bank[b], 0, 2, 256),
                                                wide(m_t[:, None, :], 2, 256), ALU.mult
                                                ).then_inc(vec_done, did(VE, (name, u, q)))
                        for q in range(2):
                            ve.wait_ge(pe_done, at(PE, ("A", u, q)))
                            V.tensor_tensor(dm[:, 2 * q:2 * q + 2, :], cut(bank[q], 0, 2, P),
                                            wide(m_a[:, None, :], 2, P), ALU.mult
                                            ).then_inc(vec_done, did(VE, ("dm", u, q)))
                        ve.wait_ge(vec_done, now(VE))
                        diag = wide(const("diag16")[:, None, :], 4, P)
                        V.tensor_tensor(E_[0], bb[:, :, 0:P], diag, ALU.mult
                                        ).then_inc(vec_done, did(VE, ("E0", u)))
                        op(("D0", u), V.tensor_tensor(D_[0], dm, diag, ALU.mult))
                        eye = wide(ident[:, None, :], 4, P)
                        V.tensor_tensor(TT_[0], E_[0], eye, ALU.add).then_inc(vec_done, did(VE, ("TT1", u)))
                        op(("T1", u), V.tensor_tensor(T_[0], D_[0], eye, ALU.add))

                        def add(name, src, dst, b):
                            V.tensor_tensor(dst, src, cut(bank[b], 0, 4, P), ALU.add
                                            ).then_inc(vec_done, did(VE, name))

                        for power, i in ((2, 0), (4, 1), (8, 0)):
                            ve.wait_ge(pe_done, at(PE, (f"T{power}", u)))
                            add((f"T{power}", u), T_[i], T_[1 - i], 3)
                            ve.wait_ge(pe_done, at(PE, (f"TT{power}", u)))
                            add((f"TT{power}", u), TT_[i], TT_[1 - i], 4)
                            ve.wait_ge(vec_done, now(VE))
                        cur = 1
                        for lv in range(3):
                            if lv:
                                ve.wait_ge(pe_done, at(PE, (("Z", lv - 1), u)))
                            off = wide(const(("off32", "off64", "off128")[lv])[:, None, :], 4, P)
                            V.tensor_tensor(bm, dm, off, ALU.mult).then_inc(vec_done, did(VE, ("bm", u, lv)))
                            if lv < 2:
                                ve.wait_ge(pe_done, at(PE, (("Tm", lv), u)))
                                add(("Tm", u, lv), T_[cur], T_[1 - cur], 3)
                            ve.wait_ge(pe_done, at(PE, (("TTm", lv), u)))
                            add(("TTm", u, lv), TT_[cur], TT_[1 - cur], 4)
                            ve.wait_ge(vec_done, now(VE))
                            cur = 1 - cur
                        ve.wait_ge(pe_done, at(PE, ("y", u)))
                        y_ = yt[:, c, 256 * pg:256 * pg + 256]
                        if d == 0:
                            V.tensor_copy(y_, bank[5][:, 0:256]).then_inc(vec_done, did(VE, ("y", "rw", u)))
                        else:
                            V.tensor_tensor(y_, y_, bank[5][:, 0:256], ALU.add
                                            ).then_inc(vec_done, did(VE, ("y", "rw", u)))
                        ve.wait_ge(pe_done, at(PE, ("s", u)))
                        op(("s sum", u), V.tensor_tensor(stt_, sin_, cut(bank[6], 0, 2, P), ALU.add))
                        for jj in range(2):
                            V.scalar_tensor_tensor(state[:, 4 * d + 2 * pg + jj, :], stt_[:, jj, :],
                                                   ex[:, jj, 257:258], const("head"), ALU.mult, ALU.mult
                                                   ).then_inc(vec_done, did(VE, ("state", u) if jj else ("state 0", u)))
                        ve.wait_ge(vec_done, now(VE))
                        u += 1
            yh = yt.rearrange("p c (h n) -> p (c h) n", n=HD)
            sq = cut(ring_t, 8192, 32, HD)
            m_, v_h, rt_ = small[:, 32:64], small[:, 64:96], small[:, 96:128]
            op("yr sum", V.tensor_reduce(m_, yh, AX.X, ALU.add))
            op("yr mean", V.tensor_scalar(m_, m_, 1.0 / HD, None, ALU.mult))
            op("yr centre", V.tensor_tensor(yh, yh, wide(m_[:, :, None], 32, HD), ALU.subtract))
            op("yr sq", V.tensor_tensor(sq, yh, yh, ALU.mult))
            op("yr ss", V.tensor_reduce(v_h, sq, AX.X, ALU.add))
            op("yr var", V.tensor_scalar(v_h, v_h, 1.0 / HD, GN_EPS, ALU.mult, ALU.add))
            ve.wait_ge(act_done, at(AC, "yr root"))
            op("yr rstd", V.reciprocal(m_, rt_))
            op("yr norm", V.tensor_tensor(yh, yh, wide(m_[:, :, None], 32, HD), ALU.mult))
            for j in range(4):
                ve.wait_ge(act_done, at(AC, ("gn", j)))
                op(("gn bonus", j), V.tensor_tensor(mix[:, j, :], mix[:, j, :], bonus[:, j, :], ALU.add))
                V.tensor_tensor(mix[:, j, :], mix[:, j, :], gate[:, j, :], ALU.mult
                                ).then_inc(vec_done, did(VE, "o_rw" if j == 3 else ("o_rw", j)))
            for j in range(KT):
                ve.wait_ge(pe_done, at(PE, ("mix out", j)))
                residual("mix res", j, bank[6 + j % 2], (0, 0, 2), (0, 1))

            norm(1, slice(0, T), False)
            for j in range(FT):
                ve.wait_ge(act_done, at(AC, ("sg", j)))
                ve.wait_ge(pe_done, at(PE, ("ffn3", "tile", j)))
                V.tensor_tensor(G[:, j, :], sg[j % 2], bank[2 * (j % 2) + 1], ALU.mult
                                ).then_inc(vec_done, did(VE, ("gu", j)))
            for n in range(KT):
                ve.wait_ge(pe_done, at(PE, ("ffn out", n)))
                residual("ffn res", n, bank[4 + n % 4], (0, 0, 5), (0, 1))

            norm(2, slice(0, T), False)
            ve.wait_ge(bias_in, 16)
            flat = rb.rearrange("p h (r k) -> p (h r) k", k=GRID_W)
            op("rb 0", V.tensor_tensor(flat, flat, wide(const("win", 64)[:, None, :], 96, 64), ALU.mult))
            op("rb", V.tensor_tensor(flat, flat, wide(const("out_win", 64)[:, None, :], 96, 64), ALU.add))
            for hd in range(16):
                for qt in range(2):
                    ve.wait_ge(pe_done, at(PE, ("s1", hd, qt)))
                    if hd:
                        ve.wait_ge(pe_done, at(PE, ("pt1", hd - 1, qt)))
                    V.tensor_copy(pr[:, qt, CTX], bank[qt][:, CTX]).then_inc(vec_done, did(VE, ("s ctx", hd, qt)))
                    i0 = (2 - 2 * qt) * GRID_W
                    op(("s lat", hd, qt), V.tensor_tensor(pr[:, qt, LAT], bank[qt][:, LAT],
                                                          rb[:, hd, i0:i0 + TL], ALU.add))
                    V.tensor_reduce(stat[:, qt:qt + 1], pr[:, qt, :], AX.X, ALU.max, negate=True
                                    ).then_inc(vec_done, did(VE, ("m1", hd, qt)))
                for qt in range(2):
                    ve.wait_ge(act_done, at(AC, ("exp1", hd, qt)))
                    op(("r1", hd, qt), V.reciprocal(stat[:, 4 + qt:5 + qt], stat[:, 2 + qt:3 + qt]))
                    V.tensor_scalar(pr[:, qt, :], pr[:, qt, :], stat[:, 4 + qt:5 + qt], None, ALU.mult
                                    ).then_inc(vec_done, did(VE, ("p1", hd, qt)))
                hp = slice(64 * (hd % 2), 64 * (hd % 2) + 64)
                ve.wait_ge(pe_done, at(PE, ("o1", hd)))
                V.tensor_copy(o1[hp, hd // 2, :], bank[4 + hd % 2][hp, 0:TL]
                              ).then_inc(vec_done, did(VE, ("o1", hd)))
            for j in range(KT):
                ve.wait_ge(pe_done, at(PE, ("na out", j)))
                residual("na res", j, bank[6 + j % 2][:, 0:TL], (0, 1, 2), (1,))

            norm(3, LAT, False)
            ve.wait_ge(pe_done, at(PE, "router"))
            op("lg", V.tensor_tensor(lg, cut(bank[1], 0, 2, NE),
                                     wide(row("moe_router_b", 8)[:, None, :], 2, NE), ALU.add))
            for c in range(2):
                a, b = lg[:, c, :][:, :, None], lg[:, c, :][:, None, :]
                V.tensor_tensor(cmp_[:, c], wide(b, NE, NE), wide(a, NE, NE), ALU.is_gt
                                ).then_inc(vec_done, did(VE, ("gt", c)))
                op(("eq", c), V.tensor_tensor(cm2[:, c], wide(b, NE, NE), wide(a, NE, NE), ALU.is_equal))
                op(("tie", c), V.tensor_tensor(cm2[:, c], cm2[:, c], cut(const("first", 64), 0, NE, NE),
                                               ALU.mult))
                op(("beats", c), V.tensor_tensor(cmp_[:, c], cmp_[:, c], cm2[:, c], ALU.add))
                op(("rank", c), V.tensor_reduce(rank[:, c, :], cmp_[:, c], AX.X, ALU.add))
            op("lg top", V.tensor_reduce(mx, lg, AX.X, ALU.max))
            op("lg max", V.tensor_tensor(ge, lg, wide(mx[:, :, None], 2, NE), ALU.subtract))
            ve.wait_ge(act_done, at(AC, "ge"))
            op("top 2", V.scalar_tensor_tensor(gates, rank, 1.5, ge, ALU.is_lt, ALU.mult))
            op("gate sum", V.tensor_reduce(sm, gates, AX.X, ALU.add))
            op("gate 1/sum", V.reciprocal(mx, sm))
            op("gates", V.tensor_tensor(gates, gates, wide(mx[:, :, None], 2, NE), ALU.mult))
            op("zero", V.memset(um[0], 0.0))
            before = now(VE)
            pper, aper = at(PE, ("per", "moe")), at(AC, ("per", "moe"))
            vper = at(VE, ("per", "moe"))
            ve.wait_ge(act_done, at(AC, ("gate row", NE - 1)))
            with ve.Fori(0, NE) as e:
                for j in range(FT):
                    u_ = cut(arena, 8192 + 256 * (j % 2), 1, TL)
                    ve.wait_ge(pe_done, e * pper + at(PE, ("moe tile", 1, j)))
                    V.tensor_tensor(u_, bank[2 * (j % 2) + 1][:, None, 0:TL],
                                    gbc[:, bass.ds(e, 1), :], ALU.mult
                                    ).then_inc(vec_done, did(VE, ("um", j)))
                    ve.wait_ge(vec_done, e * vper + now(VE))
                    ve.wait_ge(act_done, e * aper + at(AC, ("sg m", j)))
                    V.tensor_tensor(Gm[:, j, :], um[j % 2], sgm[j % 2], ALU.mult
                                    ).then_inc(vec_done, did(VE, ("gu m", j)))
            counts.loop(VE, "moe", before, NE)
            ve.wait_ge(pe_done, at(PE, ("end", "moe")))
            for n in range(KT):
                V.scalar_tensor_tensor(hT[:, n, LAT], bank[4 + n // 2][:, 256 * (n % 2):256 * (n % 2) + 256],
                                       mod(0, 1, 5, n, 1), hT[:, n, LAT], ALU.mult, ALU.add
                                       ).then_inc(vec_done, did(VE, "moe res" if n == 7 else ("moe res", n)))
            ve.wait_ge(vec_done, now(VE))
            norm(4, LAT, False)

            norm(5, slice(0, T), True)
            V.memset(vp[:, :, 0:1], 0.0).then_inc(vec_done, did(VE, "vp edge 0"))
            V.memset(vp[:, :, TL + 1:TL + 2], 0.0).then_inc(vec_done, did(VE, "vp edge 1"))
            lq = cut(row("lambda_qk_2", 256), 0, 2, 2, 64)
            op("lam products", V.tensor_tensor(lprod[:, 0:2, :], lq[:, :, 0, :], lq[:, :, 1, :], ALU.mult))
            op("lam sums", V.tensor_reduce(lamv[:, 0:2], lprod[:, 0:2, :], AX.X, ALU.add))
            ve.wait_ge(act_done, at(AC, ("in2", 11)))
            op("gc v", V.tensor_tensor(vp[:, :, 1:TL + 1], vp[:, :, 1:TL + 1], gc, ALU.mult))
            for j in range(4):
                dst = mix[:, j, LAT]
                op(("conv2", j, 0), V.tensor_scalar(dst, vp[:, j, 0:TL], col("conv_w_2", j), None, ALU.mult))
                for tap in (1, 2):
                    op(("conv2", j, tap), V.scalar_tensor_tensor(dst, vp[:, j, tap:tap + TL],
                                                                 col("conv_w_2", 4 * tap + j), dst,
                                                                 ALU.mult, ALU.add))
                V.tensor_tensor(dst, dst, gb[:, j, :], ALU.mult
                                ).then_inc(vec_done, did(VE, "o_conv" if j == 3 else ("o_conv", j)))
            for n in range(8):
                src = q2[:, n, :] if n < 4 else k2[:, n - 4, LAT]
                ve.wait_ge(pe_done, at(PE, ("turn", n)))
                V.tensor_tensor(rt[:, n % 2, :], bank[6 + n % 2][:, 0:TL], const("sin", 256), ALU.mult
                                ).then_inc(vec_done, did(VE, ("rope sin", n)))
                op(("rope cos", n), V.tensor_tensor(src, src, const("cos", 256), ALU.mult))
                op(("rope", n), V.tensor_tensor(src, src, rt[:, n % 2, :], ALU.add))
            ve.wait_ge(act_done, at(AC, "lam"))
            op("lam 0", V.tensor_tensor(lamv[:, 4:5], lamv[:, 3:4], lamv[:, 2:3], ALU.subtract))
            op("- lam", V.tensor_scalar(lamv[:, 4:5], lamv[:, 4:5], -LAM_INIT, None, ALU.add))
            s_ = small[:, 150:160]
            for hd in range(4):
                for qt in range(2):
                    for cp in range(2):
                        ve.wait_ge(pe_done, at(PE, ("s2", hd, qt, cp)))
                        V.tensor_reduce(s_[:, cp:cp + 1], bank[cp], AX.X, ALU.max, negate=True
                                        ).then_inc(vec_done, did(VE, ("m2", hd, qt, cp)))
                    ve.wait_ge(act_done, at(AC, ("exp2", hd, qt, 1)))
                    op(("r2", hd, qt), V.reciprocal(s_[:, 4:6], s_[:, 2:4]))
                    op(("lam r2", hd, qt), V.tensor_tensor(s_[:, 5:6], s_[:, 5:6], lamv[:, 4:5], ALU.mult))
                    op(("lam p", hd, qt), V.tensor_scalar(p2[:, 1, :], p2[:, 1, :], s_[:, 5:6], None, ALU.mult))
                    if hd:
                        ve.wait_ge(pe_done, at(PE, ("pt2", hd - 1, qt)))
                    op(("p2", hd, qt), V.scalar_tensor_tensor(pd[:, qt, :], p2[:, 0, :], s_[:, 4:5],
                                                              p2[:, 1, :], ALU.mult, ALU.add))
            ve.wait_ge(pe_done, at(PE, "subln"))
            for i, t in enumerate((tmpA, tmpB)):
                V.tensor_scalar(t, bank[6 + i], 1.0 / P, SUBLN_EPS, ALU.mult, ALU.add
                                ).then_inc(vec_done, did(VE, ("subln", i)))
            for i, t in enumerate((tmpA, tmpB)):
                ve.wait_ge(act_done, at(AC, ("subln", i)))
                op(("subln rstd", i), V.reciprocal(t, t))
                o_ = o2[:, 2 * i:2 * i + 2, :]
                op(("subln o", i), V.tensor_tensor(o_, o_, cut(t, 0, 2, TL), ALU.mult))
                V.tensor_scalar(mix[:, 4 + 2 * i:6 + 2 * i, LAT], o_, col("subln_g_2", 0), 1.0 - LAM_INIT,
                                ALU.mult, ALU.mult).then_inc(vec_done, did(VE, "o_attn" if i else "o_attn 0"))

            def add_scaled(name, j, src, gate):
                op((name, j, "gated"), V.tensor_scalar(tmpA[:, 0:TL], src, mod(*gate, j, 1), None, ALU.mult))
                op((name, j), V.scalar_tensor_tensor(hT[:, j, LAT], hT[:, j, LAT], ALPHA, tmpA[:, 0:TL],
                                                     ALU.mult, ALU.add))

            def outwards(name, st, gate):
                for j in range(KT):
                    ve.wait_ge(pe_done, at(PE, (name, j)))
                    add_scaled(name, j, bank[2 + j % 2][:, 0:TL], gate)
                norm(st, LAT, True)

            def mlp(i, st):
                norm(st, LAT, True)
                for j in range(F2T):
                    ve.wait_ge(pe_done, at(PE, (("mlp1", i), j)))
                    x_ = bank[2 + j % 2][:, 0:TL]
                    V.tensor_scalar(sg[0][:, 256 * (j % 2):256 * (j % 2) + 256], x_, 0.0, None, ALU.max
                                    ).then_inc(vec_done, did(VE, ("relu", i, j)))
                    ve.wait_ge(vec_done, now(VE))
                    r = sg[0][:, 256 * (j % 2):256 * (j % 2) + 256]
                    V.tensor_tensor(G2[:, j, :], r, r, ALU.mult).then_inc(vec_done, did(VE, ("relu2", i, j)))
                for j in range(KT):
                    ve.wait_ge(pe_done, at(PE, (("mlp", i), j)))
                    add_scaled(("mlp", i), j, bank[4 + j % 2][:, 0:TL], (1, i, 5))
                norm(st + 1, LAT, True)

            outwards("out2", 6, (1, 0, 2))
            mlp(0, 7)
            norm(9, LAT, True)
            outwards("fourier", 10, (1, 1, 2))
            mlp(1, 11)


INPUTS = ("w_ada", "ada_w_2", "mix_w_in", "mix_w_out", "rw_w_up", "rw_a_up", "rw_g_up",
          "ffn_w1", "ffn_w3", "ffn_w2", "na_w_qkv", "na_w_out", "moe_router_w",
          "moe_w1", "moe_w3", "moe_w2", "w_in_2", "w_out_mix_2", "w_out_fourier_2",
          "mlp_w1_2", "mlp_w2_2")


def columns(inputs):
    parts = []
    for name, width in COLUMNS:
        if name in ("mu_prev", "mu_next"):
            v = inputs["rw_mu"][0, int(name == "mu_next"), :13 * P]
        else:
            v = inputs[name].reshape(-1)
        parts.append(v.reshape(width, P).T)
    return np.ascontiguousarray(np.concatenate(parts, axis=1))


def broadcast_rows(inputs):
    parts = [inputs[name].reshape(-1) for name, _ in ROWS]
    return np.ascontiguousarray(np.broadcast_to(np.concatenate(parts), (P, NROW)))


def bias_by_query(rpb):
    cols_ = np.clip(np.arange(GRID_W)[None, :] - np.arange(GRID_W)[:, None] + NA_KW - 1,
                    0, 2 * NA_KW - 2)
    halves = [rpb[:, 5 - half:11 - half][:, :, cols_].transpose(2, 0, 1, 3) for half in range(2)]
    return np.ascontiguousarray(np.concatenate(halves, axis=0).reshape(P, -1))


def program(new_core, arrays):
    known = None
    for _ in range(2):
        nc = new_core()
        w = {name: nc.dram_tensor(f"in_{name}", a.shape, F32, kind="ExternalInput").ap()
             for name, a in arrays.items()}
        out = nc.dram_tensor("out", (D, TL), F32, kind="ExternalOutput").ap()
        counts = Counts(known)
        build(nc, w, out, counts)
        known = counts.values
    return nc


def kernel(**inputs):
    import concourse.bacc as bacc
    from concourse.bass_utils import run_bass_kernel_spmd as run

    inputs = {name: np.asarray(a) for name, a in inputs.items()}
    arrays = {name: np.ascontiguousarray(inputs[name]) for name in INPUTS}
    arrays["xT"] = np.ascontiguousarray(inputs["x"][0].T)
    arrays["ctxT"] = np.ascontiguousarray(inputs["ctx"][0].T)
    arrays["ctx2T"] = np.ascontiguousarray(inputs["ctx_2"][0].T)
    arrays["cols"] = columns(inputs)
    arrays["rows"] = broadcast_rows(inputs)
    arrays["w0row"] = np.ascontiguousarray(np.broadcast_to(inputs["rw_w0"].reshape(-1), (P, 2 * RW)))
    arrays["bias"] = bias_by_query(inputs["na_rpb"][0])
    arrays["mu_g"] = np.ascontiguousarray(inputs["rw_mu"][0, :, 13 * P:].T)
    arrays["consts"] = constants()
    nc = program(lambda: bacc.Bacc("TRN2", target_bir_lowering=False, num_devices=1), arrays)
    r = run(nc, [{f"in_{name}": a for name, a in arrays.items()}], core_ids=[0])
    return np.ascontiguousarray(r.results[0]["out"].T)[None]
```

```python
import math
from contextlib import ExitStack

import numpy as np

import concourse.bass as bass
from concourse import mybir

F32 = mybir.dt.float32
ALU = mybir.AluOpType
ACT = mybir.ActivationFunctionType
AX = mybir.AxisListType

P = 128
D = 1024
KT = D // P
TC = 256
TL = 256
T = TC + TL
NCH = T // P
CTX, LAT = slice(0, TC), slice(TC, T)
SEQS = (CTX, LAT)
RMS_EPS, LN_EPS, GN_EPS, SUBLN_EPS = 1e-6, 1e-6, 64e-5, 1e-5
RW = 512
HD = 64
RW_COLS = 3 * RW + 64 + 64 + 96
ZG0 = RW_COLS
XBC0 = ZG0 + RW
DT0 = XBC0 + 1024
FF = 2816
FT = FF // P
FF2 = 4096
F2T = FF2 // P
NE = 8
GRID_W, NA_KW = 64, 16
ALPHA = 4.0 ** 0.25
LAM_INIT = 0.8 - 0.6 * math.exp(0.0)
DECAY = math.exp(-0.5)

RING = 6
SLOT = FT * P

ADA = 24
LATER = [(0, 1), (1, 0), (1, 1)]
GROUPS = [3 - j % 2 for j in range(FT)] + [3, 3, 3, 2, 2, 2, 1, 1]
GROUP_OF = [g for g, n in enumerate(GROUPS) for _ in range(n)]
assert len(GROUP_OF) == ADA * len(LATER) and len(GROUPS) == FT + KT
CHUNKS, SUMS = 4, 8

COLUMNS = [("b_ada", 96), ("ada_b_2", 96), ("norm_mix", 16), ("norm_ffn", 16), ("norm_final", 8),
           ("c", 8), ("c_ctx", 8), ("c_2", 8), ("c_ctx_2", 8), ("rw_a0", 8), ("rw_k_k", 4),
           ("rw_k_a", 4), ("rw_r_k", 8), ("rw_gn_w", 4), ("rw_gn_b", 4), ("mb_conv_w", 40),
           ("mb_conv_b", 8), ("mb_norm_w", 4), ("mu_prev", 13), ("mu_next", 13), ("ln_g_2", 32),
           ("ln_b_2", 32), ("conv_w_2", 12), ("subln_g_2", 1)]
ROWS = [("mb_dt_bias", 16), ("mb_a_log", 16), ("mb_d", 8), ("moe_router_b", 8), ("lambda_qk_2", 256)]


def offsets(parts):
    out, n = {}, 0
    for name, width in parts:
        out[name] = n
        n += width
    return out, n


COL, NCOL = offsets(COLUMNS)
ROW, NROW = offsets(ROWS)

CONSTS = [("ident", 128), ("mean", 128), ("head", 128), ("upper", 128), ("upper_in", 128),
          ("lower", 128), ("lower_in", 128), ("diag16", 128), ("off32", 128), ("off64", 128),
          ("off128", 128), ("decay_f", 258), ("decay_b", 258), ("cs128", 256), ("dft_c", 512),
          ("dft_s", 512), ("cos", 256), ("sin", 256), ("turn", 128), ("win", 64), ("out_win", 64),
          ("first", 64), ("ones", 128), ("count", 128)]
CO, NCONST = offsets(CONSTS)
BIG = -1e30


def constants():
    i = np.arange(P)[:, None]
    t = np.arange(P)[None, :]
    c = {}
    c["ident"] = i == t
    c["mean"] = np.full((P, P), 1.0 / D)
    c["ones"] = np.ones((P, P))
    c["count"] = np.broadcast_to(t, (P, P))
    c["head"] = i // HD == t // HD
    c["upper"], c["upper_in"], c["lower"], c["lower_in"] = i < t, i <= t, i > t, i >= t
    c["diag16"] = i // 16 == t // 16
    for size in (32, 64, 128):
        c[f"off{size}"] = (i // size == t // size) & (i // (size // 2) != t // (size // 2))
    mid = P // 2
    c["decay_f"] = -DECAY * np.concatenate(
        [(i <= t) * 1.0 - (i < mid), (i < t) * 1.0 - (i < mid), i < mid, i >= mid], 1)
    c["decay_b"] = -DECAY * np.concatenate(
        [(i >= t) * 1.0 - (i >= mid), (i > t) * 1.0 - (i >= mid), i >= mid, i < mid], 1)
    ang = 2 * np.pi * ((i * t) % P) / P
    c["cs128"] = np.concatenate([np.cos(ang), np.sin(ang)], 1)
    n = np.arange(TL)
    ang = 2 * np.pi * ((n[:, None] * n[None, :]) % TL) / TL
    norm = 1 / math.sqrt(TL * P)
    c["dft_c"] = (norm * np.cos(ang)).reshape(2, P, TL).transpose(1, 0, 2).reshape(P, 512)
    c["dft_s"] = (-norm * np.sin(ang)).reshape(2, P, TL).transpose(1, 0, 2).reshape(P, 512)
    half = 16
    inv = np.float32(10000.0) ** (-np.arange(half, dtype=np.float32) / np.float32(half))
    ch = np.arange(P)
    pos = np.where((ch % 64 < 32)[:, None], (n // GRID_W)[None, :], (n % GRID_W)[None, :])
    ang = pos.astype(np.float32) * inv[ch % half][:, None].astype(np.float32)
    c["cos"], c["sin"] = np.cos(ang), np.sin(ang)
    turn = np.zeros((P, P))
    for m in range(P):
        if m % 32 < half:
            turn[m + half, m] = -1.0
        else:
            turn[m - half, m] = 1.0
    c["turn"] = turn
    q, k = np.arange(P)[:, None] % GRID_W, np.arange(GRID_W)[None, :]
    start = np.clip(q - NA_KW // 2, 0, GRID_W - NA_KW)
    win = (k >= start) & (k < start + NA_KW)
    c["win"], c["out_win"] = win, np.where(win, 0.0, BIG)
    a, b = np.arange(NE)[:, None], np.arange(NE)[None, :]
    c["first"] = np.broadcast_to((b < a).reshape(1, 64), (P, 64))
    return np.ascontiguousarray(
        np.concatenate([np.asarray(c[n], np.float32) for n, _ in CONSTS], 1))


def plan_slots(w):
    slots, first = [], {}

    def add(name, source, k0, kt, cols):
        first[name] = len(slots)
        for n0, width in cols:
            src = source[k0:k0 + kt * P, n0:n0 + width].rearrange("(k p) n -> p k n", p=P)
            slots.append((kt, width, src))

    def by(start, n, width=256):
        return [(start + n0, min(width, n - n0)) for n0 in range(0, n, width)]

    first["ada"] = 0
    slots += ["ada"] * ADA
    win = w["mix_w_in"][0]
    add("zg", win, 0, KT, by(ZG0, RW))
    add("dt", win, 0, KT, [(DT0, 16)])
    add("xbc", win, 0, KT, by(XBC0, 1024))
    add("rkv", win, 0, KT, by(0, 3 * RW))
    add("lora", win, 0, KT, [(3 * RW, 224)])
    first["rwkv_end"] = len(slots)
    add("mix_out", w["mix_w_out"][0], 0, KT, by(0, D))
    first["ffn"] = len(slots)
    for b in range(FT // 2):
        add(("ffn1", b), w["ffn_w1"][0], 0, KT, [(256 * b, 256)])
        add(("ffn3", b), w["ffn_w3"][0], 0, KT, [(256 * b, 256)])
    add("ffn2", w["ffn_w2"][0], 0, FT, by(0, D, P))
    add("qkv", w["na_w_qkv"][0], 0, KT, by(0, 3 * D))
    add("na_out", w["na_w_out"][0], 0, KT, by(0, D))
    add("router", w["moe_router_w"][0], 0, KT, [(0, NE)])
    first["moe"] = len(slots)
    add("in2", w["w_in_2"][0], 0, KT, by(0, 3072))
    add("out2", w["w_out_mix_2"][0], 0, KT, by(0, D))

    def mlp(i):
        add(("mlp1", i), w["mlp_w1_2"][i], 0, KT, by(0, FF2))
        first["mlp2", i] = len(slots)
        for n in range(KT):
            for half in range(2):
                add(("mlp2", i, n, half), w["mlp_w2_2"][i], half * 16 * P, 16, [(n * P, P)])

    mlp(0)
    add("fourier", w["w_out_fourier_2"][0], 0, KT, by(0, D))
    mlp(1)
    return slots, first


class Counts:

    def __init__(self, known=None):
        self.known = known
        self.count = {}
        self.values = {}

    def did(self, engine, *names):
        self.count[engine] = self.count.get(engine, 0) + 1
        for name in names:
            assert (engine, name) not in self.values, (engine, name)
            self.values[engine, name] = self.count[engine]
        return 1

    def at(self, engine, name):
        return 1 if self.known is None else self.known[engine, name]

    def now(self, engine):
        return self.count[engine]

    def loop(self, engine, name, before, turns):
        per = self.count.get(engine, 0) - before
        self.values[engine, ("per", name)] = per
        self.count[engine] = before + per * turns
        self.values[engine, ("end", name)] = self.count[engine]


def build(nc, w, out, counts, stop="end"):
    did, at, now = counts.did, counts.at, counts.now
    PE, AC, VE = "tensor", "scalar", "vector"
    PEM, ACM, VEM = "tensor, experts", "scalar, experts", "vector, experts"
    slots, first = plan_slots(w)
    with ExitStack() as ctx:
        def sb(name, cols, *shape):
            t = ctx.enter_context(nc.sbuf_tensor(name, [P, cols], F32))
            return t[:, :]

        def sem(name):
            return ctx.enter_context(nc.semaphore(name))

        def cut(t, start, *dims):
            n = int(np.prod(dims))
            ap = t[:, start:start + n]
            if len(dims) == 2:
                ap = ap.rearrange("p (a b) -> p a b", a=dims[0])
            if len(dims) == 3:
                ap = ap.rearrange("p (a b c) -> p a b c", a=dims[0], b=dims[1])
            if len(dims) == 4:
                ap = ap.rearrange("p (a b c d) -> p a b c d", a=dims[0], b=dims[1], c=dims[2])
            return ap

        consts, cols, rows = sb("consts", NCONST), sb("cols", NCOL), sb("rows", NROW)
        h_t, a_t, mix_t = sb("h", KT * T), sb("a", KT * T), sb("mix", KT * T)
        hT, aT, mix = (cut(t, 0, KT, T) for t in (h_t, a_t, mix_t))
        ring_t = sb("ring", RING * SLOT)
        csil = cut(sb("csil", 32), 0, 2, KT, 2)
        mods = cut(sb("mods", 384), 0, 192, 2)
        gs = cut(sb("gs", 128), 0, 8, KT, 2)
        tmpA, tmpB = sb("tmpA", T), sb("tmpB", T)
        small = sb("small", 800)
        arena = sb("arena", 15872)
        bank = [ctx.enter_context(nc.psum_tensor(f"bank{b}", [P, 512], F32))[:, :] for b in range(8)]

        def const(name, width=128):
            return consts[:, CO[name]:CO[name] + width]

        def col(name, k, n=1):
            return cols[:, COL[name] + k:COL[name] + k + n]

        def row(name, n):
            return rows[:, ROW[name]:ROW[name] + n]

        def mod(block, layer, piece, k, s):
            return mods[:, 96 * block + 48 * layer + 8 * piece + k, s:s + 1]

        ident = const("ident")
        loaded = sem("loaded")
        w_full = [sem(f"w_full{i}") for i in range(RING)]
        pe_done, act_done, vec_done = sem("pe_done"), sem("act_done"), sem("vec_done")
        pe_moe, ac_moe, ve_moe = sem("pe_moe"), sem("ac_moe"), sem("ve_moe")
        chunk_full = [sem(f"chunk_full{i}") for i in range(CHUNKS)]
        m_full = [sem(f"m_full{i}") for i in range(RING)]
        block_info = ctx.enter_context(nc.sbuf_tensor("block_info", [1, 16], mybir.dt.int32))[:, :]
        ctx2_in, bias_in, up_in, again_in, stored = (
            sem(n) for n in ("ctx2_in", "bias_in", "up_in", "again_in", "stored"))
        UNITS = [(d, step if d == 0 else step ^ 1, pg)
                 for d in range(2) for step in range(NCH) for pg in range(2)]

        def slot(s):
            kt, width, _ = slots[s]
            return cut(ring_t, (s % RING) * SLOT, kt, width)

        def filled(s):
            return 16 * (s // RING + 1)

        mod_rows = cut(mix_t[0:2, :], 0, 3, 512)

        xpad = cut(arena, 0, 8, 2, TC + 4)
        xb = cut(arena, 4160, 8, T)
        xt = cut(arena, 8256, NCH, RW)
        bt = cut(arena, 10304, NCH, 256)
        zg = cut(arena, 11328, NCH, RW)
        ym = cut(arena, 13376, NCH, RW)
        gram = cut(arena, 0, 2, 2, NCH, P)
        xdt = cut(arena, 2048, NCH, RW)
        dec_t, mt_t = mix_t[:, 0:1024], mix_t[:, 1024:2048]
        dec, mt = cut(mix_t, 0, 8, P), cut(mix_t, 1024, 8, P)
        xd2, st_m = tmpA, tmpB
        dt_raw, dtv, a_tok, cs, ecs, sp1 = (cut(small, 64 * i, NCH, 2, 8) for i in range(6))
        a_neg, etot, dcs = small[:, 384:400], small[:, 400:408], small[:, 408:416]
        ss_m, rs_m = cut(small, 416, NCH, 2), cut(small, 424, NCH, 2)

        r_, k_, v_ = (cut(arena, 2048 * i, 4, T) for i in range(3))
        kk = cut(arena, 6144, 4, T)
        vt = cut(arena, 8192, NCH, RW)
        llw, llg = arena[:, 10240:10752], arena[:, 10752:11264]
        upw, gup = arena[:, 11264:11776], arena[:, 11776:12288]
        w0row = arena[:, 12288:13312]
        zpad = [cut(arena, 13312 + 516 * i, 2, TC + 2) for i in range(4)]
        mu0 = small[:, 0:13]
        mu0g, mug = small[:, 13:14], small[:, 14:16]
        sig = [cut(ring_t, 2048 * d, NCH, RW) for d in range(2)]
        ic = [cut(ring_t, 4096 + 2048 * d, 4, T) for d in range(2)]
        kd = [cut(ring_t, 8192 + 2048 * d, 4, T) for d in range(2)]
        yt = cut(ring_t, 12288, NCH, RW)
        gate, bonus = cut(a_t, 0, 4, T), cut(a_t, 2048, 4, T)
        kdka = cut(mix_t, 0, 4, T)

        free = {"arena": [10240, 15872], "k": [2048, 4096], "v": [4096, 6144], "mix": [0, 2048],
                "ring": [14336, 16896], "h": [0, 4096]}
        of = {"arena": arena, "k": arena, "v": arena, "mix": mix_t, "ring": ring_t,
              "h": h_t}

        def take(where, *dims):
            start = free[where][0]
            free[where][0] += int(np.prod(dims))
            assert free[where][0] <= free[where][1], where
            return cut(of[where], start, *dims)

        ex = [take("arena", 2, 258) for _ in range(2)]
        ei = take("arena", 2, P)
        ar = [take(m, 2, 256) for m in ("arena", "h")]
        bh, kh = take("arena", 2, P), take("arena", 2, P)
        sin_ = [take(m, 2, P) for m in ("arena", "h")]
        bkt = [take(m, 4, P) for m in ("arena", "h")]
        bb = [take(m, 4, 256) for m in ("k", "h")]
        kb = [take(m, 4, 256) for m in ("k", "h")]
        dm = [take(m, 4, P) for m in ("arena", "h")]
        D_, E_ = [take("arena", 4, P) for _ in range(2)], [take("v", 4, P) for _ in range(2)]
        T_, TT_ = [take("ring", 4, P) for _ in range(2)], [take("ring", 4, P) for _ in range(2)]
        bm, zt = take("v", 4, P), take("v", 4, P)
        xs, us = take("mix", 2, P), take("mix", 2, P)
        stt_ = take("mix", 2, P)
        state = take("mix", 8, P)

        G = cut(arena, 0, FT, T)
        sg = [tmpA, tmpB]
        chunk = [cut(arena, FT * T + 1024 * i, 4, 256) for i in range(CHUNKS)]
        sums = [cut(mix_t, 512 * i, 2, 256) for i in range(SUMS)]

        q1 = cut(arena, 0, KT, TL)
        k1 = cut(mix_t, 0, KT, T)
        v1 = cut(arena, 2048, NCH, D)
        rb = cut(arena, 6144, 16, 6 * GRID_W)
        pr = cut(arena, 12288, 2, T)
        pt = cut(arena, 13312, NCH, TL)
        stat = small[:, 0:16]
        o1 = cut(a_t, 0, KT, TL)

        Gm = cut(arena, 0, FT, P)
        sgm = [cut(arena, 2816 + P * i, P) for i in range(2)]
        atok = cut(arena, 3072, 2, D)
        ac_ = cut(arena, 5120, KT, P)
        yp = cut(arena, 6144, D)
        pgt = cut(arena, 7168, 2 * P)
        pm, pgw = cut(arena, 7424, 2, P), cut(arena, 7680, 2, P)
        lg, gates, ge, rank, chosen = (cut(small, 16 * i, 2, NE) for i in range(5))
        cmp_, cm2 = cut(small, 80, 2, NE, NE), cut(small, 208, 2, NE, NE)
        mx, sm = small[:, 336:338], small[:, 338:340]
        place, over, order = cut(small, 340, 2, NE), small[:, 356:364], small[:, 364:372]
        posb, gateb = cut(small, 372, 2, 12), cut(small, 396, 2, 12)
        which, info = cut(small, 420, 3, NE), small[:, 444:460]
        w24 = cut(small, 460, 3, NE)

        gb = cut(arena, 0, 4, TL)
        gc = cut(arena, 1024, 4, TL)
        vp = cut(arena, 2048, 4, TL + 2)
        q2, k2 = cut(arena, 3080, 4, TL), cut(arena, 4104, 4, T)
        v2 = cut(arena, 6152, NCH, 512)
        p2 = cut(arena, 8200, 4, T)
        pt2 = cut(arena, 10248, NCH, TL)
        o2 = cut(arena, 11272, 4, TL)
        rt = cut(arena, 12296, 2, TL)
        pd = cut(arena, 12808, 2, T)
        lamv = small[:, 0:8]
        lprod = cut(small, 16, 4, 64)
        G2 = cut(arena, 0, F2T, TL)
        fab = cut(arena, 0, 2, KT, 256)

        block = ctx.enter_context(nc.Block())

        @block.sync
        def _(sy):
            for dst, src in ((consts, w["consts"]), (cols, w["cols"]), (rows, w["rows"]),
                             (hT[:, :, CTX], w["ctxT"].rearrange("(k p) n -> p k n", p=P)),
                             (hT[:, :, LAT], w["xT"].rearrange("(k p) n -> p k n", p=P))):
                sy.dma_start(dst, src).then_inc(loaded, 16)

            def load(s):
                old = s - RING
                if isinstance(slots[old], str):
                    sy.wait_ge(pe_done, at(PE, ("end", slots[old])))
                else:
                    sy.wait_ge(pe_done, at(PE, ("slot", old)))
                sy.dma_start(slot(s), slots[s][2]).then_inc(w_full[s % RING], 16)

            ada_marks = at(PE, ("per", "ada")) // 2
            src = w["w_ada"][0].rearrange("(k p) n -> p k n", p=P)
            for s in range(RING):
                sy.dma_start(cut(ring_t, s * SLOT, KT, 256), src[:, :, s * 256:s * 256 + 256]
                             ).then_inc(w_full[s], 16)
            with sy.Fori(1, ADA // RING) as turn:
                for s in range(RING):
                    sy.wait_ge(pe_done, turn * ada_marks + (at(PE, ("ada", 0, s)) - ada_marks))
                    sy.dma_start(cut(ring_t, s * SLOT, KT, 256),
                                 src[:, :, bass.ds(turn * 1536 + s * 256, 256)]
                                 ).then_inc(w_full[s], 16)

            def chunk_in(i):
                n, half = i // 2, i % 2
                b, layer = LATER[n // ADA]
                if i >= CHUNKS:
                    sy.wait_ge(vec_done, at(VE, ("chunk", i - CHUNKS)))
                src = w[("w_ada", "ada_w_2")[b]][layer].rearrange("(k p) n -> p k n", p=P)
                n0 = 256 * (n % ADA)
                sy.dma_start(chunk[i % CHUNKS], src[:, 4 * half:4 * half + 4, n0:n0 + 256]
                             ).then_inc(chunk_full[i % CHUNKS], 16)

            def tile_of(s):
                if first["ffn"] <= s < first["ffn2"]:
                    return 2 * ((s - first["ffn"]) // 2) + 1
                return FT + s - first["ffn2"] if first["ffn2"] <= s < first["qkv"] else -1

            chunks_in = 0
            s = ADA
            while s < len(slots):
                if s == first["mix_out"]:
                    sy.wait_ge(vec_done, at(VE, "ym end"))
                    sy.wait_ge(pe_done, at(PE, ("ym turned", 3)))
                    up = w["rw_w_up"][0].rearrange("d l c -> (d l) c")
                    sy.dma_start(upw[0:64, :], up).then_inc(up_in, 16)
                    up = w["rw_a_up"][0].rearrange("d l c -> (d l) c")
                    sy.dma_start(upw[64:128, :], up).then_inc(up_in, 16)
                    sy.dma_start(gup[0:96, :], w["rw_g_up"][0]).then_inc(up_in, 16)
                    sy.dma_start(w0row, w["w0row"]).then_inc(up_in, 16)
                    sy.dma_start(mug[0:96, :], w["mu_g"]).then_inc(up_in, 16)
                    sy.wait_ge(vec_done, at(VE, "o_rw"))
                    sy.wait_ge(pe_done, at(PE, ("yr turned", 3)))
                    for sl, name in ((CTX, "ctxT"), (LAT, "xT")):
                        sy.dma_start(hT[:, :, sl], w[name].rearrange("(k p) n -> p k n", p=P)
                                     ).then_inc(again_in, 16)
                if s == first["ffn"]:
                    for chunks_in in range(CHUNKS):
                        chunk_in(chunks_in)
                    chunks_in += 1
                while (0 < chunks_in < 2 * len(GROUP_OF) and
                       GROUP_OF[(chunks_in - CHUNKS) // 2] <= tile_of(s - RING)):
                    chunk_in(chunks_in)
                    chunks_in += 1
                if s == first["qkv"] + RING:
                    sy.wait_ge(pe_done, at(PE, ("ffn out", KT - 1)))
                    sy.wait_ge(vec_done, at(VE, ("chunk", 2 * len(GROUP_OF) - 1)))
                    sy.dma_start(rb.rearrange("p h n -> p (h n)"), w["bias"]).then_inc(bias_in, 16)
                if s == first["moe"]:
                    for old in range(s - RING, s):
                        sy.wait_ge(pe_done, at(PE, ("slot", old)))
                    per = at(PEM, ("per", "moe"))
                    sy.wait_ge(vec_done, at(VE, "blocks"))
                    blocks = sy.value_load(block_info[0:1, 12:13], min_val=NE, max_val=NE + 3)
                    with sy.Fori(0, blocks) as e:
                        expert = sy.value_load(block_info[0:1, bass.ds(e, 1)], min_val=0,
                                               max_val=NE - 1)
                        for i in range(30):
                            prev = (i - RING) % 30
                            sy.wait_ge(pe_moe, e * per + (at(PEM, ("slot", prev))
                                                          - (per if i < RING else 0)))
                            if i < 22:
                                src = w["moe_w1" if i % 2 == 0 else "moe_w3"][0]
                                src = src.rearrange("e (k p) n -> e p k n", p=P)
                                src = src[bass.ds(expert, 1), :, :, (i // 2) * 256:(i // 2 + 1) * 256]
                                dst = cut(ring_t, (i % RING) * SLOT, KT, 256)
                            else:
                                q, half = (i - 22) // 2, i % 2
                                src = w["moe_w2"][0].rearrange("e (h k p) n -> e p h k n", p=P, h=2)
                                src = src[bass.ds(expert, 1), :, half, :, q * 256:(q + 1) * 256]
                                dst = cut(ring_t, (i % RING) * SLOT, FT // 2, 256)
                            src = src.rearrange("e p k n -> p (e k) n")
                            sy.dma_start(dst, src).then_inc(m_full[i % RING], 16)
                    sy.wait_ge(pe_moe, blocks * per + per)
                load(s)
                if s == first["qkv"] + 11:
                    sy.wait_ge(vec_done, at(VE, ("norm", 2, KT - 1)))
                    sy.dma_start(hT[:, :, CTX], w["ctx2T"].rearrange("(k p) n -> p k n", p=P)
                                 ).then_inc(ctx2_in, 16)
                s += 1
            sy.wait_ge(act_done, at(AC, ("norm", 12, KT - 1, 1)))
            sy.dma_start(out.rearrange("(k p) n -> p k n", p=P), hT[:, :, LAT]).then_inc(stored, 16)
            sy.wait_ge(stored, 16)

        @block.tensor
        def _(pe):
            mm = nc.tensor.matmul

            def full(s):
                pe.wait_ge(w_full[s % RING], filled(s))
                return slot(s)

            def across(st, sl, src, b, name):
                n = sl.stop - sl.start
                for k in range(KT):
                    i = mm(bank[b][:, 0:n], const("mean"), src[:, k, sl], start=(k == 0),
                           stop=(k == KT - 1))
                i.then_inc(pe_done, did(PE, (name, st)))

            def rms(st, sl):
                pe.wait_ge(act_done, at(AC, ("square", st)))
                across(st, sl, mix, 0, "norm sum")

            def ln(st, sl):
                across(st, sl, hT, 1, "norm mean")
                rms(st, sl)

            def product(name, s0, n_slots, rhs, sl, banks, before):
                n = sl.stop - sl.start
                j = 0
                for s in range(s0, s0 + n_slots):
                    ws = full(s)
                    for t in range(2):
                        b = banks[j % len(banks)]
                        if j >= len(banks):
                            before(j - len(banks))
                        for k in range(KT):
                            i = mm(bank[b][:, 0:n], ws[:, k, t * P:t * P + P], rhs[:, k, sl],
                                   start=(k == 0), stop=(k == KT - 1))
                        marks = [(name, j)] + ([("slot", s)] if t else [])
                        i.then_inc(pe_done, did(PE, *marks))
                        j += 1

            pe.wait_ge(loaded, 5 * 16)
            pe.wait_ge(act_done, at(AC, ("cond", 3)))
            before = counts.count.get(PE, 0)
            with pe.Fori(0, 2) as pair:
                for half in range(2):
                    pe.wait_ge(vec_done, pair * 2 + (half + at(VE, "xpad edges") - 1))

                    def turn_rows(i):
                        pe.wait_ge(act_done, pair * 6 + (3 * half + i + 1 + at(AC, ("cond", 3))))
                        for t in range(4):
                            o = 8 * i + 2 * t
                            m = mm(bank[6 + half][:, o:o + 2], mod_rows[:, i, t * P:t * P + P],
                                   ident[0:2, 0:2], start=True, stop=True, skip_group_check=True)
                        m.then_inc(pe_done, did(PE, ("ada turned", half, i)))

                    for s in range(RING):
                        pe.wait_ge(w_full[s], pair * 32 + 16 * (half + 1))
                        ws = cut(ring_t, s * SLOT, KT, 256)
                        for k in range(KT):
                            i = mm(bank[3 * half + s // 2][0:2, 256 * (s % 2):256 * (s % 2) + 256],
                                   csil[:, 0, k, :], ws[:, k, :], start=(k == 0),
                                   stop=(k == KT - 1), skip_group_check=True)
                        i.then_inc(pe_done, did(PE, ("ada", half, s)))
                        if s in (3, 5):
                            turn_rows(s // 2 - 1)
                    turn_rows(2)
            counts.loop(PE, "ada", before, 2)

            rms(0, slice(0, T))
            pe.wait_ge(act_done, at(AC, ("norm", 0, KT - 1, 1)))
            for half in range(2):
                s = first["zg"] + half
                ws = full(s)
                for c in range(NCH):
                    for k in range(KT):
                        i = mm(bank[2 + c][:, half * 256:half * 256 + 256], aT[:, k, c * P:c * P + P],
                               ws[:, k, :], start=(k == 0), stop=(k == KT - 1),
                               skip_group_check=True)
                i.then_inc(pe_done, did(PE, ("zg", half), ("slot", s)))
            s = first["dt"]
            ws = full(s)
            for c in range(NCH):
                for k in range(KT):
                    i = mm(bank[6][:, 16 * c:16 * c + 16], aT[:, k, c * P:c * P + P], ws[:, k, :],
                           start=(k == 0), stop=(k == KT - 1), skip_group_check=True)
            i.then_inc(pe_done, did(PE, "dt", ("slot", s)))
            product("xbc", first["xbc"], 4, aT, slice(0, T), [0, 1],
                    lambda j: pe.wait_ge(act_done, at(AC, ("xbc", j))))

            def turned(name, src, b, sources=4):
                for m in range(sources):
                    i = nc.tensor.transpose(bank[b][:, m * P:m * P + P], src(m), ident)
                i.then_inc(pe_done, did(PE, name))

            pe.wait_ge(act_done, at(AC, ("xb", 7)))
            pe.wait_ge(act_done, at(AC, ("zg", 3)))
            for c in range(NCH):
                cs_ = slice(c * P, c * P + P)
                if c >= 2:
                    pe.wait_ge(vec_done, at(VE, ("bt", c - 2)))
                turned(("xt", c), lambda m: xb[:, m, cs_], 2 + c % 2)
                turned(("bt", c), lambda m: xb[:, 4 + m, cs_], 4 + c % 2, 2)
            for g in range(2):
                for c in range(NCH):
                    cs_ = slice(c * P, c * P + P)
                    i = mm(bank[g][:, c * P:c * P + P], xb[:, 4 + g, cs_], xb[:, 6 + g, cs_],
                           start=True, stop=True, skip_group_check=True)
            i.then_inc(pe_done, did(PE, "gram"))
            pe.wait_ge(vec_done, at(VE, "a_tok"))
            for c in range(NCH):
                for d in range(2):
                    i = mm(bank[6][:, 16 * c + 8 * d:16 * c + 8 * d + 8],
                           const("upper_in" if d == 0 else "lower_in"), a_tok[:, c, d, :],
                           start=True, stop=True, skip_group_check=True)
            i.then_inc(pe_done, did(PE, "cs"))
            u = 0
            for d in range(2):
                for step in range(NCH):
                    c = step if d == 0 else step ^ 1
                    cs_ = slice(c * P, c * P + P)
                    if u:
                        pe.wait_ge(vec_done, at(VE, ("dcs", u - 1)))
                    else:
                        pe.wait_ge(vec_done, at(VE, ("gram", 1)))
                        pe.wait_ge(vec_done, at(VE, ("bt", 3)))
                    for h in range(8):
                        i = mm(bank[h // 4][:, (h % 4) * P:(h % 4) * P + P],
                               a_tok[:, c, d, h:h + 1].broadcast_to([P, P]),
                               const("upper_in" if d == 0 else "lower_in"),
                               start=True, stop=True, skip_group_check=True)
                    i.then_inc(pe_done, did(PE, ("decay", u)))
                    if step:
                        for g in range(2):
                            i = mm(bank[3][:, 256 * g:256 * g + 256], xb[:, 6 + g, cs_],
                                   st_m[:, 256 * g:256 * g + 256], start=True, stop=True,
                                   skip_group_check=True)
                        i.then_inc(pe_done, did(PE, ("y off", u)))
                    pe.wait_ge(vec_done, at(VE, ("mt", u)))
                    for h in range(8):
                        i = mm(bank[2][:, h * HD:h * HD + HD], mt[:, h, :],
                               xdt[:, c, h * HD:h * HD + HD], start=True, stop=True,
                               skip_group_check=True)
                    i.then_inc(pe_done, did(PE, ("y diag", u)))
                    pe.wait_ge(vec_done, at(VE, ("xd2", u)))
                    for g in range(2):
                        i = mm(bank[4][:, 256 * g:256 * g + 256], bt[:, c, g * P:g * P + P],
                               xd2[:, 256 * g:256 * g + 256], start=True, stop=True,
                               skip_group_check=True)
                    i.then_inc(pe_done, did(PE, ("states", u)))
                    pe.wait_ge(vec_done, at(VE, ("unit", u)))
                    u += 1
            pe.wait_ge(vec_done, at(VE, "ym end"))
            for j in range(4):
                turned(("ym turned", j), lambda m: ym[:, m, j * P:j * P + P], 2 + j)

            product("rkv", first["rkv"], 6, aT, slice(0, T), [0, 1],
                    lambda j: pe.wait_ge(act_done, at(AC, ("rkv", j))))
            s = first["lora"]
            ws = full(s)
            for t, m in ((0, 128), (1, 96)):
                pe.wait_ge(act_done, at(AC, ("rkv", 10 + t)))
                for k in range(KT):
                    i = mm(bank[t][0:m, :], ws[:, k, t * P:t * P + m], aT[:, k, :],
                           start=(k == 0), stop=(k == KT - 1))
                i.then_inc(pe_done, did(PE, ("rkv", 12 + t), *([("slot", s)] if t else [])))
            pe.wait_ge(act_done, at(AC, ("norm ym", 3)))
            pe.wait_ge(vec_done, at(VE, ("shift", 11)))
            for c in range(NCH):
                turned(("vt", c), lambda m: v_[:, m, c * P:c * P + P], 4 + c)
            pe.wait_ge(act_done, at(AC, "lg"))
            pe.wait_ge(up_in, 5 * 16)
            for d in range(2):
                for c in range(NCH):
                    b = c % 2
                    if c >= 2 or d:
                        pe.wait_ge(vec_done, at(VE, ("w0", d if c >= 2 else 0, (c - 2) % 4)))
                    else:
                        pe.wait_ge(act_done, at(AC, ("rkv", 12 + c)))
                    mm(bank[b], llw[32 * d:32 * d + 32, c * P:c * P + P],
                       upw[32 * d:32 * d + 32, :], start=True, stop=True
                       ).then_inc(pe_done, did(PE, ("w", d, c)))
            n = 0
            for d in range(2):
                for j in range(4):
                    b = 2 + n % 2
                    if n >= 2:
                        pe.wait_ge(act_done, at(AC, ("ic", (n - 2) // 4, (n - 2) % 4)))
                    else:
                        pe.wait_ge(vec_done, at(VE, ("w0", 0, 1)))
                    mm(bank[b], upw[64 + 32 * d:96 + 32 * d, j * P:j * P + P],
                       llw[64 + 32 * d:96 + 32 * d, :], start=True, stop=True
                       ).then_inc(pe_done, did(PE, ("ic", d, j)))
                    n += 1
            for j in range(4):
                if j >= 2:
                    pe.wait_ge(act_done, at(AC, ("gate", j - 2)))
                else:
                    pe.wait_ge(vec_done, at(VE, ("w0", 1, 2 + j)))
                mm(bank[j % 2], gup[0:96, j * P:j * P + P], llg[0:96, :], start=True, stop=True
                   ).then_inc(pe_done, did(PE, ("gate", j)))
            for j in range(4):
                pe.wait_ge(vec_done, at(VE, ("kk sq", j)))
                if j == 0:
                    pe.wait_ge(act_done, at(AC, ("vt", 3)))
                mm(bank[4 + j], const("head"), kdka[:, j, :], start=True, stop=True
                   ).then_inc(pe_done, did(PE, ("kk", j)))
            for j in range(4):
                pe.wait_ge(vec_done, at(VE, ("rk", j)))
                if j == 0:
                    pe.wait_ge(vec_done, at(VE, ("kk", 3)))
                mm(bank[4 + j], const("head"), kdka[:, j, :], start=True, stop=True
                   ).then_inc(pe_done, did(PE, ("rk", j)))

            def decays(u):
                d, c, pg = UNITS[u]
                if u >= 2:
                    pe.wait_ge(vec_done, at(VE, ("state", u - 2)))
                elif u == 0:
                    pe.wait_ge(vec_done, at(VE, "bonus"))
                    pe.wait_ge(act_done, at(AC, ("gate", 3)))
                    pe.wait_ge(act_done, at(AC, ("sig", 1, 3)))
                for jj in range(2):
                    j = 2 * pg + jj
                    mm(bank[jj][:, 0:258], sig[d][:, c, j * P:j * P + P],
                       const("decay_f" if d == 0 else "decay_b", 258), start=True, stop=True
                       ).then_inc(pe_done, did(PE, ("decays", u, jj)))

            def by_token(u):
                pe.wait_ge(vec_done, at(VE, ("kh", u)))
                for m in range(4):
                    i = nc.tensor.transpose(bank[5][:, m * P:m * P + P],
                                            (bh if m < 2 else kh)[:, m % 2, :], ident)
                i.then_inc(pe_done, did(PE, ("bkt", u)))

            def grams(u, q):
                hp = slice(64 * q, 64 * q + 64)
                if q:
                    pe.wait_ge(act_done, at(AC, ("bkt", u)))
                for jj in range(2):
                    mm(bank[(6, 1)[q]][:, 256 * jj:256 * jj + 256], bh[hp, jj, :],
                       ar[u % 2][hp, jj, :], start=True, stop=True, skip_group_check=True)
                    i = mm(bank[(0, 5)[q]][:, 256 * jj:256 * jj + 256], kh[hp, jj, :],
                           ar[u % 2][hp, jj, :], start=True, stop=True, skip_group_check=True)
                i.then_inc(pe_done, did(PE, ("grams", u, q)))

            def gram_a(u, q):
                hp = slice(64 * q, 64 * q + 64)
                pe.wait_ge(vec_done, at(VE, ("bb", u, q)))
                for jj in range(2):
                    i = mm(bank[(6, 1)[q]][:, P * jj:P * jj + P], ar[u % 2][hp, jj, 0:P],
                           bh[hp, jj, :], start=True, stop=True, skip_group_check=True)
                i.then_inc(pe_done, did(PE, ("A", u, q)))

            def four(name, u, b, lhs, rhs):
                for m in range(4):
                    i = mm(bank[b][:, m * P:m * P + P], lhs[:, m, :], rhs[:, m, :],
                           start=True, stop=True, skip_group_check=True)
                i.then_inc(pe_done, did(PE, (name, u)))

            def squares(u):
                pe.wait_ge(vec_done, at(VE, ("D0", u)))
                four("E2", u, 7, D_[0], E_[0])
                four("D2", u, 2, E_[0], D_[0])

            decays(0)
            by_token(0)
            grams(0, 0)
            grams(0, 1)
            gram_a(0, 0)
            gram_a(0, 1)
            squares(0)
            for u, (d, c, pg) in enumerate(UNITS):
                last = u + 1 == len(UNITS)
                if not last:
                    decays(u + 1)
                pe.wait_ge(act_done, at(AC, ("E2", u)))
                pe.wait_ge(vec_done, at(VE, ("TT1", u)))
                four("T2", u, 3, E_[1], T_[0])
                four("TT2", u, 4, T_[0], E_[1])
                pe.wait_ge(act_done, at(AC, ("D2", u)))
                four("E4", u, 7, D_[1], E_[1])
                four("D4", u, 2, E_[1], D_[1])
                if not last:
                    by_token(u + 1)
                pe.wait_ge(act_done, at(AC, ("E4", u)))
                pe.wait_ge(vec_done, at(VE, ("TT2", u)))
                four("T4", u, 3, E_[0], T_[1])
                four("TT4", u, 4, T_[1], E_[0])
                pe.wait_ge(act_done, at(AC, ("D4", u)))
                four("E8", u, 7, D_[0], E_[0])
                if not last:
                    grams(u + 1, 0)
                pe.wait_ge(act_done, at(AC, ("E8", u)))
                pe.wait_ge(vec_done, at(VE, ("TT4", u)))
                four("T8", u, 3, E_[1], T_[0])
                four("TT8", u, 4, T_[0], E_[1])
                if not last:
                    grams(u + 1, 1)
                cur = 1
                for lv in range(3):
                    pe.wait_ge(vec_done, at(VE, ("bm", u, lv)))
                    pe.wait_ge(vec_done, at(VE, ("TT8", u) if lv == 0 else ("TTm", u, lv - 1)))
                    four(("Z", lv), u, 7, bm, TT_[cur])
                    if not last and lv < 2:
                        gram_a(u + 1, lv)
                    if lv == 2:
                        pe.wait_ge(vec_done, at(VE, ("sin", u)))
                        if not last:
                            pe.wait_ge(vec_done, at(VE, ("kb", u + 1, 0)))
                        for jj in range(2):
                            mm(bank[0][:, P * jj:P * jj + P], ar[u % 2][:, jj, 0:P],
                               sin_[u % 2][:, jj, :], start=True, stop=False,
                               skip_group_check=True)
                            for q in range(2):
                                h = 4 * pg + 2 * jj + q
                                i = mm(bank[0][:, P * jj + HD * q:P * jj + HD * q + HD],
                                       kb[u % 2][:, 2 * q + jj, 0:P],
                                       vt[:, c, h * HD:h * HD + HD],
                                       start=False, stop=True, skip_group_check=True)
                        i.then_inc(pe_done, did(PE, ("x", u)))
                    pe.wait_ge(act_done, at(AC, ("Z", u, lv)))
                    if lv < 2:
                        four(("Tm", lv), u, 3, zt, T_[cur])
                    four(("TTm", lv), u, 4, T_[cur], zt)
                    cur = 1 - cur
                if not last:
                    pe.wait_ge(vec_done, at(VE, ("kb", u + 1, 1)))
                for jj in range(2):
                    mm(bank[5][:, P * jj:P * jj + P], ar[u % 2][:, jj, P:2 * P],
                       sin_[u % 2][:, jj, :], start=(jj == 0), stop=False, skip_group_check=True)
                    for q in range(2):
                        h = 4 * pg + 2 * jj + q
                        mm(bank[5][:, P * jj + HD * q:P * jj + HD * q + HD],
                           kb[u % 2][:, 2 * q + jj, P:2 * P], vt[:, c, h * HD:h * HD + HD],
                           start=False, stop=False, skip_group_check=True)
                pe.wait_ge(act_done, at(AC, ("xs", u)))
                pe.wait_ge(vec_done, at(VE, ("TTm", u, 2)))
                for jj in range(2):
                    for q in range(2):
                        i = mm(bank[1][:, P * jj + HD * q:P * jj + HD * q + HD],
                               TT_[cur][:, 2 * q + jj, :], xs[:, jj, HD * q:HD * q + HD],
                               start=True, stop=True, skip_group_check=True)
                i.then_inc(pe_done, did(PE, ("u", u)))
                if not last:
                    squares(u + 1)
                pe.wait_ge(act_done, at(AC, ("us", u)))
                for jj in range(2):
                    j = 2 * pg + jj
                    mm(bank[6][:, P * jj:P * jj + P], bkt[u % 2][:, jj, :], us[:, jj, :],
                       start=True, stop=False, skip_group_check=True)
                    i = mm(bank[6][:, P * jj:P * jj + P], bkt[u % 2][:, 2 + jj, :],
                           vt[:, c, j * P:j * P + P], start=False, stop=True,
                           skip_group_check=True)
                i.then_inc(pe_done, did(PE, ("s", u)))
                for jj in range(2):
                    for q in range(2):
                        i = mm(bank[5][:, P * jj + HD * q:P * jj + HD * q + HD],
                               bb[u % 2][:, 2 * q + jj, P:2 * P], us[:, jj, HD * q:HD * q + HD],
                               start=False, stop=True, skip_group_check=True)
                i.then_inc(pe_done, did(PE, ("y", u)))
            pe.wait_ge(vec_done, at(VE, "yr norm"))
            for j in range(4):
                turned(("yr turned", j), lambda m: yt[:, m, j * P:j * P + P], 1 + j)
            pe.wait_ge(vec_done, at(VE, "o_rw"))
            product("mix out", first["mix_out"], 4, mix, slice(0, T), [6, 7],
                    lambda j: pe.wait_ge(vec_done, at(VE, ("mix res", j))))

            def sum_up(g):
                if g >= 2:
                    pe.wait_ge(vec_done, at(VE, ("later", g - 2)))
                for n in (n for n, group in enumerate(GROUP_OF) if group == g):
                    pe.wait_ge(vec_done, at(VE, ("chunk", 2 * n + 1)))
                    o = 4 * (n - GROUP_OF.index(g))
                    for t in range(2):
                        for s in range(2):
                            i = mm(bank[(6 if g < FT - 1 else 0) + g % 2][:, o + 2 * t + s:o + 2 * t + s + 1],
                                   sums[n % SUMS][:, s, t * P:t * P + P], const("ones", 1),
                                   start=True, stop=True, skip_group_check=True)
                i.then_inc(pe_done, did(PE, ("summed", g)))

            rms(1, slice(0, T))
            pe.wait_ge(act_done, at(AC, ("norm", 1, KT - 1, 1)))
            for j in range(FT):
                for i_, kind in enumerate(("ffn1", "ffn3")):
                    s = first[kind, j // 2]
                    ws = full(s)
                    if j >= 2 and i_ == 0:
                        pe.wait_ge(vec_done, at(VE, ("gu", j - 2)))
                    t = j % 2
                    for k in range(KT):
                        i = mm(bank[2 * t + i_], ws[:, k, t * P:t * P + P], aT[:, k, :],
                               start=(k == 0), stop=(k == KT - 1))
                    i.then_inc(pe_done, did(PE, (kind, "tile", j), *([("slot", s)] if t else [])))
                    if j and i_ == 0:
                        sum_up(j - 1)
            pe.wait_ge(vec_done, at(VE, ("gu", FT - 1)))
            for n in range(KT):
                s = first["ffn2"] + n
                ws = full(s)
                if n >= 4:
                    pe.wait_ge(vec_done, at(VE, ("ffn res", n - 4)))
                elif n == 2:
                    pe.wait_ge(vec_done, at(VE, ("later", FT - 2)))
                for k in range(FT):
                    i = mm(bank[4 + n % 4], ws[:, k, :], G[:, k, :], start=(k == 0), stop=(k == FT - 1))
                i.then_inc(pe_done, did(PE, ("ffn out", n), ("slot", s)))
                sum_up(FT + n - 1)
            sum_up(FT + KT - 1)
            pe.wait_ge(vec_done, at(VE, ("later", FT + KT - 2)))

            rms(2, slice(0, T))
            pe.wait_ge(act_done, at(AC, ("norm", 2, KT - 1, 1)))
            product("q1", first["qkv"], 4, aT, LAT, [1, 2],
                    lambda j: pe.wait_ge(act_done, at(AC, ("q1", j))))
            pe.wait_ge(act_done, at(AC, ("q1", 7)))
            product("k1", first["qkv"] + 4, 4, aT, slice(0, T), [1, 2],
                    lambda j: pe.wait_ge(act_done, at(AC, ("k1", j))))
            n = 0
            for half in range(4):
                s = first["qkv"] + 8 + half
                ws = full(s)
                for c in range(NCH):
                    if n >= 2:
                        pe.wait_ge(act_done, at(AC, ("v1", n - 2)))
                    for k in range(KT):
                        i = mm(bank[3 + n % 2][:, 0:256], aT[:, k, c * P:c * P + P], ws[:, k, :],
                               start=(k == 0), stop=(k == KT - 1))
                    i.then_inc(pe_done, did(PE, ("v1", n), *([("slot", s)] if c == 3 else [])))
                    n += 1
            pe.wait_ge(act_done, at(AC, ("v1", 15)))
            pe.wait_ge(act_done, at(AC, ("k1", 7)))
            for hd in range(16):
                hp, j = slice(64 * (hd % 2), 64 * (hd % 2) + 64), hd // 2
                for qt in range(2):
                    if hd:
                        pe.wait_ge(act_done, at(AC, ("exp1", hd - 1, qt)))
                    mm(bank[qt], q1[hp, j, qt * P:qt * P + P], k1[hp, j, :], start=True, stop=True
                       ).then_inc(pe_done, did(PE, ("s1", hd, qt)))
                for qt in range(2):
                    pe.wait_ge(vec_done, at(VE, ("p1", hd, qt)))
                    if hd:
                        pe.wait_ge(act_done, at(AC, ("pt1", hd - 1, qt)))
                    turned(("pt1", hd, qt), lambda m: pr[:, qt, m * P:m * P + P], 2 + qt)
                pe.wait_ge(act_done, at(AC, ("pt1", hd, 1)))
                if hd >= 2:
                    pe.wait_ge(vec_done, at(VE, ("o1", hd - 2)))
                for m in range(NCH):
                    i = mm(bank[4 + hd % 2][hp, 0:TL], v1[:, m, hd * HD:hd * HD + HD], pt[:, m, :],
                           start=(m == 0), stop=(m == NCH - 1))
                i.then_inc(pe_done, did(PE, ("o1", hd)))
            pe.wait_ge(vec_done, at(VE, ("o1", 15)))
            product("na out", first["na_out"], 4, o1, slice(0, TL), [6, 7],
                    lambda j: pe.wait_ge(vec_done, at(VE, ("na res", j))))

            rms(3, LAT)
            pe.wait_ge(act_done, at(AC, ("norm", 3, KT - 1, 1)))
            s = first["router"]
            ws = full(s)
            for c in range(2):
                for k in range(KT):
                    i = mm(bank[1][:, 8 * c:8 * c + 8], aT[:, k, TC + c * P:TC + c * P + P],
                           ws[:, k, :], start=(k == 0), stop=(k == KT - 1), skip_group_check=True)
            i.then_inc(pe_done, did(PE, "router", ("slot", s)))
            for n in range(4):
                c, f0 = n // 2, 4 * (n % 2)
                for m in range(4):
                    i = nc.tensor.transpose(bank[2 + n][:, m * P:m * P + P],
                                            aT[:, f0 + m, TC + c * P:TC + c * P + P], ident)
                i.then_inc(pe_done, did(PE, ("atok", n)))
            pe.wait_ge(vec_done, at(VE, "chosen"))
            mm(bank[6][:, 0:8], const("upper"), chosen[:, 0, :], start=True, stop=True,
               skip_group_check=True)
            mm(bank[6][:, 8:16], const("upper"), chosen[:, 1, :], start=True, stop=False,
               skip_group_check=True)
            mm(bank[6][:, 8:16], const("ones"), chosen[:, 0, :], start=False, stop=True,
               skip_group_check=True)
            for c in range(2):
                i = mm(bank[6][:, 16:24], const("ones"), chosen[:, c, :], start=(c == 0),
                       stop=(c == 1), skip_group_check=True)
            per = at(PEM, ("per", "moe"))
            i.then_inc(pe_done, did(PE, "places"))
            counts.count[PEM] = per
            vper, aper = at(VEM, ("per", "moe")), at(ACM, ("per", "moe"))
            pe.wait_ge(vec_done, at(VE, "blocks"))
            pe.wait_ge(act_done, at(AC, ("atok", 3)))
            mm(bank[7][:, 0:8], const("ones"), chosen[:, 0, :], start=True, stop=True
               ).then_inc(pe_moe, per)
            blocks = pe.value_load(block_info[0:1, 12:13], min_val=NE, max_val=NE + 3)
            with pe.Fori(0, blocks) as e:
                pe.wait_ge(ve_moe, e * vper + at(VEM, "P"))
                pe.wait_ge(pe_moe, e * per + now(PEM))
                for f in range(KT):
                    for c in range(2):
                        i = mm(bank[6 + f // 4][:, (f % 4) * P:(f % 4) * P + P],
                               atok[:, c, f * P:f * P + P], pm[:, c, :], start=(c == 0), stop=(c == 1),
                               skip_group_check=True)
                i.then_inc(pe_moe, did(PEM, "gather"))
                pe.wait_ge(ve_moe, e * vper + at(VEM, "Pg"))
                for c in range(2):
                    i = nc.tensor.transpose(bank[4][:, c * P:c * P + P], pgw[:, c, :], ident)
                i.then_inc(pe_moe, did(PEM, "gates turned"))
                pe.wait_ge(ac_moe, e * aper + at(ACM, "gathered"))
                for j in range(FT):
                    t = j % 2
                    if j >= 2:
                        pe.wait_ge(ve_moe, e * vper + at(VEM, ("gu", j - 2)))
                    for i_ in range(2):
                        i0 = 2 * (j // 2) + i_
                        pe.wait_ge(m_full[i0 % RING], e * 80 + 16 * (i0 // RING + 1))
                        ws = cut(ring_t, (i0 % RING) * SLOT, KT, 256)
                        for k in range(KT):
                            i = mm(bank[2 * t + i_][:, 0:P], ws[:, k, t * P:t * P + P],
                                   ac_[:, k, :], start=(k == 0), stop=(k == KT - 1))
                        i.then_inc(pe_moe, did(PEM, ("tile", i_, j), *([("slot", i0)] if t else [])))
                pe.wait_ge(ve_moe, e * vper + at(VEM, ("gu", FT - 1)))
                pe.wait_ge(ac_moe, e * aper + at(ACM, "gates"))
                for q in range(4):
                    for half in range(2):
                        i0 = 22 + 2 * q + half
                        pe.wait_ge(m_full[i0 % RING], e * 80 + 16 * (i0 // RING + 1))
                        ws = cut(ring_t, (i0 % RING) * SLOT, FT // 2, 256)
                        for k in range(FT // 2):
                            i = mm(bank[4 + q // 2][:, 256 * (q % 2):256 * (q % 2) + 256],
                                   Gm[:, 11 * half + k, :], ws[:, k, :], start=(half + k == 0),
                                   stop=(half * k == 10), skip_group_check=True)
                        i.then_inc(pe_moe, did(PEM, ("slot", i0), *([("y", q)] if half else [])))
                for f in range(KT):
                    if f % 4 == 0:
                        pe.wait_ge(ac_moe, e * aper + at(ACM, ("y", f // 4)))
                    i = mm(bank[f // 2][:, 256 * (f % 2):256 * (f % 2) + 256], yp[:, f * P:f * P + P],
                           pgt, start=True, stop=True, skip_group_check=True)
                    if f % 2:
                        i.then_inc(pe_moe, did(PEM, ("back", f // 2)))
            counts.values[PEM, ("per", "moe")] = counts.count[PEM] - per

            pe.wait_ge(vec_done, at(VE, "moe res"))
            rms(4, LAT)

            pe.wait_ge(ctx2_in, 16)
            pe.wait_ge(act_done, at(AC, ("norm", 4, KT - 1, 1)))
            ln(5, slice(0, T))
            pe.wait_ge(act_done, at(AC, ("norm", 5, KT - 1, 1)))
            product("in2", first["in2"], 8, aT, LAT, [2, 3],
                    lambda j: pe.wait_ge(act_done, at(AC, ("in2", j))))
            pe.wait_ge(act_done, at(AC, ("in2", 15)))
            product("k2", first["in2"] + 8, 2, aT, slice(0, T), [2, 3],
                    lambda j: pe.wait_ge(act_done, at(AC, ("k2", j))))
            n = 0
            for half in range(2):
                s = first["in2"] + 10 + half
                ws = full(s)
                for c in range(NCH):
                    if n >= 2:
                        pe.wait_ge(act_done, at(AC, ("v2", n - 2)))
                    for k in range(KT):
                        i = mm(bank[4 + n % 2][:, 0:256], aT[:, k, c * P:c * P + P], ws[:, k, :],
                               start=(k == 0), stop=(k == KT - 1))
                    i.then_inc(pe_done, did(PE, ("v2", n), *([("slot", s)] if c == 3 else [])))
                    n += 1
            pe.wait_ge(act_done, at(AC, ("k2", 3)))
            for n in range(8):
                src = q2[:, n, :] if n < 4 else k2[:, n - 4, LAT]
                if n >= 2:
                    pe.wait_ge(vec_done, at(VE, ("rope", n - 2)))
                mm(bank[6 + n % 2][:, 0:TL], const("turn"), src, start=True, stop=True
                   ).then_inc(pe_done, did(PE, ("turn", n)))
            pe.wait_ge(vec_done, at(VE, ("rope", 7)))
            pe.wait_ge(act_done, at(AC, ("v2", 7)))
            for hd in range(4):
                for qt in range(2):
                    for cp in range(2):
                        hp = slice(64 * cp, 64 * cp + 64)
                        if hd or qt:
                            pe.wait_ge(act_done, at(AC, ("exp2", *((hd, 0) if qt else (hd - 1, 1)), cp)))
                        mm(bank[cp], q2[hp, hd, qt * P:qt * P + P], k2[hp, hd, :], start=True, stop=True
                           ).then_inc(pe_done, did(PE, ("s2", hd, qt, cp)))
                    pe.wait_ge(vec_done, at(VE, ("p2", hd, qt)))
                    if hd:
                        pe.wait_ge(act_done, at(AC, ("pt2", hd - 1, qt)))
                    turned(("pt2", hd, qt), lambda m: pd[:, qt, m * P:m * P + P], 2 + qt)
                pe.wait_ge(act_done, at(AC, ("pt2", hd, 1)))
                if hd >= 2:
                    pe.wait_ge(act_done, at(AC, ("o2", hd - 2)))
                for m in range(NCH):
                    i = mm(bank[4 + hd % 2][:, 0:TL], v2[:, m, hd * P:hd * P + P], pt2[:, m, :],
                           start=(m == 0), stop=(m == NCH - 1))
                i.then_inc(pe_done, did(PE, ("o2", hd)))
            for hd in range(4):
                pe.wait_ge(act_done, at(AC, ("o2 sq", hd)))
                i = mm(bank[6 + hd // 2][:, 256 * (hd % 2):256 * (hd % 2) + 256], const("ones"),
                       mix[:, 4 + hd, CTX], start=True, stop=True, skip_group_check=True)
            i.then_inc(pe_done, did(PE, "subln"))
            pe.wait_ge(vec_done, at(VE, "o_attn"))
            pe.wait_ge(vec_done, at(VE, "o_conv"))

            def outwards(name, s0, st, rhs):
                product(name, s0, 4, rhs, LAT, [2, 3],
                        lambda j: pe.wait_ge(vec_done, at(VE, (name, j))))
                pe.wait_ge(vec_done, at(VE, (name, KT - 1)))
                ln(st, LAT)
                pe.wait_ge(act_done, at(AC, ("norm", st, KT - 1, 1)))

            def mlp(i, st):
                ln(st, LAT)
                pe.wait_ge(act_done, at(AC, ("norm", st, KT - 1, 1)))
                product(("mlp1", i), first["mlp1", i], 16, aT, LAT, [2, 3],
                        lambda j: pe.wait_ge(vec_done, at(VE, ("relu2", i, j))))
                pe.wait_ge(vec_done, at(VE, ("relu2", i, F2T - 1)))
                for n in range(KT):
                    if n >= 2:
                        pe.wait_ge(vec_done, at(VE, (("mlp", i), n - 2)))
                    for half in range(2):
                        s = first["mlp2", i, n, half]
                        ws = full(s)
                        for k in range(16):
                            j = mm(bank[4 + n % 2][:, 0:TL], ws[:, k, :], G2[:, 16 * half + k, :],
                                   start=(half + k == 0), stop=(half * k == 15))
                        j.then_inc(pe_done, did(PE, ("slot", s), *([(("mlp", i), n)] if half else [])))
                pe.wait_ge(vec_done, at(VE, (("mlp", i), KT - 1)))
                ln(st + 1, LAT)
                pe.wait_ge(act_done, at(AC, ("norm", st + 1, KT - 1, 1)))

            outwards("out2", first["out2"], 6, mix)
            mlp(0, 7)

            ln(9, LAT)
            pe.wait_ge(act_done, at(AC, ("norm", 9, KT - 1, 1)))
            n = 0
            for c in range(2):
                for g in range(0, KT, 2):
                    if n >= 2:
                        pe.wait_ge(act_done, at(AC, ("fab", n - 2)))
                    for m in range(2):
                        i = mm(bank[2 + n % 2][:, 256 * m:256 * m + 256],
                               aT[:, g + m, TC + c * P:TC + c * P + P], const("cs128", 256),
                               start=True, stop=True, skip_group_check=True)
                    i.then_inc(pe_done, did(PE, ("fab", n)))
                    n += 1
            pe.wait_ge(act_done, at(AC, ("fab", 7)))
            dft = (cut(const("dft_c", 512), 0, 2, TL), cut(const("dft_s", 512), 0, 2, TL))
            for g in range(KT):
                if g >= 2:
                    pe.wait_ge(act_done, at(AC, ("fm", g - 2)))
                for c in range(2):
                    for part in range(2):
                        i = mm(bank[4 + g % 2][:, 0:TL], fab[:, c, g, part * P:part * P + P],
                               dft[part][:, c, :], start=(c + part == 0), stop=(c + part == 2))
                i.then_inc(pe_done, did(PE, ("fm", g)))
            pe.wait_ge(act_done, at(AC, ("fm", KT - 1)))
            outwards("fourier", first["fourier"], 10, mix)
            mlp(1, 11)

        MODULATED = {0: (0, 0, 0), 1: (0, 0, 3), 2: (0, 1, 0), 3: (0, 1, 3),
                     5: (1, 0, 0), 7: (1, 0, 3), 9: (1, 1, 0), 11: (1, 1, 3)}
        GS = {st: i for i, st in enumerate(MODULATED)}
        AFFINE = {6: 0, 8: 8, 10: 16, 12: 24}

        @block.scalar
        def _(ac):
            act = nc.scalar.activation

            def norm(st, sl, centred):
                n = sl.stop - sl.start
                if centred:
                    ac.wait_ge(vec_done, at(VE, ("centre", st)))
                src = aT if centred else hT
                act(mix[:, :, sl], src[:, :, sl], ACT.Square).then_inc(act_done, did(AC, ("square", st)))
                ac.wait_ge(vec_done, at(VE, ("var", st)))
                act(tmpB[:, 0:n], tmpA[:, 0:n], ACT.Sqrt).then_inc(act_done, did(AC, ("sqrt", st)))
                for k in range(KT):
                    ac.wait_ge(vec_done, at(VE, ("norm", st, k)))
                    for s in range(2):
                        if s == 0 and sl == LAT:
                            continue
                        dst, bias = aT, 0.0
                        if st in MODULATED:
                            scale, bias = gs[:, GS[st], k, s:s + 1], mod(*MODULATED[st], k, s)
                        elif st in AFFINE:
                            dst = hT
                            scale = col("ln_g_2", AFFINE[st] + k)
                            bias = col("ln_b_2", AFFINE[st] + k)
                        else:
                            dst, scale = hT, col("norm_final", k)
                        act(dst[:, k, SEQS[s]], aT[:, k, SEQS[s]], ACT.Identity, bias=bias,
                            scale=scale).then_inc(act_done, did(AC, ("norm", st, k, s)))

            def copy(name, dst, src, scale=1.0):
                act(dst, src, ACT.Copy, scale=scale).then_inc(act_done, did(AC, name))

            ac.wait_ge(loaded, 5 * 16)
            ada_marks = at(PE, ("per", "ada")) // 2
            for i, name in enumerate(("c_ctx", "c", "c_ctx_2", "c_2")):
                act(csil[:, i // 2, :, i % 2], col(name, 0, 8), ACT.Silu
                    ).then_inc(act_done, did(AC, ("cond", i)))

            before = now(AC)
            with ac.Fori(0, 2) as pair:
                for half in range(2):
                    for i in range(3):
                        ac.wait_ge(pe_done, pair * (2 * ada_marks) + (
                            half * ada_marks + at(PE, ("ada", 0, 2 * i + 1))))
                        copy(("ada", half, i), mod_rows[:, i, :], bank[3 * half + i][0:2, :])
            counts.loop(AC, "ada", before, 2)

            ac.wait_ge(pe_done, at(PE, ("end", "ada")))
            norm(0, slice(0, T), False)
            ac.wait_ge(pe_done, at(PE, ("zg", 1)))
            for c in range(NCH):
                act(zg[:, c, :], bank[2 + c], ACT.Silu).then_inc(act_done, did(AC, ("zg", c)))
            ac.wait_ge(vec_done, at(VE, "xpad edges"))
            for j in range(8):
                ac.wait_ge(pe_done, at(PE, ("xbc", j)))
                copy(("xbc", j), xpad[:, j, :, 2:TC + 2],
                     bank[j % 2].rearrange("p (s t) -> p s t", s=2))
            for j in range(8):
                ac.wait_ge(vec_done, at(VE, ("conv", j)))
                act(xb[:, j, :], xb[:, j, :], ACT.Silu).then_inc(act_done, did(AC, ("xb", j)))
            ac.wait_ge(vec_done, at(VE, "dt_raw"))
            flat = small[:, 320:384]
            act(flat, small[:, 0:64], ACT.Abs).then_inc(act_done, did(AC, "abs"))
            ac.wait_ge(act_done, now(AC))
            act(flat, flat, ACT.Exp, scale=-1.0).then_inc(act_done, did(AC, "exp abs"))
            ac.wait_ge(act_done, now(AC))
            act(flat, flat, ACT.Ln, bias=1.0).then_inc(act_done, did(AC, "ln"))
            act(a_neg, row("mb_a_log", 16), ACT.Exp).then_inc(act_done, did(AC, "a_neg"))
            ac.wait_ge(vec_done, at(VE, "cs"))
            act(small[:, 256:320], small[:, 192:256], ACT.Exp).then_inc(act_done, did(AC, "ecs"))
            for u in range(8):
                ac.wait_ge(vec_done, at(VE, ("dec", u)))
                act(mt_t, dec_t, ACT.Exp).then_inc(act_done, did(AC, ("exp dec", u)))
                ac.wait_ge(vec_done, at(VE, ("dcs", u)))
                act(small[:, 400:416], small[:, 400:416], ACT.Exp
                    ).then_inc(act_done, did(AC, ("exp tot", u)))
            ac.wait_ge(vec_done, at(VE, "ss_m"))
            act(small[:, 424:432], small[:, 416:424], ACT.Sqrt).then_inc(act_done, did(AC, "rs_m"))
            for j in range(4):
                ac.wait_ge(pe_done, at(PE, ("ym turned", j)))
                act(mix[:, 4 + j, :], bank[2 + j], ACT.Copy, scale=col("mb_norm_w", j)
                    ).then_inc(act_done, did(AC, ("norm ym", j)))

            ac.wait_ge(vec_done, at(VE, "zpad edges"))
            for j in range(14):
                ac.wait_ge(pe_done, at(PE, ("rkv", j)))
                if j >= 4:
                    ac.wait_ge(vec_done, at(VE, ("shift", j - 4)))
                m = 96 if j == 13 else P
                copy(("rkv", j), zpad[j % 4][0:m, :, 1:TC + 1],
                     bank[j % 2][0:m, :].rearrange("p (s t) -> p s t", s=2))
            for c in range(NCH):
                ac.wait_ge(pe_done, at(PE, ("vt", c)))
                copy(("vt", c), vt[:, c, :], bank[4 + c])
            ac.wait_ge(vec_done, at(VE, ("shift", 12)))
            act(llw[0:64, :], llw[0:64, :], ACT.Tanh).then_inc(act_done, did(AC, "tanh"))
            ac.wait_ge(vec_done, at(VE, ("shift", 13)))
            act(llg[0:96, :], llg[0:96, :], ACT.Sigmoid).then_inc(act_done, did(AC, "lg"))
            for d in range(2):
                for c in range(NCH):
                    ac.wait_ge(vec_done, at(VE, ("w0", d, c)))
                    act(sig[d][:, c, :], sig[d][:, c, :], ACT.Sigmoid
                        ).then_inc(act_done, did(AC, ("sig", d, c)))
            for d in range(2):
                for j in range(4):
                    ac.wait_ge(pe_done, at(PE, ("ic", d, j)))
                    act(ic[d][:, j, :], bank[2 + j % 2], ACT.Sigmoid, bias=col("rw_a0", 4 * d + j)
                        ).then_inc(act_done, did(AC, ("ic", d, j)))
            for j in range(4):
                ac.wait_ge(pe_done, at(PE, ("gate", j)))
                copy(("gate", j), gate[:, j, :], bank[j % 2])
            for j in range(4):
                ac.wait_ge(vec_done, at(VE, ("kk var", j)))
                act(tmpB, tmpA, ACT.Sqrt).then_inc(act_done, did(AC, ("kk root", j)))
            def decays(u):
                for jj in range(2):
                    ac.wait_ge(pe_done, at(PE, ("decays", u, jj)))
                    act(ex[u % 2][:, jj, :], bank[jj][:, 0:258], ACT.Exp
                        ).then_inc(act_done, did(AC, ("ex", u, jj)))
                    act(ei[:, jj, :], bank[jj][:, 0:P], ACT.Exp, scale=-1.0
                        ).then_inc(act_done, did(AC, ("ei", u, jj)))

            def out_of(name, u, b, dst):
                ac.wait_ge(pe_done, at(PE, (name, u)))
                copy((name, u), dst, cut(bank[b], 0, 4, P))

            decays(0)
            out_of("bkt", 0, 5, bkt[0])
            out_of("E2", 0, 7, E_[1])
            out_of("D2", 0, 2, D_[1])
            for u in range(len(UNITS)):
                last = u + 1 == len(UNITS)
                if not last:
                    decays(u + 1)
                out_of("E4", u, 7, E_[0])
                out_of("D4", u, 2, D_[0])
                if not last:
                    out_of("bkt", u + 1, 5, bkt[(u + 1) % 2])
                out_of("E8", u, 7, E_[1])
                for lv in range(3):
                    ac.wait_ge(pe_done, at(PE, (("Z", lv), u)))
                    copy(("Z", u, lv), zt, cut(bank[7], 0, 4, P))
                ac.wait_ge(pe_done, at(PE, ("x", u)))
                copy(("xs", u), xs, cut(bank[0], 0, 2, P))
                ac.wait_ge(pe_done, at(PE, ("u", u)))
                copy(("us", u), us, cut(bank[1], 0, 2, P))
                if not last:
                    out_of("E2", u + 1, 7, E_[1])
                    out_of("D2", u + 1, 2, D_[1])
            ac.wait_ge(vec_done, at(VE, "yr var"))
            act(small[:, 96:128], small[:, 64:96], ACT.Sqrt).then_inc(act_done, did(AC, "yr root"))
            for j in range(4):
                ac.wait_ge(pe_done, at(PE, ("yr turned", j)))
                act(mix[:, j, :], bank[1 + j], ACT.Identity, scale=col("rw_gn_w", j),
                    bias=col("rw_gn_b", j)).then_inc(act_done, did(AC, ("gn", j)))

            ac.wait_ge(vec_done, at(VE, ("mix res", KT - 1)))
            norm(1, slice(0, T), False)
            for j in range(FT):
                ac.wait_ge(pe_done, at(PE, ("ffn1", "tile", j)))
                if j >= 2:
                    ac.wait_ge(vec_done, at(VE, ("gu", j - 2)))
                act(sg[j % 2], bank[2 * (j % 2)], ACT.Silu).then_inc(act_done, did(AC, ("sg", j)))

            ac.wait_ge(pe_done, at(PE, ("summed", FT + KT - 1)))
            ac.wait_ge(vec_done, at(VE, ("ffn res", KT - 1)))
            norm(2, slice(0, T), False)
            for j in range(KT):
                ac.wait_ge(pe_done, at(PE, ("q1", j)))
                copy(("q1", j), q1[:, j, :], bank[1 + j % 2][:, 0:TL], HD ** -0.5)
            for j in range(KT):
                ac.wait_ge(pe_done, at(PE, ("k1", j)))
                copy(("k1", j), k1[:, j, :], bank[1 + j % 2])
            for n in range(16):
                ac.wait_ge(pe_done, at(PE, ("v1", n)))
                copy(("v1", n), v1[:, n % 4, 256 * (n // 4):256 * (n // 4) + 256],
                     bank[3 + n % 2][:, 0:256])
            for hd in range(16):
                for qt in range(2):
                    ac.wait_ge(vec_done, at(VE, ("m1", hd, qt)))
                    act(pr[:, qt, :], pr[:, qt, :], ACT.Exp, bias=stat[:, qt:qt + 1],
                        accum_out=stat[:, 2 + qt:3 + qt]).then_inc(act_done, did(AC, ("exp1", hd, qt)))
                for qt in range(2):
                    ac.wait_ge(pe_done, at(PE, ("pt1", hd, qt)))
                    if hd:
                        ac.wait_ge(pe_done, at(PE, ("o1", hd - 1)))
                    copy(("pt1", hd, qt), pt[:, :, qt * P:qt * P + P],
                         bank[2 + qt].rearrange("p (a b) -> p a b", a=4))

            ac.wait_ge(vec_done, at(VE, ("na res", KT - 1)))
            norm(3, LAT, False)
            ac.wait_ge(vec_done, at(VE, "lg max"))
            act(small[:, 32:48], small[:, 32:48], ACT.Exp).then_inc(act_done, did(AC, "ge"))
            for n in range(4):
                ac.wait_ge(pe_done, at(PE, ("atok", n)))
                copy(("atok", n), atok[:, n // 2, 512 * (n % 2):512 * (n % 2) + 512], bank[2 + n])
            per = at(ACM, ("per", "moe"))
            pper, vper = at(PEM, ("per", "moe")), at(VEM, ("per", "moe"))
            counts.count[ACM] = per
            ac.wait_ge(vec_done, at(VE, "blocks"))
            act(small[:, 500:501], small[:, 444:445], ACT.Copy).then_inc(ac_moe, per)
            blocks = ac.value_load(block_info[0:1, 12:13], min_val=NE, max_val=NE + 3)
            with ac.Fori(0, blocks) as e:
                ac.wait_ge(pe_moe, e * pper + at(PEM, "gather"))
                for h in range(2):
                    act(ac_[:, 4 * h:4 * h + 4, :], cut(bank[6 + h], 0, 4, P), ACT.Copy
                        ).then_inc(ac_moe, did(ACM, "gathered" if h else "gathered 0"))
                ac.wait_ge(pe_moe, e * pper + at(PEM, "gates turned"))
                act(pgt, bank[4][:, 0:2 * P], ACT.Copy).then_inc(ac_moe, did(ACM, "gates"))
                for j in range(FT):
                    ac.wait_ge(pe_moe, e * pper + at(PEM, ("tile", 0, j)))
                    if j >= 2:
                        ac.wait_ge(ve_moe, e * vper + at(VEM, ("gu", j - 2)))
                    act(sgm[j % 2], bank[2 * (j % 2)][:, 0:P], ACT.Silu
                        ).then_inc(ac_moe, did(ACM, ("sg", j)))
                for h in range(2):
                    ac.wait_ge(pe_moe, e * pper + at(PEM, ("y", 2 * h + 1)))
                    act(yp[:, 512 * h:512 * h + 512], bank[4 + h], ACT.Copy
                        ).then_inc(ac_moe, did(ACM, ("y", h)))
            counts.values[ACM, ("per", "moe")] = counts.count[ACM] - per
            ac.wait_ge(vec_done, at(VE, "moe res"))
            norm(4, LAT, False)

            norm(5, slice(0, T), True)
            for j in range(16):
                ac.wait_ge(pe_done, at(PE, ("in2", j)))
                src = bank[2 + j % 2][:, 0:TL]
                if j < 8:
                    copy(("in2", j), (gb if j < 4 else gc)[:, j % 4, :], src)
                elif j < 12:
                    copy(("in2", j), vp[:, j - 8, 1:TL + 1], src)
                else:
                    copy(("in2", j), q2[:, j - 12, :], src, HD ** -0.5)
            for j in range(4):
                ac.wait_ge(pe_done, at(PE, ("k2", j)))
                copy(("k2", j), k2[:, j, :], bank[2 + j % 2])
            for n in range(8):
                ac.wait_ge(pe_done, at(PE, ("v2", n)))
                copy(("v2", n), v2[:, n % 4, 256 * (n // 4):256 * (n // 4) + 256],
                     bank[4 + n % 2][:, 0:256])
            ac.wait_ge(vec_done, at(VE, "lam sums"))
            act(lamv[:, 2:4], lamv[:, 0:2], ACT.Exp).then_inc(act_done, did(AC, "lam"))
            for hd in range(4):
                for qt in range(2):
                    for cp in range(2):
                        ac.wait_ge(vec_done, at(VE, ("m2", hd, qt, cp)))
                        act(p2[:, cp, :], bank[cp], ACT.Exp, bias=small[:, 150 + cp:151 + cp],
                            accum_out=small[:, 152 + cp:153 + cp]
                            ).then_inc(act_done, did(AC, ("exp2", hd, qt, cp)))
                for qt in range(2):
                    ac.wait_ge(pe_done, at(PE, ("pt2", hd, qt)))
                    if hd:
                        ac.wait_ge(pe_done, at(PE, ("o2", hd - 1)))
                    copy(("pt2", hd, qt), pt2[:, :, qt * P:qt * P + P],
                         bank[2 + qt].rearrange("p (a b) -> p a b", a=4))
                ac.wait_ge(pe_done, at(PE, ("o2", hd)))
                copy(("o2", hd), o2[:, hd, :], bank[4 + hd % 2][:, 0:TL])
                act(mix[:, 4 + hd, CTX], bank[4 + hd % 2][:, 0:TL], ACT.Square
                    ).then_inc(act_done, did(AC, ("o2 sq", hd)))
            for i, t in enumerate((tmpA, tmpB)):
                ac.wait_ge(vec_done, at(VE, ("subln", i)))
                act(t, t, ACT.Sqrt).then_inc(act_done, did(AC, ("subln", i)))

            norm(6, LAT, True)
            norm(7, LAT, True)
            norm(8, LAT, True)
            norm(9, LAT, True)
            for n in range(8):
                ac.wait_ge(pe_done, at(PE, ("fab", n)))
                copy(("fab", n), fab[:, n // 4, 2 * (n % 4):2 * (n % 4) + 2, :],
                     bank[2 + n % 2].rearrange("p (a b) -> p a b", a=2))
            for g in range(KT):
                ac.wait_ge(pe_done, at(PE, ("fm", g)))
                copy(("fm", g), mix[:, g, LAT], bank[4 + g % 2][:, 0:TL])
            norm(10, LAT, True)
            norm(11, LAT, True)
            norm(12, LAT, True)

        @block.vector
        def _(ve):
            V = nc.vector

            def wide(ap, *shape):
                return ap.broadcast_to([P, *shape])

            def norm(st, sl, centred):
                n = sl.stop - sl.start
                eps = LN_EPS if centred else RMS_EPS
                if centred:
                    ve.wait_ge(pe_done, at(PE, ("norm mean", st)))
                    V.tensor_tensor(aT[:, :, sl], hT[:, :, sl], wide(bank[1][:, None, 0:n], KT, n),
                                    ALU.subtract).then_inc(vec_done, did(VE, ("centre", st)))
                ve.wait_ge(pe_done, at(PE, ("norm sum", st)))
                V.tensor_scalar(tmpA[:, 0:n], bank[0][:, 0:n], eps, None, ALU.add
                                ).then_inc(vec_done, did(VE, ("var", st)))
                ve.wait_ge(act_done, at(AC, ("sqrt", st)))
                V.reciprocal(tmpA[:, 0:n], tmpB[:, 0:n]).then_inc(vec_done, did(VE, ("rstd", st)))
                ve.wait_ge(vec_done, now(VE))
                src = aT if centred else hT
                for k in range(KT):
                    V.tensor_tensor(aT[:, k, sl], src[:, k, sl], tmpA[:, 0:n], ALU.mult
                                    ).then_inc(vec_done, did(VE, ("norm", st, k)))

            def op(name, ins):
                ins.then_inc(vec_done, did(VE, name))
                ve.wait_ge(vec_done, now(VE))

            def residual(name, j, src, gate, seqs):
                for s in seqs:
                    part = src[:, SEQS[s]] if len(seqs) == 2 else src
                    V.scalar_tensor_tensor(hT[:, j, SEQS[s]], part, mod(*gate, j, s), hT[:, j, SEQS[s]],
                                           ALU.mult, ALU.add
                                           ).then_inc(vec_done, did(VE, (name, j) if s else (name, j, "ctx")))

            for h in range(2):
                V.memset(xpad[:, 4 * h:4 * h + 4, :, :], 0.0
                         ).then_inc(vec_done, did(VE, "xpad edges" if h else "xpad half"))
            ve.wait_ge(loaded, 5 * 16)
            ada_marks = at(PE, ("per", "ada")) // 2
            before = now(VE)
            with ve.Fori(0, 2) as pair:
                for half in range(2):
                    ve.wait_ge(pe_done, pair * (2 * ada_marks) + (half + 1) * ada_marks)
                    m0 = pair * 24 + 12 * half
                    b0 = pair * 24 + (COL["b_ada"] + 12 * half)
                    V.tensor_tensor(mods[:, bass.ds(m0, 12), :], cut(bank[6 + half], 0, 12, 2),
                                    wide(cols[:, bass.ds(b0, 12)][:, :, None], 12, 2), ALU.add
                                    ).then_inc(vec_done, did(VE, ("mods", half)))
            counts.loop(VE, "mods", before, 2)

            def scales(stages):
                ve.wait_ge(vec_done, now(VE))
                for st in stages:
                    b, layer, piece = MODULATED[st]
                    at0 = 96 * b + 48 * layer + 8 * (piece + 1)
                    g = GS[st]
                    if b:
                        V.tensor_scalar(gs[:, g, :, :], mods[:, at0:at0 + 8, :], 1.0, None, ALU.add
                                        ).then_inc(vec_done, did(VE, ("gs", g)))
                    else:
                        w_ = col("norm_ffn" if piece else "norm_mix", 8 * layer, 8)
                        V.scalar_tensor_tensor(gs[:, g, :, :], mods[:, at0:at0 + 8, :], 1.0,
                                               wide(w_[:, :, None], 8, 2), ALU.add, ALU.mult
                                               ).then_inc(vec_done, did(VE, ("gs", g)))

            def products_by_partition(g):
                for n in (n for n, group in enumerate(GROUP_OF) if group == g):
                    if n >= SUMS:
                        ve.wait_ge(pe_done, at(PE, ("summed", GROUP_OF[n - SUMS])))
                    b = LATER[n // ADA][0]
                    for k in range(KT):
                        i, x = 2 * n + k // 4, chunk[(2 * n + k // 4) % CHUNKS][:, k % 4, :]
                        if k % 4 == 0:
                            ve.wait_ge(chunk_full[i % CHUNKS], 16 * (i // CHUNKS + 1))
                        for s in range(2):
                            dst, cond = sums[n % SUMS][:, s, :], csil[:, b, k, s:s + 1]
                            if k == 0:
                                ins = V.tensor_scalar(dst, x, cond, None, ALU.mult)
                            else:
                                ve.wait_ge(vec_done, now(VE) - 1)
                                ins = V.scalar_tensor_tensor(dst, x, cond, dst, ALU.mult, ALU.add)
                            ins.then_inc(vec_done, did(VE, ("chunk", i) if k % 4 == 3 and s
                                                       else ("later part", n, k, s)))

            def columns_out(g):
                n, m = GROUP_OF.index(g), GROUPS[g]
                ve.wait_ge(pe_done, at(PE, ("summed", g)))
                pieces = {}
                for n in range(n, n + m):
                    pieces.setdefault(n // ADA, []).append(n)
                for of, ns in pieces.items():
                    b, layer = LATER[of]
                    q = 48 * layer + 2 * (ns[0] % ADA)
                    src = cut(bank[(6 if g < FT - 1 else 0) + g % 2],
                              4 * (ns[0] - GROUP_OF.index(g)), 2 * len(ns), 2)
                    V.tensor_tensor(mods[:, 96 * b + q:96 * b + q + 2 * len(ns), :], src,
                                    wide(col(("b_ada", "ada_b_2")[b], q, 2 * len(ns))[:, :, None],
                                         2 * len(ns), 2), ALU.add
                                    ).then_inc(vec_done, did(VE, ("later", g) if ns[-1] == n
                                                             else ("later part", g)))

            scales([0, 1])

            norm(0, slice(0, T), False)
            ve.wait_ge(pe_done, at(PE, "dt"))
            V.tensor_tensor(dt_raw.rearrange("p c d h -> p c (d h)"), cut(bank[6], 0, NCH, 16),
                            wide(row("mb_dt_bias", 16)[:, None, :], NCH, 16), ALU.add
                            ).then_inc(vec_done, did(VE, "dt_raw"))
            for j in range(8):
                ve.wait_ge(act_done, at(AC, ("xbc", j)))
                dst = xb[:, j, :].rearrange("p (s t) -> p s t", s=2)
                op(("conv 0", j), V.tensor_scalar(dst, xpad[:, j, :, 0:TC], col("mb_conv_w", j),
                                                  col("mb_conv_b", j), ALU.mult, ALU.add))
                for tap in range(1, 5):
                    name = ("conv", j) if tap == 4 else ("conv part", j, tap)
                    op(name, V.scalar_tensor_tensor(dst, xpad[:, j, :, tap:tap + TC],
                                                    col("mb_conv_w", 8 * tap + j), dst,
                                                    ALU.mult, ALU.add))
            ve.wait_ge(act_done, at(AC, "a_neg"))
            op("dtv", V.scalar_tensor_tensor(small[:, 64:128], small[:, 0:64], 0.0, small[:, 320:384],
                                             ALU.max, ALU.add))
            op("a_tok", V.scalar_tensor_tensor(
                a_tok.rearrange("p c d h -> p c (d h)"), dtv.rearrange("p c d h -> p c (d h)"), -1.0,
                wide(a_neg[:, None, :], NCH, 16), ALU.mult, ALU.mult))
            for c in range(NCH):
                ve.wait_ge(pe_done, at(PE, ("xt", c)))
                V.tensor_copy(xt[:, c, :], bank[2 + c % 2]).then_inc(vec_done, did(VE, ("xt", c)))
                ve.wait_ge(pe_done, at(PE, ("bt", c)))
                V.tensor_copy(bt[:, c, :], bank[4 + c % 2][:, 0:256]).then_inc(vec_done, did(VE, ("bt", c)))
            ve.wait_ge(pe_done, at(PE, "cs"))
            V.tensor_copy(small[:, 192:256], bank[6][:, 0:64]).then_inc(vec_done, did(VE, "cs"))
            ve.wait_ge(pe_done, at(PE, "gram"))
            for d in range(2):
                for g in range(2):
                    mask = const("upper_in" if d == 0 else "lower_in")
                    V.tensor_tensor(gram[:, d, g, :, :], cut(bank[g], 0, NCH, P),
                                    wide(mask[:, None, :], NCH, P), ALU.mult
                                    ).then_inc(vec_done, did(VE, ("gram", d) if g else ("gram 0", d)))
            ve.wait_ge(vec_done, now(VE))
            u = 0
            for d in range(2):
                for c in range(NCH):
                    V.tensor_tensor(cut(xdt[:, c, :], 0, 8, HD), cut(xt[:, c, :], 0, 8, HD),
                                    wide(dtv[:, c, d, :][:, :, None], 8, HD), ALU.mult
                                    ).then_inc(vec_done, did(VE, ("xdt", d, c)))
                for step in range(NCH):
                    c = step if d == 0 else step ^ 1
                    last = P - 1 if d == 0 else 0
                    ve.wait_ge(pe_done, at(PE, ("decay", u)))
                    ve.wait_ge(vec_done, now(VE))
                    for h in range(8):
                        V.tensor_scalar(dec[:, h, :], bank[h // 4][:, (h % 4) * P:(h % 4) * P + P],
                                        cs[:, c, d, h:h + 1], 0.0, ALU.subtract, ALU.min
                                        ).then_inc(vec_done, did(VE, ("dec", u) if h == 7 else ("dec", u, h)))
                    for half in range(2):
                        tot = cut(bank[half], 0, 4, P)[:, :, last]
                        V.tensor_tensor(dcs[:, 4 * half:4 * half + 4], tot,
                                        cs[:, c, d, 4 * half:4 * half + 4], ALU.subtract
                                        ).then_inc(vec_done, did(VE, ("dcs part", u, half)))
                        V.tensor_copy(etot[:, 4 * half:4 * half + 4], tot
                                      ).then_inc(vec_done, did(VE, ("dcs", u) if half else ("etot", u)))
                    ve.wait_ge(act_done, at(AC, ("exp dec", u)))
                    for g in range(2):
                        V.tensor_tensor(mt[:, 4 * g:4 * g + 4, :], mt[:, 4 * g:4 * g + 4, :],
                                        wide(gram[:, d, g, c, :][:, None, :], 4, P), ALU.mult
                                        ).then_inc(vec_done, did(VE, ("mt", u) if g else ("mt 0", u)))
                    ve.wait_ge(act_done, at(AC, ("exp tot", u)))
                    V.tensor_tensor(cut(xd2, 0, 8, HD), cut(xdt[:, c, :], 0, 8, HD),
                                    wide(dcs[:, :, None], 8, HD), ALU.mult
                                    ).then_inc(vec_done, did(VE, ("xd2", u)))
                    ve.wait_ge(pe_done, at(PE, ("y diag", u)))
                    if d == 0:
                        op(("y", u), V.tensor_copy(ym[:, c, :], bank[2]))
                    else:
                        op(("y", u), V.tensor_tensor(ym[:, c, :], ym[:, c, :], bank[2], ALU.add))
                    if step:
                        if step == 1 and d == 0:
                            ve.wait_ge(act_done, at(AC, "ecs"))
                        op(("off", u), V.tensor_tensor(
                            cut(dec_t, 0, 8, HD), cut(bank[3], 0, 8, HD),
                            wide(ecs[:, c, d, :][:, :, None], 8, HD), ALU.mult))
                        op(("y2", u), V.tensor_tensor(ym[:, c, :], ym[:, c, :], dec_t[:, 0:512], ALU.add))
                        op(("st", u), V.tensor_tensor(cut(st_m, 0, 8, HD), cut(st_m, 0, 8, HD),
                                                      wide(etot[:, :, None], 8, HD), ALU.mult))
                        ve.wait_ge(pe_done, at(PE, ("states", u)))
                        op(("unit", u), V.tensor_tensor(st_m, st_m, bank[4], ALU.add))
                    else:
                        ve.wait_ge(pe_done, at(PE, ("states", u)))
                        op(("unit", u), V.tensor_copy(st_m, bank[4]))
                    u += 1
            tmp = cut(mix_t, 0, NCH, RW)
            for c in range(NCH):
                op(("dx", c), V.tensor_tensor(cut(tmp[:, c, :], 0, 8, HD), cut(xt[:, c, :], 0, 8, HD),
                                              wide(row("mb_d", 8)[:, :, None], 8, HD), ALU.mult))
            op("ym 1", V.tensor_tensor(ym, ym, tmp, ALU.add))
            op("ym 2", V.tensor_tensor(ym, ym, zg, ALU.mult))
            op("ym sq", V.tensor_tensor(tmp, ym, ym, ALU.mult))
            op("ym ss", V.tensor_reduce(small[:, 416:424], cut(mix_t, 0, 8, 256), AX.X, ALU.add))
            op("ss_m", V.tensor_scalar(small[:, 416:424], small[:, 416:424], 1.0 / 256, RMS_EPS,
                                       ALU.mult, ALU.add))
            ve.wait_ge(act_done, at(AC, "rs_m"))
            op("rs_m", V.reciprocal(small[:, 416:424], small[:, 424:432]))
            flat = ym.rearrange("p c (g n) -> p (c g) n", g=2)
            V.tensor_tensor(flat, flat, wide(small[:, 416:424][:, :, None], 8, 256), ALU.mult
                            ).then_inc(vec_done, did(VE, "ym end"))

            ve.wait_ge(pe_done, at(PE, ("ym turned", 3)))
            for i in range(4):
                V.memset(zpad[i], 0.0).then_inc(vec_done, did(VE, "zpad edges" if i == 3 else ("zpad", i)))
            op("mu sum", V.tensor_tensor(mu0, col("mu_prev", 0, 13), col("mu_next", 0, 13), ALU.add))
            op("mu0", V.tensor_scalar(mu0, mu0, -1.0, 1.0, ALU.mult, ALU.add))
            op("1 - k_a", V.tensor_scalar(small[:, 16:20], col("rw_k_a", 0, 4), -1.0, 1.0, ALU.mult, ALU.add))
            for j in range(14):
                m = 96 if j == 13 else P
                ve.wait_ge(act_done, at(AC, ("rkv", j)))
                if j == 13:
                    ve.wait_ge(up_in, 5 * 16)
                    op("mug sum", V.tensor_tensor(mu0g[0:96, :], mug[0:96, 0:1], mug[0:96, 1:2], ALU.add))
                    op("mu0g", V.tensor_scalar(mu0g[0:96, :], mu0g[0:96, :], -1.0, 1.0, ALU.mult, ALU.add))
                    dst, own, prev, next_ = llg[0:96, :], mu0g, mug[:, 0:1], mug[:, 1:2]
                else:
                    dst = llw if j == 12 else (r_, k_, v_)[j // 4][:, j % 4, :]
                    own, prev, next_ = mu0[:, j:j + 1], col("mu_prev", j), col("mu_next", j)
                dst = dst.rearrange("p (s t) -> p s t", s=2)
                z = zpad[j % 4][0:m, :, :]
                op(("shift 0", j), V.tensor_scalar(dst, z[:, :, 1:TC + 1], own[0:m, :], None, ALU.mult))
                op(("shift 1", j), V.scalar_tensor_tensor(dst, z[:, :, 0:TC], prev[0:m, :], dst,
                                                          ALU.mult, ALU.add))
                op(("shift", j), V.scalar_tensor_tensor(dst, z[:, :, 2:TC + 2], next_[0:m, :], dst,
                                                        ALU.mult, ALU.add))
            for d in range(2):
                for c in range(NCH):
                    ve.wait_ge(pe_done, at(PE, ("w", d, c)))
                    V.tensor_tensor(sig[d][:, c, :], bank[c % 2], w0row[:, RW * d:RW * d + RW], ALU.add
                                    ).then_inc(vec_done, did(VE, ("w0", d, c)))
            for j in range(4):
                op(("kk 0", j), V.tensor_scalar(kk[:, j, :], k_[:, j, :], col("rw_k_k", j), None, ALU.mult))
                op(("kk sq", j), V.tensor_tensor(kdka[:, j, :], kk[:, j, :], kk[:, j, :], ALU.mult))
            for j in range(4):
                ve.wait_ge(pe_done, at(PE, ("kk", j)))
                op(("kk var", j), V.tensor_scalar(tmpA, bank[4 + j], 1e-24, None, ALU.max))
                ve.wait_ge(act_done, at(AC, ("kk root", j)))
                op(("kk rstd", j), V.reciprocal(tmpA, tmpB))
                op(("kk", j), V.tensor_tensor(kk[:, j, :], kk[:, j, :], tmpA, ALU.mult))
            for d in range(2):
                for j in range(4):
                    ve.wait_ge(act_done, at(AC, ("ic", d, j)))
                    op(("kd 0", d, j), V.tensor_scalar(kd[d][:, j, :], ic[d][:, j, :], col("rw_k_a", j),
                                                       small[:, 16 + j:17 + j], ALU.mult, ALU.add))
                    op(("kd", d, j), V.tensor_tensor(kd[d][:, j, :], kd[d][:, j, :], k_[:, j, :], ALU.mult))
                    op(("b", d, j), V.tensor_tensor(ic[d][:, j, :], ic[d][:, j, :], kk[:, j, :], ALU.mult))
            for j in range(4):
                op(("rk 0", j), V.tensor_scalar(kdka[:, j, :], kd[0][:, j, :], col("rw_r_k", j), None, ALU.mult))
                op(("rk 1", j), V.scalar_tensor_tensor(kdka[:, j, :], kd[1][:, j, :], col("rw_r_k", 4 + j),
                                                       kdka[:, j, :], ALU.mult, ALU.add))
                op(("rk", j), V.tensor_tensor(kdka[:, j, :], kdka[:, j, :], r_[:, j, :], ALU.mult))
            for j in range(4):
                ve.wait_ge(pe_done, at(PE, ("rk", j)))
                V.tensor_tensor(bonus[:, j, :], bank[4 + j], v_[:, j, :], ALU.mult
                                ).then_inc(vec_done, did(VE, "bonus" if j == 3 else ("bonus", j)))
            op("state 0", V.memset(state, 0.0))
            def decayed(u):
                d, c, pg = UNITS[u]
                js, cs_, e = slice(2 * pg, 2 * pg + 2), slice(c * P, c * P + P), ex[u % 2]
                ve.wait_ge(act_done, at(AC, ("ei", u, 1)))
                V.scalar_tensor_tensor(ar[u % 2][:, :, 0:P], kk[:, js, cs_], -1.0, e[:, :, P:2 * P],
                                       ALU.mult, ALU.mult).then_inc(vec_done, did(VE, ("ar a", u)))
                V.tensor_tensor(ar[u % 2][:, :, P:2 * P], r_[:, js, cs_], e[:, :, 0:P], ALU.mult
                                ).then_inc(vec_done, did(VE, ("ar r", u)))
                V.tensor_tensor(bh, ic[d][:, js, cs_], ei, ALU.mult
                                ).then_inc(vec_done, did(VE, ("bh", u)))
                V.tensor_tensor(kh, kd[d][:, js, cs_], ei, ALU.mult
                                ).then_inc(vec_done, did(VE, ("kh", u)))
                for jj in range(2):
                    V.tensor_scalar(sin_[u % 2][:, jj, :], state[:, 4 * d + 2 * pg + jj, :],
                                    e[:, jj, 256:257], None, ALU.mult
                                    ).then_inc(vec_done, did(VE, ("sin", u) if jj else ("sin 0", u)))

            def masked(u, q):
                m_t = const("lower" if UNITS[u][0] else "upper", 256)
                ve.wait_ge(pe_done, at(PE, ("grams", u, q)))
                for name, b, dst in (("bb", (6, 1)[q], bb), ("kb", (0, 5)[q], kb)):
                    V.tensor_tensor(dst[u % 2][:, 2 * q:2 * q + 2, :], cut(bank[b], 0, 2, 256),
                                    wide(m_t[:, None, :], 2, 256), ALU.mult
                                    ).then_inc(vec_done, did(VE, (name, u, q)))

            def masked_a(u, q):
                m_a = const("upper" if UNITS[u][0] else "lower")
                ve.wait_ge(pe_done, at(PE, ("A", u, q)))
                V.tensor_tensor(dm[u % 2][:, 2 * q:2 * q + 2, :], cut(bank[(6, 1)[q]], 0, 2, P),
                                wide(m_a[:, None, :], 2, P), ALU.mult
                                ).then_inc(vec_done, did(VE, ("dm", u, q)))

            diag = wide(const("diag16")[:, None, :], 4, P)
            eye = wide(ident[:, None, :], 4, P)

            def diagonal(u):
                ve.wait_ge(vec_done, now(VE))
                if u:
                    ve.wait_ge(pe_done, at(PE, (("TTm", 1), u - 1)))
                V.tensor_tensor(E_[0], bb[u % 2][:, :, 0:P], diag, ALU.mult
                                ).then_inc(vec_done, did(VE, ("E0", u)))
                op(("D0", u), V.tensor_tensor(D_[0], dm[u % 2], diag, ALU.mult))
                V.tensor_tensor(T_[0], D_[0], eye, ALU.add).then_inc(vec_done, did(VE, ("T1", u)))

            def first_tt(u):
                if u:
                    ve.wait_ge(pe_done, at(PE, ("u", u - 1)))
                op(("TT1", u), V.tensor_tensor(TT_[0], E_[0], eye, ALU.add))

            def add(name, src, dst, b):
                V.tensor_tensor(dst, src, cut(bank[b], 0, 4, P), ALU.add
                                ).then_inc(vec_done, did(VE, name))

            decayed(0)
            masked(0, 0)
            masked(0, 1)
            masked_a(0, 0)
            masked_a(0, 1)
            diagonal(0)
            first_tt(0)
            for u, (d, c, pg) in enumerate(UNITS):
                last = u + 1 == len(UNITS)
                for power, i in ((2, 0), (4, 1), (8, 0)):
                    ve.wait_ge(pe_done, at(PE, (f"T{power}", u)))
                    add((f"T{power}", u), T_[i], T_[1 - i], 3)
                    ve.wait_ge(pe_done, at(PE, (f"TT{power}", u)))
                    add((f"TT{power}", u), TT_[i], TT_[1 - i], 4)
                    if power == 2 and not last:
                        decayed(u + 1)
                    if power == 4:
                        if not last:
                            masked(u + 1, 0)
                        off = wide(const("off32")[:, None, :], 4, P)
                        V.tensor_tensor(bm, dm[u % 2], off, ALU.mult
                                        ).then_inc(vec_done, did(VE, ("bm", u, 0)))
                    ve.wait_ge(vec_done, now(VE))
                cur = 1
                for lv in range(3):
                    if lv == 0 and not last:
                        masked(u + 1, 1)
                    if lv:
                        if not last:
                            masked_a(u + 1, lv - 1)
                            if lv == 2:
                                diagonal(u + 1)
                    if lv < 2:
                        ve.wait_ge(pe_done, at(PE, (("Z", lv), u)))
                        off = wide(const(("off64", "off128")[lv])[:, None, :], 4, P)
                        V.tensor_tensor(bm, dm[u % 2], off, ALU.mult
                                        ).then_inc(vec_done, did(VE, ("bm", u, lv + 1)))
                        ve.wait_ge(pe_done, at(PE, (("Tm", lv), u)))
                        add(("Tm", u, lv), T_[cur], T_[1 - cur], 3)
                    ve.wait_ge(pe_done, at(PE, (("TTm", lv), u)))
                    add(("TTm", u, lv), TT_[cur], TT_[1 - cur], 4)
                    ve.wait_ge(vec_done, now(VE))
                    cur = 1 - cur
                if not last:
                    first_tt(u + 1)
                ve.wait_ge(pe_done, at(PE, ("s", u)))
                op(("s sum", u), V.tensor_tensor(stt_, sin_[u % 2], cut(bank[6], 0, 2, P), ALU.add))
                for jj in range(2):
                    V.scalar_tensor_tensor(state[:, 4 * d + 2 * pg + jj, :], stt_[:, jj, :],
                                           ex[u % 2][:, jj, 257:258], const("head"), ALU.mult, ALU.mult
                                           ).then_inc(vec_done, did(VE, ("state 1" if jj else "state 0", u)))
                ve.wait_ge(pe_done, at(PE, ("y", u)))
                y_ = yt[:, c, 256 * pg:256 * pg + 256]
                if d == 0:
                    V.tensor_copy(y_, bank[5][:, 0:256]).then_inc(vec_done, did(VE, ("state", u)))
                else:
                    V.tensor_tensor(y_, y_, bank[5][:, 0:256], ALU.add
                                    ).then_inc(vec_done, did(VE, ("state", u)))
                ve.wait_ge(vec_done, now(VE))
            yh = yt.rearrange("p c (h n) -> p (c h) n", n=HD)
            sq = cut(ring_t, 8192, 32, HD)
            m_, v_h, rt_ = small[:, 32:64], small[:, 64:96], small[:, 96:128]
            op("yr sum", V.tensor_reduce(m_, yh, AX.X, ALU.add))
            op("yr mean", V.tensor_scalar(m_, m_, 1.0 / HD, None, ALU.mult))
            op("yr centre", V.tensor_tensor(yh, yh, wide(m_[:, :, None], 32, HD), ALU.subtract))
            op("yr sq", V.tensor_tensor(sq, yh, yh, ALU.mult))
            op("yr ss", V.tensor_reduce(v_h, sq, AX.X, ALU.add))
            op("yr var", V.tensor_scalar(v_h, v_h, 1.0 / HD, GN_EPS, ALU.mult, ALU.add))
            ve.wait_ge(act_done, at(AC, "yr root"))
            op("yr rstd", V.reciprocal(m_, rt_))
            op("yr norm", V.tensor_tensor(yh, yh, wide(m_[:, :, None], 32, HD), ALU.mult))
            for j in range(4):
                ve.wait_ge(act_done, at(AC, ("gn", j)))
                op(("gn bonus", j), V.tensor_tensor(mix[:, j, :], mix[:, j, :], bonus[:, j, :], ALU.add))
                V.tensor_tensor(mix[:, j, :], mix[:, j, :], gate[:, j, :], ALU.mult
                                ).then_inc(vec_done, did(VE, "o_rw" if j == 3 else ("o_rw", j)))
            ve.wait_ge(again_in, 2 * 16)
            for j in range(KT):
                ve.wait_ge(pe_done, at(PE, ("mix out", j)))
                residual("mix res", j, bank[6 + j % 2], (0, 0, 2), (0, 1))

            norm(1, slice(0, T), False)
            products_by_partition(0)
            for j in range(FT):
                ve.wait_ge(act_done, at(AC, ("sg", j)))
                ve.wait_ge(pe_done, at(PE, ("ffn3", "tile", j)))
                V.tensor_tensor(G[:, j, :], sg[j % 2], bank[2 * (j % 2) + 1], ALU.mult
                                ).then_inc(vec_done, did(VE, ("gu", j)))
                if j:
                    columns_out(j - 1)
                products_by_partition(j + 1)
            for n in range(KT):
                if n + 1 < KT:
                    products_by_partition(FT + n + 1)
                ve.wait_ge(pe_done, at(PE, ("ffn out", n)))
                residual("ffn res", n, bank[4 + n % 4], (0, 0, 5), (0, 1))
                columns_out(FT + n - 1)
            columns_out(FT + KT - 1)
            scales([2, 3, 5, 7, 9, 11])

            norm(2, slice(0, T), False)
            ve.wait_ge(bias_in, 16)
            flat = rb.rearrange("p h (r k) -> p (h r) k", k=GRID_W)
            op("rb 0", V.tensor_tensor(flat, flat, wide(const("win", 64)[:, None, :], 96, 64), ALU.mult))
            op("rb", V.tensor_tensor(flat, flat, wide(const("out_win", 64)[:, None, :], 96, 64), ALU.add))
            for hd in range(16):
                for qt in range(2):
                    ve.wait_ge(pe_done, at(PE, ("s1", hd, qt)))
                    if hd:
                        ve.wait_ge(pe_done, at(PE, ("pt1", hd - 1, qt)))
                    V.tensor_copy(pr[:, qt, CTX], bank[qt][:, CTX]).then_inc(vec_done, did(VE, ("s ctx", hd, qt)))
                    i0 = (2 - 2 * qt) * GRID_W
                    op(("s lat", hd, qt), V.tensor_tensor(pr[:, qt, LAT], bank[qt][:, LAT],
                                                          rb[:, hd, i0:i0 + TL], ALU.add))
                    V.tensor_reduce(stat[:, qt:qt + 1], pr[:, qt, :], AX.X, ALU.max, negate=True
                                    ).then_inc(vec_done, did(VE, ("m1", hd, qt)))
                for qt in range(2):
                    ve.wait_ge(act_done, at(AC, ("exp1", hd, qt)))
                    op(("r1", hd, qt), V.reciprocal(stat[:, 4 + qt:5 + qt], stat[:, 2 + qt:3 + qt]))
                    V.tensor_scalar(pr[:, qt, :], pr[:, qt, :], stat[:, 4 + qt:5 + qt], None, ALU.mult
                                    ).then_inc(vec_done, did(VE, ("p1", hd, qt)))
                hp = slice(64 * (hd % 2), 64 * (hd % 2) + 64)
                ve.wait_ge(pe_done, at(PE, ("o1", hd)))
                V.tensor_copy(o1[hp, hd // 2, :], bank[4 + hd % 2][hp, 0:TL]
                              ).then_inc(vec_done, did(VE, ("o1", hd)))
            for j in range(KT):
                ve.wait_ge(pe_done, at(PE, ("na out", j)))
                residual("na res", j, bank[6 + j % 2][:, 0:TL], (0, 1, 2), (1,))

            norm(3, LAT, False)
            ve.wait_ge(pe_done, at(PE, "router"))
            op("lg", V.tensor_tensor(lg, cut(bank[1], 0, 2, NE),
                                     wide(row("moe_router_b", 8)[:, None, :], 2, NE), ALU.add))
            for c in range(2):
                a, b = lg[:, c, :][:, :, None], lg[:, c, :][:, None, :]
                V.tensor_tensor(cmp_[:, c], wide(b, NE, NE), wide(a, NE, NE), ALU.is_gt
                                ).then_inc(vec_done, did(VE, ("gt", c)))
                op(("eq", c), V.tensor_tensor(cm2[:, c], wide(b, NE, NE), wide(a, NE, NE), ALU.is_equal))
                op(("tie", c), V.tensor_tensor(cm2[:, c], cm2[:, c], cut(const("first", 64), 0, NE, NE),
                                               ALU.mult))
                op(("beats", c), V.tensor_tensor(cmp_[:, c], cmp_[:, c], cm2[:, c], ALU.add))
                op(("rank", c), V.tensor_reduce(rank[:, c, :], cmp_[:, c], AX.X, ALU.add))
            op("lg top", V.tensor_reduce(mx, lg, AX.X, ALU.max))
            op("lg max", V.tensor_tensor(ge, lg, wide(mx[:, :, None], 2, NE), ALU.subtract))
            ve.wait_ge(act_done, at(AC, "ge"))
            op("chosen", V.tensor_scalar(chosen, rank, 1.5, None, ALU.is_lt))
            op("top 2", V.tensor_tensor(gates, chosen, ge, ALU.mult))
            op("gate sum", V.tensor_reduce(sm, gates, AX.X, ALU.add))
            op("gate 1/sum", V.reciprocal(mx, sm))
            op("gates", V.tensor_tensor(gates, gates, wide(mx[:, :, None], 2, NE), ALU.mult))
            ve.wait_ge(pe_done, at(PE, "places"))
            op("place 0", V.scalar_tensor_tensor(place, cut(bank[6], 0, 2, NE), 1.0, chosen,
                                                 ALU.add, ALU.mult))
            op("place", V.tensor_scalar(place, place, -1.0, None, ALU.add))
            op("over", V.tensor_scalar(over, bank[6][:, 16:24], P + 0.5, None, ALU.is_gt))
            op("order 0", V.tensor_tensor(cmp_[:, 0], cut(const("first", 64), 0, NE, NE),
                                          wide(over[:, None, :], NE, NE), ALU.mult))
            op("order", V.tensor_reduce(order, cmp_[:, 0], AX.X, ALU.add))
            for i in range(3):
                op(("which", i), V.scalar_tensor_tensor(which[:, i, :], order, float(i), over,
                                                        ALU.is_equal, ALU.mult))
            V.tensor_copy(posb[:, :, 0:NE], place).then_inc(vec_done, did(VE, "posb"))
            V.tensor_copy(gateb[:, :, 0:NE], gates).then_inc(vec_done, did(VE, "gateb"))
            op("posb rest", V.memset(posb[:, :, NE:12], -1.0))
            op("gateb rest", V.memset(gateb[:, :, NE:12], 0.0))
            op("place - 128", V.tensor_scalar(place, place, -float(P), None, ALU.add))
            for c in range(2):
                for src, dst in ((place, posb), (gates, gateb)):
                    name = "posb" if src is place else "gateb"
                    op((name, c, 0), V.tensor_tensor(w24, which, wide(src[:, c, :][:, None, :], 3, NE),
                                                     ALU.mult))
                    op((name, c), V.tensor_reduce(dst[:, c, NE:NE + 3], w24, AX.X, ALU.add))
            op("info 0", V.tensor_copy(info[:, 0:12], const("count")[:, 0:12]))
            op("expert 0", V.tensor_tensor(w24, which, wide(const("count")[:, 0:8][:, None, :], 3, NE),
                                           ALU.mult))
            op("expert", V.tensor_reduce(info[:, NE:NE + 3], w24, AX.X, ALU.add))
            op("over sum", V.tensor_reduce(info[:, 12:13], over, AX.X, ALU.add))
            op("blocks 0", V.tensor_scalar(info[:, 12:13], info[:, 12:13], float(NE), None, ALU.add))
            op("blocks", V.tensor_copy(block_info[0:1, 0:13], info[0:1, 0:13]))
            per = at(VEM, ("per", "moe"))
            pper, aper = at(PEM, ("per", "moe")), at(ACM, ("per", "moe"))
            counts.count[VEM] = per
            V.memset(small[:, 501:502], 0.0).then_inc(ve_moe, per)
            blocks = ve.value_load(block_info[0:1, 12:13], min_val=NE, max_val=NE + 3)
            with ve.Fori(0, blocks) as e:
                ve.wait_ge(pe_moe, e * pper + (at(PEM, "gates turned") - pper))
                for c in range(2):
                    V.tensor_scalar(pm[:, c, :], const("count"), posb[:, c, bass.ds(e, 1)], None,
                                    ALU.is_equal).then_inc(ve_moe, did(VEM, "P" if c else "P 0"))
                for c in range(2):
                    V.tensor_scalar(pgw[:, c, :], const("count"), posb[:, c, bass.ds(e, 1)],
                                    gateb[:, c, bass.ds(e, 1)], ALU.is_equal, ALU.mult
                                    ).then_inc(ve_moe, did(VEM, "Pg" if c else "Pg 0"))
                for j in range(FT):
                    ve.wait_ge(pe_moe, e * pper + at(PEM, ("tile", 1, j)))
                    ve.wait_ge(ac_moe, e * aper + at(ACM, ("sg", j)))
                    V.tensor_tensor(Gm[:, j, :], sgm[j % 2], bank[2 * (j % 2) + 1][:, 0:P], ALU.mult
                                    ).then_inc(ve_moe, did(VEM, ("gu", j)))
                for f in range(KT):
                    if f % 2 == 0:
                        ve.wait_ge(pe_moe, e * pper + at(PEM, ("back", f // 2)))
                    V.scalar_tensor_tensor(hT[:, f, LAT], bank[f // 2][:, 256 * (f % 2):256 * (f % 2) + 256],
                                           mod(0, 1, 5, f, 1), hT[:, f, LAT], ALU.mult, ALU.add
                                           ).then_inc(ve_moe, did(VEM, ("h", f)))
                ve.wait_ge(ve_moe, e * per + now(VEM))
            counts.values[VEM, ("per", "moe")] = counts.count[VEM] - per
            op("moe res", V.memset(small[:, 501:502], 0.0))
            ve.wait_ge(vec_done, now(VE))
            norm(4, LAT, False)

            norm(5, slice(0, T), True)
            V.memset(vp[:, :, 0:1], 0.0).then_inc(vec_done, did(VE, "vp edge 0"))
            V.memset(vp[:, :, TL + 1:TL + 2], 0.0).then_inc(vec_done, did(VE, "vp edge 1"))
            lq = cut(row("lambda_qk_2", 256), 0, 2, 2, 64)
            op("lam products", V.tensor_tensor(lprod[:, 0:2, :], lq[:, :, 0, :], lq[:, :, 1, :], ALU.mult))
            op("lam sums", V.tensor_reduce(lamv[:, 0:2], lprod[:, 0:2, :], AX.X, ALU.add))
            ve.wait_ge(act_done, at(AC, ("in2", 11)))
            op("gc v", V.tensor_tensor(vp[:, :, 1:TL + 1], vp[:, :, 1:TL + 1], gc, ALU.mult))
            for j in range(4):
                dst = mix[:, j, LAT]
                op(("conv2", j, 0), V.tensor_scalar(dst, vp[:, j, 0:TL], col("conv_w_2", j), None, ALU.mult))
                for tap in (1, 2):
                    op(("conv2", j, tap), V.scalar_tensor_tensor(dst, vp[:, j, tap:tap + TL],
                                                                 col("conv_w_2", 4 * tap + j), dst,
                                                                 ALU.mult, ALU.add))
                V.tensor_tensor(dst, dst, gb[:, j, :], ALU.mult
                                ).then_inc(vec_done, did(VE, "o_conv" if j == 3 else ("o_conv", j)))
            for n in range(8):
                src = q2[:, n, :] if n < 4 else k2[:, n - 4, LAT]
                ve.wait_ge(pe_done, at(PE, ("turn", n)))
                V.tensor_tensor(rt[:, n % 2, :], bank[6 + n % 2][:, 0:TL], const("sin", 256), ALU.mult
                                ).then_inc(vec_done, did(VE, ("rope sin", n)))
                op(("rope cos", n), V.tensor_tensor(src, src, const("cos", 256), ALU.mult))
                op(("rope", n), V.tensor_tensor(src, src, rt[:, n % 2, :], ALU.add))
            ve.wait_ge(act_done, at(AC, "lam"))
            op("lam 0", V.tensor_tensor(lamv[:, 4:5], lamv[:, 3:4], lamv[:, 2:3], ALU.subtract))
            op("- lam", V.tensor_scalar(lamv[:, 4:5], lamv[:, 4:5], -LAM_INIT, None, ALU.add))
            s_ = small[:, 150:160]
            for hd in range(4):
                for qt in range(2):
                    for cp in range(2):
                        ve.wait_ge(pe_done, at(PE, ("s2", hd, qt, cp)))
                        V.tensor_reduce(s_[:, cp:cp + 1], bank[cp], AX.X, ALU.max, negate=True
                                        ).then_inc(vec_done, did(VE, ("m2", hd, qt, cp)))
                    ve.wait_ge(act_done, at(AC, ("exp2", hd, qt, 1)))
                    op(("r2", hd, qt), V.reciprocal(s_[:, 4:6], s_[:, 2:4]))
                    op(("lam r2", hd, qt), V.tensor_tensor(s_[:, 5:6], s_[:, 5:6], lamv[:, 4:5], ALU.mult))
                    op(("lam p", hd, qt), V.tensor_scalar(p2[:, 1, :], p2[:, 1, :], s_[:, 5:6], None, ALU.mult))
                    if hd:
                        ve.wait_ge(pe_done, at(PE, ("pt2", hd - 1, qt)))
                    op(("p2", hd, qt), V.scalar_tensor_tensor(pd[:, qt, :], p2[:, 0, :], s_[:, 4:5],
                                                              p2[:, 1, :], ALU.mult, ALU.add))
            ve.wait_ge(pe_done, at(PE, "subln"))
            for i, t in enumerate((tmpA, tmpB)):
                V.tensor_scalar(t, bank[6 + i], 1.0 / P, SUBLN_EPS, ALU.mult, ALU.add
                                ).then_inc(vec_done, did(VE, ("subln", i)))
            for i, t in enumerate((tmpA, tmpB)):
                ve.wait_ge(act_done, at(AC, ("subln", i)))
                op(("subln rstd", i), V.reciprocal(t, t))
                o_ = o2[:, 2 * i:2 * i + 2, :]
                op(("subln o", i), V.tensor_tensor(o_, o_, cut(t, 0, 2, TL), ALU.mult))
                V.tensor_scalar(mix[:, 4 + 2 * i:6 + 2 * i, LAT], o_, col("subln_g_2", 0), 1.0 - LAM_INIT,
                                ALU.mult, ALU.mult).then_inc(vec_done, did(VE, "o_attn" if i else "o_attn 0"))

            def add_scaled(name, j, src, gate):
                op((name, j, "gated"), V.tensor_scalar(tmpA[:, 0:TL], src, mod(*gate, j, 1), None, ALU.mult))
                op((name, j), V.scalar_tensor_tensor(hT[:, j, LAT], hT[:, j, LAT], ALPHA, tmpA[:, 0:TL],
                                                     ALU.mult, ALU.add))

            def outwards(name, st, gate):
                for j in range(KT):
                    ve.wait_ge(pe_done, at(PE, (name, j)))
                    add_scaled(name, j, bank[2 + j % 2][:, 0:TL], gate)
                norm(st, LAT, True)

            def mlp(i, st):
                norm(st, LAT, True)
                for j in range(F2T):
                    ve.wait_ge(pe_done, at(PE, (("mlp1", i), j)))
                    x_ = bank[2 + j % 2][:, 0:TL]
                    V.tensor_scalar(sg[0][:, 256 * (j % 2):256 * (j % 2) + 256], x_, 0.0, None, ALU.max
                                    ).then_inc(vec_done, did(VE, ("relu", i, j)))
                    ve.wait_ge(vec_done, now(VE))
                    r = sg[0][:, 256 * (j % 2):256 * (j % 2) + 256]
                    V.tensor_tensor(G2[:, j, :], r, r, ALU.mult).then_inc(vec_done, did(VE, ("relu2", i, j)))
                for j in range(KT):
                    ve.wait_ge(pe_done, at(PE, (("mlp", i), j)))
                    add_scaled(("mlp", i), j, bank[4 + j % 2][:, 0:TL], (1, i, 5))
                norm(st + 1, LAT, True)

            outwards("out2", 6, (1, 0, 2))
            mlp(0, 7)
            norm(9, LAT, True)
            outwards("fourier", 10, (1, 1, 2))
            mlp(1, 11)


INPUTS = ("w_ada", "ada_w_2", "mix_w_in", "mix_w_out", "rw_w_up", "rw_a_up", "rw_g_up",
          "ffn_w1", "ffn_w3", "ffn_w2", "na_w_qkv", "na_w_out", "moe_router_w",
          "moe_w1", "moe_w3", "moe_w2", "w_in_2", "w_out_mix_2", "w_out_fourier_2",
          "mlp_w1_2", "mlp_w2_2")


def columns(inputs):
    parts = []
    for name, width in COLUMNS:
        if name in ("mu_prev", "mu_next"):
            v = inputs["rw_mu"][0, int(name == "mu_next"), :13 * P]
        else:
            v = inputs[name].reshape(-1)
        parts.append(v.reshape(width, P).T)
    return np.ascontiguousarray(np.concatenate(parts, axis=1))


def broadcast_rows(inputs):
    parts = [inputs[name].reshape(-1) for name, _ in ROWS]
    return np.ascontiguousarray(np.broadcast_to(np.concatenate(parts), (P, NROW)))


def bias_by_query(rpb):
    cols_ = np.clip(np.arange(GRID_W)[None, :] - np.arange(GRID_W)[:, None] + NA_KW - 1,
                    0, 2 * NA_KW - 2)
    halves = [rpb[:, 5 - half:11 - half][:, :, cols_].transpose(2, 0, 1, 3) for half in range(2)]
    return np.ascontiguousarray(np.concatenate(halves, axis=0).reshape(P, -1))


def program(new_core, arrays):
    known, values = None, {}
    while known != values:
        known = values or None
        nc = new_core()
        w = {name: nc.dram_tensor(f"in_{name}", a.shape, F32, kind="ExternalInput").ap()
             for name, a in arrays.items()}
        out = nc.dram_tensor("out", (D, TL), F32, kind="ExternalOutput").ap()
        counts = Counts(known)
        build(nc, w, out, counts)
        values = counts.values
    return nc


def kernel(**inputs):
    import concourse.bacc as bacc
    from concourse.bass_utils import run_bass_kernel_spmd as run

    inputs = {name: np.asarray(a) for name, a in inputs.items()}
    arrays = {name: np.ascontiguousarray(inputs[name]) for name in INPUTS}
    arrays["xT"] = np.ascontiguousarray(inputs["x"][0].T)
    arrays["ctxT"] = np.ascontiguousarray(inputs["ctx"][0].T)
    arrays["ctx2T"] = np.ascontiguousarray(inputs["ctx_2"][0].T)
    arrays["cols"] = columns(inputs)
    arrays["rows"] = broadcast_rows(inputs)
    arrays["w0row"] = np.ascontiguousarray(np.broadcast_to(inputs["rw_w0"].reshape(-1), (P, 2 * RW)))
    arrays["bias"] = bias_by_query(inputs["na_rpb"][0])
    arrays["mu_g"] = np.ascontiguousarray(inputs["rw_mu"][0, :, 13 * P:].T)
    arrays["consts"] = constants()
    nc = program(lambda: bacc.Bacc("TRN2", target_bir_lowering=False, num_devices=1), arrays)
    r = run(nc, [{f"in_{name}": a for name, a in arrays.items()}], core_ids=[0])
    return np.ascontiguousarray(r.results[0]["out"].T)[None]
```
